# Optimizing a Trainium2 kernel written in Bass

```python
import functools
import jax, jax.numpy as jnp
from jax import lax
import numpy as np

D_MODEL = 1024
BATCH = 1
SEQ = 512
DEPTH = 2
DEC_BATCH = 8
DEC_SEQ = 4
PAST_LEN = 4096
PAGE_SIZE = 128

MIX_WIDTH = D_MODEL
HG_HEADS = 4
HG_DK = MIX_WIDTH // 2 // HG_HEADS
HG_DV = HG_DK
RT_HEADS = 4
RT_DK = MIX_WIDTH // 2 // RT_HEADS
RT_DV = RT_DK
HG_W = HG_HEADS * HG_DK
RT_W = RT_HEADS * RT_DK
PROJ_COLS = 4 * HG_W + 4 * RT_W
SPLITS = [HG_W, 2 * HG_W, 3 * HG_W, 4 * HG_W, 4 * HG_W + RT_W, 4 * HG_W + 2 * RT_W, 4 * HG_W + 3 * RT_W]
N_META = 16
CHUNK = 64
CONV_W = 3
D_FF = 2816
ROPE_BASE = 10000.0
LN_EPS = 1e-5
F_EPS = 1e-6
ALPHA = (2 * DEPTH) ** 0.25
BETA = (8 * DEPTH) ** -0.25

kernel_name = 'hymba_hgrn2_retention_convffn_step'

def layer_norm(x, g, b):
    xf = x.astype(jnp.float32)
    mu = jnp.mean(xf, -1, keepdims=True)
    var = jnp.mean(jnp.square(xf - mu), -1, keepdims=True)
    return ((xf - mu) * lax.rsqrt(var + LN_EPS) * g + b).astype(x.dtype)

def head_rms_norm(o):
    return o * lax.rsqrt(jnp.mean(jnp.square(o), -1, keepdims=True) + LN_EPS)

def head_group_norm(o):
    mu = jnp.mean(o, -1, keepdims=True)
    var = jnp.mean(jnp.square(o - mu), -1, keepdims=True)
    return (o - mu) * lax.rsqrt(var + LN_EPS)

def rotary(x, pos):
    half = x.shape[-1] // 2
    inv = ROPE_BASE ** (-jnp.arange(half, dtype=jnp.float32) / half)
    ang = pos.astype(jnp.float32)[:, None] * inv[None, :]
    cos = jnp.cos(ang)[None, :, None, :]
    sin = jnp.sin(ang)[None, :, None, :]
    x1, x2 = x[..., :half], x[..., half:]
    return jnp.concatenate([x1 * cos - x2 * sin, x1 * sin + x2 * cos], -1)

def hgrn2_block(s0, q, k, v, log_f):
    c = q.shape[1]
    b = jnp.cumsum(log_f, axis=1)
    causal = jnp.tril(jnp.ones((c, c), bool))[None, :, :, None, None]
    diff = jnp.where(causal, b[:, :, None] - b[:, None, :], 0.0)
    decay = jnp.where(causal, jnp.exp(diff), 0.0)
    scores = jnp.einsum('bthk,btshk,bshk->bhts', q, decay, k)
    o = jnp.einsum('bhts,bshv->bthv', scores, v) + jnp.einsum('bthk,bhkv->bthv', q * jnp.exp(b), s0)
    b_last = b[:, -1]
    s_new = jnp.exp(b_last)[..., None] * s0 + jnp.einsum('bshk,bshv->bhkv', k * jnp.exp(b_last[:, None] - b), v)
    return s_new, o

def retention_block(s0, q, k, v):
    c = q.shape[1]
    log_gamma = jnp.log1p(-jnp.exp2(-5.0 - jnp.arange(RT_HEADS, dtype=jnp.float32)))
    idx = jnp.arange(c, dtype=jnp.float32)
    rel = idx[:, None] - idx[None, :]
    mask = (rel >= 0)[None]
    decay = jnp.where(mask, jnp.exp(jnp.where(mask, rel[None] * log_gamma[:, None, None], 0.0)), 0.0)
    scores = jnp.einsum('bthk,bshk->bhts', q, k) * decay[None]
    q_dec = jnp.exp((idx + 1.0)[:, None] * log_gamma[None, :])
    o = jnp.einsum('bhts,bshv->bthv', scores, v) + jnp.einsum('bthk,bhkv->bthv', q, s0) * q_dec[None, :, :, None]
    k_dec = jnp.exp((c - 1.0 - idx)[:, None] * log_gamma[None, :])
    s_new = jnp.exp(c * log_gamma)[None, :, None, None] * s0 + jnp.einsum('bshk,bshv->bhkv', k * k_dec[None, :, :, None], v)
    return s_new, o

def mix_sequence(block_fn, s0, arrays, lead):
    s, o_lead = block_fn(s0, *(a[:, :lead] for a in arrays))
    rest = tuple(a[:, lead:] for a in arrays)
    n_blocks = rest[0].shape[1] // CHUNK
    if n_blocks == 0:
        return s, o_lead

    def to_blocks(a):
        return jnp.swapaxes(a.reshape(a.shape[0], n_blocks, CHUNK, *a.shape[2:]), 0, 1)

    s, o_rest = lax.scan(lambda st, xs: block_fn(st, *xs), s, tuple(to_blocks(a) for a in rest))
    o_rest = jnp.swapaxes(o_rest, 0, 1).reshape(o_lead.shape[0], n_blocks * CHUNK, *o_lead.shape[2:])
    return s, jnp.concatenate([o_lead, o_rest], axis=1)

def token_mixer(x, pos, s_hg, s_rt, lead, lb, w_in, hg_norm_g, rt_gn_g, rt_gn_b, w_o):
    bsz, t, _ = x.shape
    f32 = jnp.float32
    proj = jnp.einsum('btd,dc->btc', x, w_in).astype(f32)
    hq, hf, hv, hg, rq, rk, rv, rg = jnp.split(proj, SPLITS, axis=-1)

    def heads(a, h):
        return a.reshape(bsz, t, h, -1)

    f_gate = lb + (1.0 - lb) * jax.nn.sigmoid(hf)
    log_f = jnp.log(jnp.maximum(f_gate, F_EPS))
    k_hg = (1.0 - lb) * jax.nn.sigmoid(-hf)
    s_hg, o_hg = mix_sequence(hgrn2_block, s_hg.astype(f32),
                              (heads(jax.nn.silu(hq), HG_HEADS), heads(k_hg, HG_HEADS),
                               heads(hv, HG_HEADS), heads(log_f, HG_HEADS)), lead)
    o_hg = head_rms_norm(o_hg).reshape(bsz, t, HG_W) * hg_norm_g * jax.nn.silu(hg)

    q_r = rotary(heads(rq, RT_HEADS), pos)
    k_r = rotary(heads(rk, RT_HEADS), pos) * (RT_DK ** -0.5)
    s_rt, o_rt = mix_sequence(retention_block, s_rt.astype(f32), (q_r, k_r, heads(rv, RT_HEADS)), lead)
    o_rt = (head_group_norm(o_rt).reshape(bsz, t, RT_W) * rt_gn_g + rt_gn_b) * jax.nn.silu(rg)

    o = jnp.concatenate([o_hg, o_rt], axis=-1).astype(x.dtype)
    return jnp.einsum('btc,cd->btd', o, w_o), s_hg, s_rt

def conv_ffn(x, conv_buf, w_a, w_b, conv_w, conv_b, w_down):
    a = jnp.einsum('btd,df->btf', x, w_a)
    g = jnp.einsum('btd,df->btf', x, w_b)
    t = a.shape[1]
    a_ext = jnp.concatenate([conv_buf.astype(a.dtype), a], axis=1)
    conv = conv_b + sum(conv_w[j] * a_ext[:, j:j + t] for j in range(CONV_W))
    h = jax.nn.gelu(conv) * g
    return jnp.einsum('btf,fd->btd', h, w_down), a_ext[:, -(CONV_W - 1):]

def trunk(x, pos, lead, s_hg, s_rt, s_conv, lb_all, w_in, hg_norm_g, rt_gn_g, rt_gn_b, w_o,
          ln1_g, ln1_b, w_a, w_b, conv_w, conv_b, w_down, ln2_g, ln2_b):
    new_hg, new_rt, new_conv = [], [], []
    for l in range(DEPTH):
        mix, h_state, r_state = token_mixer(x, pos, s_hg[l], s_rt[l], lead, lb_all[l], w_in[l],
                                            hg_norm_g[l], rt_gn_g[l], rt_gn_b[l], w_o[l])
        x = layer_norm(ALPHA * x + mix, ln1_g[l], ln1_b[l])
        ffn, c_state = conv_ffn(x, s_conv[l], w_a[l], w_b[l], conv_w[l], conv_b[l], w_down[l])
        x = layer_norm(ALPHA * x + ffn, ln2_g[l], ln2_b[l])
        new_hg.append(h_state)
        new_rt.append(r_state)
        new_conv.append(c_state)
    return x, jnp.stack(new_hg), jnp.stack(new_rt), jnp.stack(new_conv)

def setup_inputs(seed: int = 0) -> dict:
    key = jax.random.key(seed)
    ks = jax.random.split(key, 24)
    f32 = jnp.float32

    def nrm(k, shape, s):
        return jax.random.normal(k, shape, f32) * s

    col_scale = jnp.concatenate([jnp.ones((2 * HG_W,), f32), jnp.full((HG_W,), BETA, f32), jnp.ones((HG_W,), f32),
                                 jnp.ones((2 * RT_W,), f32), jnp.full((RT_W,), BETA, f32), jnp.ones((RT_W,), f32)])
    return {
        'x_prompt': nrm(ks[0], (BATCH, SEQ, D_MODEL), 1.0),
        'x_sample': nrm(ks[1], (DEC_BATCH, DEC_SEQ, D_MODEL), 1.0),
        'state_hgrn': nrm(ks[2], (DEPTH, DEC_BATCH, HG_HEADS, HG_DK, HG_DV), 0.5),
        'state_ret': nrm(ks[3], (DEPTH, DEC_BATCH, RT_HEADS, RT_DK, RT_DV), 1.0),
        'state_conv': nrm(ks[4], (DEPTH, DEC_BATCH, CONV_W - 1, D_FF), 1.0),
        'meta_tokens': nrm(ks[5], (N_META, D_MODEL), 1.0),
        'emb_ln_g': 1.0 + nrm(ks[6], (D_MODEL,), 0.02),
        'emb_ln_b': nrm(ks[7], (D_MODEL,), 0.02),
        'lb_logits': nrm(ks[8], (DEPTH, HG_W), 0.5),
        'w_in': nrm(ks[9], (DEPTH, D_MODEL, PROJ_COLS), D_MODEL ** -0.5) * col_scale,
        'hg_norm_g': 1.0 + nrm(ks[10], (DEPTH, HG_W), 0.02),
        'rt_gn_g': 1.0 + nrm(ks[11], (DEPTH, RT_W), 0.02),
        'rt_gn_b': nrm(ks[12], (DEPTH, RT_W), 0.02),
        'w_o': nrm(ks[13], (DEPTH, MIX_WIDTH, D_MODEL), MIX_WIDTH ** -0.5 * BETA),
        'ln1_g': 1.0 + nrm(ks[14], (DEPTH, D_MODEL), 0.02),
        'ln1_b': nrm(ks[15], (DEPTH, D_MODEL), 0.02),
        'w_a': nrm(ks[16], (DEPTH, D_MODEL, D_FF), D_MODEL ** -0.5),
        'w_b': nrm(ks[17], (DEPTH, D_MODEL, D_FF), D_MODEL ** -0.5),
        'conv_w': nrm(ks[18], (DEPTH, CONV_W, D_FF), CONV_W ** -0.5),
        'conv_b': nrm(ks[19], (DEPTH, D_FF), 0.02),
        'w_down': nrm(ks[20], (DEPTH, D_FF, D_MODEL), D_FF ** -0.5 * BETA),
        'ln2_g': 1.0 + nrm(ks[21], (DEPTH, D_MODEL), 0.02),
        'ln2_b': nrm(ks[22], (DEPTH, D_MODEL), 0.02),
    }

def reference(x_prompt, x_sample, state_hgrn, state_ret, state_conv, meta_tokens, emb_ln_g, emb_ln_b,
              lb_logits, w_in, hg_norm_g, rt_gn_g, rt_gn_b, w_o, ln1_g, ln1_b, w_a, w_b, conv_w, conv_b,
              w_down, ln2_g, ln2_b):
    sm = jax.nn.softmax(lb_logits.astype(jnp.float32), axis=0)
    lb_all = jnp.cumsum(sm, axis=0) - sm[0:1]
    weights = (lb_all, w_in, hg_norm_g, rt_gn_g, rt_gn_b, w_o, ln1_g, ln1_b,
               w_a, w_b, conv_w, conv_b, w_down, ln2_g, ln2_b)

    bsz, seq = x_prompt.shape[0], x_prompt.shape[1]
    meta = jnp.broadcast_to(meta_tokens.astype(x_prompt.dtype)[None], (bsz, N_META, D_MODEL))
    xp = layer_norm(jnp.concatenate([meta, x_prompt], axis=1), emb_ln_g, emb_ln_b)
    pos_p = jnp.arange(N_META + seq, dtype=jnp.int32)
    zero_hg = jnp.zeros((DEPTH, bsz, HG_HEADS, HG_DK, HG_DV), jnp.float32)
    zero_rt = jnp.zeros((DEPTH, bsz, RT_HEADS, RT_DK, RT_DV), jnp.float32)
    zero_conv = jnp.zeros((DEPTH, bsz, CONV_W - 1, D_FF), x_prompt.dtype)
    yp, hg_p, rt_p, conv_p = trunk(xp, pos_p, N_META, zero_hg, zero_rt, zero_conv, *weights)
    y_prompt = yp[:, N_META:]

    xs = layer_norm(x_sample, emb_ln_g, emb_ln_b)
    pos_s = PAST_LEN + jnp.arange(x_sample.shape[1], dtype=jnp.int32)
    y_sample, hg_s, rt_s, conv_s = trunk(xs, pos_s, x_sample.shape[1], state_hgrn, state_ret, state_conv, *weights)

    return (y_prompt, y_sample, hg_p, hg_s, rt_p, rt_s, conv_p, conv_s)


_drawn_inputs = setup_inputs


def setup_inputs(seed=0):
    import zlib

    import numpy as np

    out = dict(_drawn_inputs(seed))
    spreads = {}
    factors = {'hg_norm_g': 8.0, 'rt_gn_g': 8.0, 'rt_gn_b': 8.0, 'conv_b': 8.0}
    for name, (base, spread) in spreads.items():
        noise = np.random.default_rng([zlib.crc32(name.encode()), seed]).standard_normal(out[name].shape)
        drawn = base * np.exp(spread * noise) if base else spread * noise
        out[name] = __import__('jax').numpy.asarray(drawn.astype(out[name].dtype))
    for name, factor in factors.items():
        out[name] = (out[name] * factor).astype(out[name].dtype)
    return out
```

```python
from contextlib import ExitStack

import concourse.bass as bass
import numpy as np
from concourse import mybir

F32 = mybir.dt.float32
F16 = mybir.dt.float16
ALU = mybir.AluOpType
ACT = mybir.ActivationFunctionType

P = 128
D_MODEL = 1024
DEPTH = 2
SEQ = 512
N_META = 16
DEC_BATCH = 8
DEC_SEQ = 4
PAST_LEN = 4096
HEADS = 4
D_FF = 2816
CONV_W = 3
LN_EPS = 1e-5
LOG_F_MIN = float(np.log(1e-6))
ALPHA = (2 * DEPTH) ** 0.25

TP = N_META + SEQ
TS = DEC_BATCH * DEC_SEQ
T = TP + TS
HALF = T // 2
KT = D_MODEL // P
FT = D_FF // P
KD = FT // 2
UNIT = KT * 2 * P
UNIT_D = KD * P
W_SCALE = 64.0
INV_W = 1.0 / W_SCALE

C = 48
NC = TP // C
A = 6
NA = C // A
AT = 2
SPLIT = 6 * C
REST = T - SPLIT
CLAMP = -44.0

TT5 = 5
R5 = T - 4 * P
TAIL = TP - 4 * P
RT_COLS = [TP - P * i for i in range(TT5)]
RT_OFF = [sum(RT_COLS[:i]) for i in range(TT5)]

U_P, U_O, U_F, U_D = 16, 4, 22, 16
SLOT_UNITS = (U_P + U_O + U_F + U_D) // 2
TILES = 32 + 8 + 2 * FT + 8
ACC_TILES = TILES // 2
O_TILE, F_TILE, D_TILE = 32, 40, 40 + 2 * FT
SCR_START = (11, 6, 5)
SCR_LN = (2, 1, 1)
SCR_HG = (16, 8, 8)
SCR_RT = (13, 7, 6)
SCR_CIN = (1, 1, 0)
SCR_COUT = (6, 3, 3)
SCR_LAYER = tuple(2 * a + HEADS * (b + c) + d + e for a, b, c, d, e in zip(SCR_LN, SCR_HG, SCR_RT, SCR_CIN, SCR_COUT))
OT_LAYER = 2 + HEADS + 2 * HEADS
ROW_HG, ROW_RG, ROW_RB, ROW_LB, ROWS2 = 80, 88, 96, 104, 112
ROWS01 = (CONV_W + 1) * FT


def const_columns():
    at, out = 0, {}
    for name, width in [("ident", P), ("ones_ln", P), ("ones_h", P), ("center", P), ("eps", 8), ("cos", T), ("sin", T),
                        ("keep", T), ("mask48", C), ("mask32", TS), ("seq", DEC_BATCH), ("decay", HEADS * TP),
                        ("mask_rt", HEADS * TS), ("q_dec", HEADS * TS), ("k_dec", TT5 * HEADS), ("k_dec_s", HEADS),
                        ("gamma4", HEADS)]:
        out[name] = (at, width)
        at += width
    return out, at


def const_tables():
    cols, n = const_columns()
    tab = np.zeros((P, n), np.float32)

    def put(name, value):
        at, width = cols[name]
        value = np.asarray(value, np.float32).reshape(len(value), width)
        tab[:len(value), at:at + width] = value

    put("ident", np.eye(P))
    put("ones_ln", np.full((P, P), 1.0 / D_MODEL))
    put("ones_h", np.full((P, P), 1.0 / P))
    put("center", np.eye(P) - 1.0 / P)
    eps = np.zeros((P, 8))
    eps[:, 0] = LN_EPS
    eps[:, 1:5] = LN_EPS / ALPHA ** 2
    eps[:, 5] = LN_EPS
    put("eps", eps)
    half = P // 2
    inv = np.float32(10000.0) ** (-np.arange(half, dtype=np.float32) / np.float32(half))
    pos = np.concatenate([np.arange(TP), np.tile(PAST_LEN + np.arange(DEC_SEQ), DEC_BATCH)]).astype(np.float32)
    ang = inv[:, None] * pos[None, :]
    put("cos", np.concatenate([np.cos(ang)] * 2) * INV_W)
    put("sin", np.concatenate([np.sin(ang), -np.sin(ang)]) * INV_W)
    keep = np.ones((P, T))
    keep[:, 0:TP:C] = 0
    keep[:, TP::DEC_SEQ] = 0
    put("keep", keep)
    put("mask48", np.triu(np.ones((C, C))))
    tok = np.arange(TS)
    same = tok[:, None] // DEC_SEQ == tok[None, :] // DEC_SEQ
    causal = same & (tok[:, None] <= tok[None, :])
    put("mask32", causal)
    put("seq", tok[:, None] // DEC_SEQ == np.arange(DEC_BATCH)[None, :])
    log_g = np.log1p(-np.exp2(-5.0 - np.arange(HEADS)))
    s, u = np.arange(P)[:, None, None], np.arange(TP)[None, None, :]
    root = P ** -0.5
    rel = np.maximum(u - s, 0)
    put("decay", np.where(u >= s, np.exp(rel * log_g[None, :, None]), 0.0) * root)
    rel = np.maximum(tok[None, :] - tok[:, None], 0)
    put("mask_rt", np.where(causal[:, None, :], np.exp(rel[:, None, :] * log_g[None, :, None]), 0.0) * root)
    put("q_dec", np.broadcast_to(np.exp((tok % DEC_SEQ + 1)[None, None, :] * log_g[None, :, None]), (P, HEADS, TS)))
    left = TP - 1 - (np.arange(TT5)[None, :, None] * P + np.arange(P)[:, None, None])
    put("k_dec", np.where(left >= 0, np.exp(np.maximum(left, 0) * log_g[None, None, :]), 0.0) * root)
    put("k_dec_s", np.exp((DEC_SEQ - 1 - tok % DEC_SEQ)[:, None] * log_g[None, :]) * root)
    put("gamma4", np.broadcast_to(np.exp(DEC_SEQ * log_g), (P, HEADS)))
    return tab


class Scratch:

    def __init__(self, base, *done):
        self.full, self.bank = base[0], [base[1], base[2]]
        for d in done:
            self.full, self.bank = self.full + d[0], [self.bank[0] + d[1], self.bank[1] + d[2]]

    def job(self, bank):
        free = self.bank[bank]
        self.full, self.bank[bank] = self.full + 1, free + 1
        return self.full, free


def hybrid_decoder_step(nc, x_prompt, x_sample, state_hgrn, state_ret, state_conv, meta_tokens, emb_ln_g, emb_ln_b,
                        lb_logits, w_in, hg_norm_g, rt_gn_g, rt_gn_b, w_o, ln1_g, ln1_b, w_a, w_b, conv_w, conv_b,
                        w_down, ln2_g, ln2_b, consts, y_prompt, y_sample, hg_prompt, hg_sample, rt_prompt,
                        rt_sample, conv_prompt, conv_sample):
    cols, n_const = const_columns()
    ds = bass.ds

    w_in_v = w_in.rearrange("l (k p) c -> p (l k) c", p=P)
    w_o_v = w_o.rearrange("l (k p) c -> p (l k) c", p=P)
    w_a_v = w_a.rearrange("l (k p) c -> p (l k) c", p=P)
    w_b_v = w_b.rearrange("l (k p) c -> p (l k) c", p=P)
    w_down_v = w_down.rearrange("l (k p) c -> p (l k) c", p=P)
    s0_hg_v = state_hgrn.rearrange("l b h k v -> (l b h) k v")
    s0_rt_v = state_ret.rearrange("l b h k v -> (l b h) k v")
    sn_hg_v = hg_sample.rearrange("l b h k v -> (l b h) k v")
    sn_rt_v = rt_sample.rearrange("l b h k v -> (l b h) k v")
    fin_hg_v = hg_prompt.rearrange("l b h k v -> (l b h k) v")
    fin_rt_v = rt_prompt.rearrange("l b h k v -> (l b h k) v")
    cin_v = state_conv.rearrange("l b j f -> (l b j) f")
    cp_v = conv_prompt.rearrange("l b j f -> (l b j) f")
    cs_v = conv_sample.rearrange("l b j f -> (l b j) f")
    SEQS = DEC_BATCH * HEADS

    with ExitStack() as ctx:
        def sb(name, shape, dt=F32):
            return ctx.enter_context(nc.sbuf_tensor(name, shape, dt))

        def sem(name):
            return ctx.enter_context(nc.semaphore(name))

        tab = sb("tab", [P, n_const])
        X = sb("X", [P, KT, T])
        XH, XL = sb("XH", [P, KT, T], F16), sb("XL", [P, KT, T], F16)
        OHL = sb("OHL", [P, 2 * KT, T], F16)
        OH, OL = OHL[:, 0:KT, :], OHL[:, KT:2 * KT, :]
        stage = sb("stage", [P, 2, UNIT])
        WH, WL = sb("WH", [P, 2, UNIT], F16), sb("WL", [P, 2, UNIT], F16)
        shared = sb("shared", [P, FT * T])
        HHL = shared[:, :].bitcast(F16).rearrange("p (k t) -> p k t", k=2 * FT)
        HH, HL = HHL[:, 0:FT, :], HHL[:, FT:2 * FT, :]
        KV = sb("KV", [P, NC, NA, C])
        Fb, T1, T2, T3, B, Q, QS, QD, KE, E, V, G = (
            sb(n, [P, T + 2]) for n in ("Fb", "T1", "T2", "T3", "B", "Q", "QS", "QD", "KE", "E", "V", "G"))
        at = [0]

        def part(width):
            at[0] += width
            return shared[:, at[0] - width:at[0]]

        KTOK, VTOK, SC = part(NC * P), part(NC * P), part(NC * P)
        S0, SN = part(DEC_BATCH * P), part(DEC_BATCH * P)
        PTR = part(RT_OFF[-1] + TAIL)
        SQ, R, TO = part(T), part(T), part(T)
        assert at[0] <= FT * T - D_FF
        CIN = shared[0:2 * DEC_BATCH, FT * T - D_FF:FT * T]
        CSO = OHL[:, :, :].rearrange("p k t -> p (k t)").bitcast(F32)[0:2 + 2 * DEC_BATCH, 0:D_FF]
        XT = shared[:, 0:TT5 * D_MODEL].rearrange("p (i d) -> p i d", i=TT5)
        S0b, SNb = (t.rearrange("p (b v) -> p b v", b=DEC_BATCH) for t in (S0, SN))
        S1, S2, SQT, MU, MSQ, VAR, RSTD, MR = B, Q, E, T1, T2, T3, QS, QD
        AX, CX = (T1, T2), (T3, Fb)
        VX = sb("VX", [TS, DEC_BATCH, P])
        KVTS = sb("KVTS", [TS, 2, P])
        PTS = sb("PTS", [C, TP])
        PTSS = sb("PTSS", [TS, TS])
        RSB = sb("RSB", [P, P])
        KVS = sb("KVS", [P, TS])
        EN = sb("EN", [P, TS])
        AS = sb("AS", [P, DEC_BATCH, CONV_W - 1 + DEC_SEQ])
        CST = sb("CST", [P, FT, 2 * DEC_BATCH])
        CSB = sb("CSB", [P, FT, 2 + 2 * DEC_BATCH])
        rows = stage[:, 1, 0:3 * P].rearrange("p (b c) -> p b c", b=3)
        par = sb("par", [P, 3 * P])
        CW2 = sb("CW2", [P, DEPTH * FT])
        LBT, OMLB = sb("LBT", [P, DEPTH * HEADS]), sb("OMLB", [P, DEPTH * HEADS])
        LE = sb("LE", [P, 6, HEADS])

        def table(name):
            a, w = cols[name]
            return tab[:, a:a + w]

        ident, ones_ln, ones_h, center = (table(n) for n in ("ident", "ones_ln", "ones_h", "center"))
        cosT, sinT, keep, mask48, mask32, seqm = (table(n) for n in ("cos", "sin", "keep", "mask48", "mask32", "seq"))
        decay_at, eps_at = cols["decay"][0], cols["eps"][0]

        ACC = ctx.enter_context(nc.psum_tensor("ACC", [P, 2, 2, 512], F32))
        OT = ctx.enter_context(nc.psum_tensor("OT", [P, 2, 512], F32))
        SCR = ctx.enter_context(nc.psum_tensor("SCR", [P, 2, 512], F32))

        consts_in, params_in, x_in = sem("consts_in"), sem("params_in"), sem("x_in")
        stage_full = [sem(f"stage_full{s}") for s in range(2)]
        w_hi = [sem(f"w_hi{s}") for s in range(2)]
        w_lo = [sem(f"w_lo{s}") for s in range(2)]
        half_used = sem("half_used")
        acc_full = sem("acc_full")
        acc_read = [sem(f"acc_read{s}") for s in range(2)]
        scr_full = sem("scr_full")
        scr_read = [sem(f"scr_read{s}") for s in range(2)]
        ot_full, ot_read = sem("ot_full"), sem("ot_read")
        params_ready, lb_max, lb_exp = sem("params_ready"), sem("lb_max"), sem("lb_exp")
        kv_zero = sem("kv_zero")
        y_ready, sq_ready, sq_used, sums_ready = sem("y_ready"), sem("sq_ready"), sem("sq_used"), sem("sums_ready")
        mu_ready, var_ready, rstd_ready, mr_ready = sem("mu_ready"), sem("var_ready"), sem("rstd_ready"), sem("mr_ready")
        ln_mul, ln_sub, ln_out, x_ready = sem("ln_mul"), sem("ln_sub"), sem("ln_out"), sem("x_ready")
        f_ready, lnf_parts, f2_ready, k_raw = sem("f_ready"), sem("lnf_parts"), sem("f2_ready"), sem("k_raw")
        q_clamped, q_sig, diff_ready, exps_ready = sem("q_clamped"), sem("q_sig"), sem("diff_ready"), sem("exps_ready")
        ew_ready, v_ready, g_raw, g_clamped, g_sig = (
            sem("ew_ready"), sem("v_ready"), sem("g_raw"), sem("g_clamped"), sem("g_sig"))
        tok_ready, vx_ready, pts_ready, states_ready = sem("tok_ready"), sem("vx_ready"), sem("pts_ready"), sem("states_ready")
        sn_ready, s0_in, sn_stored, fin_stored, fin_ready = (
            sem("sn_ready"), sem("s0_in"), sem("sn_stored"), sem("fin_stored"), sem("fin_ready"))
        o_copied, oc_ready, hsq_ready, hr_ready = sem("o_copied"), sem("oc_ready"), sem("hsq_ready"), sem("hr_ready")
        to_ready, oh_ready, ol_ready = sem("to_ready"), sem("oh_ready"), sem("ol_ready")
        cin_in, cst_ready, a_ready, conv_ready, gelu_ready = (
            sem("cin_in"), sem("cst_ready"), sem("a_ready"), sem("conv_ready"), sem("gelu_ready"))
        ht_ready, hh_ready, h_ready, cso_ready, cso_stored = (
            sem("ht_ready"), sem("hh_ready"), sem("h_ready"), sem("cso_ready"), sem("cso_stored"))
        out_ready, out_stored = sem("out_ready"), sem("out_stored")

        def halves(ap):
            return ap.rearrange("p (a n) -> p a n", a=2)

        def base(l):
            return tuple(s + l * n for s, n in zip(SCR_START, SCR_LAYER))

        def scr_hg(l, p):
            return Scratch(base(l), SCR_LN, tuple(p * n for n in SCR_HG))

        def scr_rt(l, p):
            return Scratch(base(l), SCR_LN, tuple(HEADS * n for n in SCR_HG), tuple(p * n for n in SCR_RT))

        def scr_cin(l):
            return scr_rt(l, HEADS)

        def scr_ln1(l):
            return Scratch(tuple(scr_rt(l, HEADS).job(0)[:1]) + tuple(scr_rt(l, HEADS).bank), (0, 1, 0))

        def scr_cout(l):
            s = scr_ln1(l)
            return Scratch((s.full, *s.bank), SCR_LN)

        def bcast(ap, n):
            return ap.unsqueeze(2).to_broadcast([ap.shape[0], ap.shape[1], n])

        block = ctx.enter_context(nc.Block())

        @block.sync
        def _(sp):
            xp = x_prompt.rearrange("b t d -> (b t) d")
            first = P - N_META
            sp.dma_start(XT[0:N_META, 0, :], meta_tokens).then_inc(x_in, 16)
            sp.dma_start(XT[N_META:P, 0, :], xp[0:first, :]).then_inc(x_in, 16)
            sp.dma_start(XT[:, 1:4, :], xp[first:first + 3 * P, :].rearrange("(i p) d -> p i d", p=P)).then_inc(x_in, 16)
            sp.dma_start(XT[0:TAIL, 4, :], xp[first + 3 * P:SEQ, :]).then_inc(x_in, 16)
            sp.dma_start(XT[TAIL:R5, 4, :], x_sample.rearrange("b t d -> (b t) d")).then_inc(x_in, 16)

            def load(s, j, halves_):
                sp.wait_ge(w_lo[s], j)
                for dst, src in halves_:
                    sp.dma_start(dst, src).then_inc(stage_full[s], 16)

            def unit(s):
                return stage[:, s, :].rearrange("p (k c) -> p k c", k=KT)

            def load_sections(s, j, l, p, sections):
                load(s, j, [(unit(s)[:, :, P * n:P * n + P], w_in_v[:, ds(l * KT, KT), ds(p * P + sec * HEADS * P, P)])
                            for n, sec in enumerate(sections)])

            def load_columns(s, j, l, w, c):
                load(s, j, [(unit(s)[:, k:k + KT // 2, :], w[:, ds(l * KT + k, KT // 2), ds(c, 2 * P)])
                            for k in (0, KT // 2)])

            def load_down(s, j, l, m, part_):
                d = stage[:, s, 0:UNIT_D].rearrange("p (k c) -> p k c", k=KD)
                load(s, j, [(d[:, a:b, :], w_down_v[:, ds(l * FT + part_ * KD + a, b - a), ds(m * P, P)])
                            for a, b in ((0, 6), (6, KD))])

            sp.wait_ge(scr_full, 1)
            with sp.Fori(0, DEPTH) as l:
                j0 = l * SLOT_UNITS
                with sp.Fori(0, HEADS) as p:
                    load_sections(0, j0 + p, l, p, (1, 0))
                    load_sections(1, j0 + p, l, p, (2, 3))
                with sp.Fori(0, HEADS) as p:
                    load_sections(0, j0 + HEADS + p, l, p, (5, 4))
                    load_sections(1, j0 + HEADS + p, l, p, (6, 7))
                with sp.Fori(0, 2) as i:
                    load_columns(0, j0 + 8 + i, l, w_o_v, i * 4 * P)
                    load_columns(1, j0 + 8 + i, l, w_o_v, i * 4 * P + 2 * P)
                with sp.Fori(0, FT // 2) as i:
                    load_columns(0, j0 + 10 + i, l, w_a_v, i * 2 * P)
                    load_columns(1, j0 + 10 + i, l, w_b_v, i * 2 * P)
                with sp.Fori(0, KT) as m:
                    load_down(0, j0 + 21 + m, l, m, 0)
                    load_down(1, j0 + 21 + m, l, m, 1)

        @block.gpsimd
        def _(pool):
            nc.gpsimd.memset(KV[:, :, :, :], 0.0).then_inc(kv_zero, 1)

            def move(ready, out, src, done):
                pool.wait_ge(params_ready, 1)
                pool.wait_ge(*ready)
                pool.dma_start(out, src).then_inc(done, 16)

            def norm_middle(n):
                pool.wait_ge(mr_ready, n + 1)
                for m in range(KT):
                    pool.wait_ge(ln_mul, n * KT + m + 1)
                    nc.gpsimd.tensor_tensor(X[:, m, :], X[:, m, :], MR[:, 0:T], ALU.subtract).then_inc(ln_sub, 1)

            def head_states(l, p, kind, s0_v, sn_v, fin_v, fin_src):
                hh = l * 2 * HEADS + kind * HEADS + p
                ot_done = l * OT_LAYER + 1 + (p if kind == 0 else HEADS + 2 * p)
                move((ot_full, ot_done), S0b, s0_v[ds(l * SEQS + p, DEC_BATCH, HEADS)].rearrange("b k v -> k b v"), s0_in)
                move((fin_ready, hh + 1), fin_v[ds((l * HEADS + p) * P, P), :], fin_src, fin_stored)
                move((sn_ready, hh + 1), sn_v[ds(l * SEQS + p, DEC_BATCH, HEADS)].rearrange("b k v -> k b v"), SNb, sn_stored)

            with pool.Fori(0, DEPTH) as l:
                norm_middle(2 * l)
                move((acc_full, l * TILES), CIN, cin_v[ds(l * 2 * DEC_BATCH, 2 * DEC_BATCH), :], cin_in)
                with pool.Fori(0, HEADS) as p:
                    head_states(l, p, 0, s0_hg_v, sn_hg_v, fin_hg_v, SC[:, (NC - 1) * P:NC * P])
                with pool.Fori(0, HEADS) as p:
                    head_states(l, p, 1, s0_rt_v, sn_rt_v, fin_rt_v, RSB[:, :])
                norm_middle(2 * l + 1)
                move((cso_ready, l + 1), cp_v[ds(l * 2, 2), :], CSO[0:2, :], cso_stored)
                move((cso_ready, l + 1), cs_v[ds(l * 2 * DEC_BATCH, 2 * DEC_BATCH), :], CSO[2:18, :], cso_stored)
            norm_middle(2 * DEPTH)
            pool.wait_ge(fin_stored, 16 * DEPTH * 2 * HEADS)
            pool.wait_ge(sn_stored, 16 * DEPTH * 2 * HEADS)
            pool.wait_ge(cso_stored, 32 * DEPTH)

        @block.tensor
        def _(pe):
            mm = nc.tensor.matmul

            def transpose_params():
                pe.wait_ge(consts_in, 16)
                pe.wait_ge(params_in, 16 * N_PARAM_DMAS)
                for b, (at_, n) in enumerate(((0, ROWS01), (P, ROWS01), (2 * P, ROWS2))):
                    last = nc.tensor.transpose(SCR[:, 0, at_:at_ + n], rows[0:n, b, :], ident[0:n, 0:n])
                last.then_inc(scr_full, 1)

            def transpose_x(scr):
                pe.wait_ge(x_in, 5 * 16)
                for i in range(TT5):
                    n = P if i < 4 else R5
                    for q in range(2):
                        bank = 1 - q
                        _, free = scr.job(bank)
                        pe.wait_ge(scr_read[bank], free)
                        for k in range(4):
                            last = nc.tensor.transpose(SCR[:, bank, k * P:k * P + n],
                                                       XT[0:n, i, (4 * q + k) * P:(4 * q + k + 1) * P], ident[0:n, 0:n])
                        last.then_inc(scr_full, 1)

            def norm_stats(n, ot, scr):
                pe.wait_ge(sums_ready, n + 1)
                pe.wait_ge(ot_read, ot)
                for h in range(2):
                    last = mm(OT[:, h, 0:HALF], ones_ln, S1[:, h * HALF:(h + 1) * HALF], start=True, stop=True)
                last.then_inc(ot_full, 1)
                for h in range(2):
                    _, free = scr.job(h)
                    pe.wait_ge(scr_read[h], free)
                    mm(SCR[:, h, 0:HALF], ones_ln, S2[:, h * HALF:(h + 1) * HALF], start=True, stop=True).then_inc(scr_full, 1)

            def products(acc, s, width, col, wk, xh, xl, xk, n, first, final, wait_k=None):
                for k in range(n):
                    if wait_k is not None:
                        pe.wait_ge(wait_k[0], wait_k[1] + k)
                    for w, x in ((WH, xh), (WH, xl), (WL, xh)):
                        lhs = w[:, s, wk(k) * width + col:wk(k) * width + col + P]
                        begin = first and k == 0 and w is WH and x is xh
                        end = final and k == n - 1 and w is WL
                        for h in range(2):
                            last = mm(ACC[:, acc, h, 0:HALF], lhs, x[:, xk + k, h * HALF:(h + 1) * HALF], start=begin, stop=end)
                return last

            def gemm_tile(l, j, s, c, half_tile, xh, xl, wait_k=None):
                if c == 0:
                    pe.wait_ge(w_lo[s], j + 1)
                pe.wait_ge(acc_read[c], l * ACC_TILES + half_tile)
                products(c, s, 2 * P, c * P, lambda k: k, xh, xl, 0, KT, True, True, wait_k).then_inc(acc_full, 1)

            def hg_a(l, p, scr):
                hh = l * 2 * HEADS + p
                pe.wait_ge(ew_ready, hh + 1)
                pe.wait_ge(v_ready, hh + 1)
                bank = 0
                for src in (KE, V):
                    for c0 in (0, 4, 8):
                        _, free = scr.job(bank)
                        pe.wait_ge(scr_read[bank], free)
                        for c in range(c0, min(c0 + 4, NC)):
                            n = P if c == c0 else C
                            last = nc.tensor.transpose(SCR[0:n, bank, (c - c0) * P:(c - c0 + 1) * P], src[:, C * c:C * c + n], ident)
                        last.then_inc(scr_full, 1)
                        bank = 1 - bank
                _, free = scr.job(0)
                pe.wait_ge(scr_read[0], free)
                for n, src in enumerate((KE, V)):
                    last = nc.tensor.transpose(SCR[0:TS, 0, n * P:(n + 1) * P], src[:, TP:T], ident)
                last.then_inc(scr_full, 1)

            def hg_b(l, p, scr):
                hh = l * 2 * HEADS + p
                for bank, chunks in ((1, range(0, 6)), (0, range(6, NC))):
                    _, free = scr.job(bank)
                    pe.wait_ge(scr_read[bank], free)
                    for c in chunks:
                        for i in range(NA):
                            o = (c - chunks[0]) * C + i * A
                            last = mm(SCR[0:C, bank, o:o + A], KV[:, c, i, :], QS[:, c * C + i * A:c * C + (i + 1) * A], start=True, stop=True)
                    if bank == 0:
                        last = mm(SCR[0:TS, 0, 5 * C:5 * C + TS], KVS[:, :], QD[:, TP:T], start=True, stop=True)
                    last.then_inc(scr_full, 1)
                pe.wait_ge(tok_ready, hh + 1)
                bank = 1
                for c0 in (0, 4, 8):
                    _, free = scr.job(bank)
                    pe.wait_ge(scr_read[bank], free)
                    for c in range(c0, min(c0 + 4, NC)):
                        last = mm(SCR[:, bank, (c - c0) * P:(c - c0 + 1) * P], KTOK[0:C, c * P:(c + 1) * P],
                                  VTOK[0:C, c * P:(c + 1) * P], start=True, stop=True)
                    last.then_inc(scr_full, 1)
                    bank = 1 - bank
                sample_steps(hh, scr, (0, 1))

            def sample_steps(hh, scr, banks):
                pe.wait_ge(vx_ready, hh + 1)
                for n, bank in enumerate(banks):
                    _, free = scr.job(bank)
                    pe.wait_ge(scr_read[bank], free)
                    mm(SCR[:, bank, :], KVTS[:, 0, :], VX[:, 4 * n:4 * n + 4, :].rearrange("p b v -> p (b v)"),
                       start=True, stop=True).then_inc(scr_full, 1)

            def sample_output(qs):
                cols_ = OT[:, 1, TP - SPLIT:REST]
                mm(cols_, KVTS[:, 1, :], PTSS[:, :], start=True, stop=False, skip_group_check=True)
                for b in range(DEC_BATCH):
                    last = mm(OT[:, 1, TP - SPLIT + DEC_SEQ * b:TP - SPLIT + DEC_SEQ * (b + 1)], S0b[:, b, :],
                              qs[:, TP + DEC_SEQ * b:TP + DEC_SEQ * (b + 1)], start=False, stop=(b == DEC_BATCH - 1),
                              skip_group_check=True)
                return last

            def hg_c(l, p):
                hh = l * 2 * HEADS + p
                pe.wait_ge(pts_ready, hh + 1)
                pe.wait_ge(states_ready, l * HEADS + p + 1)
                pe.wait_ge(s0_in, 16 * (hh + 1))
                pe.wait_ge(ot_read, l * OT_LAYER + 1 + p)
                for c in range(NC):
                    o = OT[:, c // 6, (c % 6) * C:(c % 6 + 1) * C]
                    if c:
                        mm(o, SC[:, (c - 1) * P:c * P], QD[:, C * c:C * c + C], start=True, stop=False)
                    mm(o, VTOK[0:C, c * P:(c + 1) * P], PTS[:, C * c:C * c + C], start=(c == 0), stop=True)
                sample_output(QD).then_inc(ot_full, 1)

            def hg_d(l, p, scr):
                pe.wait_ge(hsq_ready, l * 2 * HEADS + p + 1)
                for bank, (a, b) in enumerate(((0, SPLIT), (SPLIT, T))):
                    _, free = scr.job(bank)
                    pe.wait_ge(scr_read[bank], free)
                    mm(SCR[:, bank, 0:b - a], ones_h, SQ[:, a:b], start=True, stop=True).then_inc(scr_full, 1)

            def rt_a(l, p, scr):
                hh = l * 2 * HEADS + HEADS + p
                pe.wait_ge(ew_ready, hh + 1)
                pe.wait_ge(v_ready, hh + 1)
                for bank, src in enumerate((KE, V)):
                    _, free = scr.job(bank)
                    pe.wait_ge(scr_read[bank], free)
                    for i in range(4):
                        last = nc.tensor.transpose(SCR[:, bank, i * P:(i + 1) * P], src[:, i * P:(i + 1) * P], ident)
                    last.then_inc(scr_full, 1)
                _, free = scr.job(0)
                pe.wait_ge(scr_read[0], free)
                for n, src in enumerate((KE, V)):
                    nc.tensor.transpose(SCR[0:TAIL, 0, n * P:(n + 1) * P], src[:, 4 * P:TP], ident)
                    last = nc.tensor.transpose(SCR[0:TS, 0, (2 + n) * P:(3 + n) * P], src[:, TP:T], ident)
                last.then_inc(scr_full, 1)
                bank = 1
                for job in RT_JOBS:
                    _, free = scr.job(bank)
                    pe.wait_ge(scr_read[bank], free)
                    for i, t0, t1, o in job:
                        rows_ = P if i < 4 else TAIL
                        last = mm(SCR[0:rows_, bank, o:o + t1 - t0], KE[:, i * P:i * P + rows_], QD[:, t0:t1], start=True, stop=True)
                    if job is RT_JOBS[-1]:
                        last = mm(SCR[0:TS, bank, TAIL:TAIL + TS], KE[:, TP:T], QD[:, TP:T], start=True, stop=True)
                    last.then_inc(scr_full, 1)
                    bank = 1 - bank

            def rt_b(l, p, scr):
                hh = l * 2 * HEADS + HEADS + p
                pe.wait_ge(tok_ready, hh + 1)
                _, free = scr.job(0)
                pe.wait_ge(scr_read[0], free)
                for i in range(TT5):
                    r = P if i < 4 else TAIL
                    last = mm(SCR[:, 0, 0:P], KTOK[0:r, i * P:(i + 1) * P], VTOK[0:r, i * P:(i + 1) * P], start=(i == 0), stop=(i == 4))
                last.then_inc(scr_full, 1)
                sample_steps(hh, scr, (1, 0))
                pe.wait_ge(pts_ready, hh + 1)
                pe.wait_ge(s0_in, 16 * (hh + 1))
                pe.wait_ge(ot_read, l * OT_LAYER + 1 + HEADS + 2 * p)
                for h, (a, b) in enumerate(((0, SPLIT), (SPLIT, TP))):
                    tiles = [i for i in range(TT5) if i * P < b]
                    for i in tiles:
                        r, t0 = (P if i < 4 else TAIL), max(a, i * P)
                        mm(OT[:, h, t0 - a:b - a], VTOK[0:r, i * P:(i + 1) * P],
                           PTR[0:r, RT_OFF[i] + t0 - i * P:RT_OFF[i] + b - i * P], start=(i == 0), stop=(i == tiles[-1]),
                           skip_group_check=True)
                sample_output(QS).then_inc(ot_full, 1)

            def rt_c(l, p, scr):
                pe.wait_ge(o_copied, l * HEADS + p + 1)
                for bank, (a, b) in ((1, (0, SPLIT)), (0, (SPLIT, T))):
                    _, free = scr.job(bank)
                    pe.wait_ge(scr_read[bank], free)
                    mm(SCR[:, bank, 0:b - a], center, SQ[:, a:b], start=True, stop=True).then_inc(scr_full, 1)

            def rt_d(l, p):
                pe.wait_ge(hsq_ready, l * 2 * HEADS + HEADS + p + 1)
                pe.wait_ge(ot_read, l * OT_LAYER + 2 + HEADS + 2 * p)
                mm(OT[:, 0, 0:SPLIT], ones_h, SQ[:, 0:SPLIT], start=True, stop=True)
                mm(OT[:, 1, 0:REST], ones_h, SQ[:, SPLIT:T], start=True, stop=True).then_inc(ot_full, 1)

            def group(l, g, a=None, b=None, c=None, d=None):
                j = l * SLOT_UNITS + g
                stages = (a, b, c, d)
                for n in range(4):
                    if stages[n] is not None:
                        stages[n]()
                    gemm_tile(l, j, n // 2, n % 2, 2 * g + n // 2, XH, XL,
                              (x_ready, 2 * l * KT + 1) if n == 0 else None)

            transpose_params()
            transpose_x(Scratch((1, 1, 0)))
            with pe.Fori(0, DEPTH) as l:
                norm_stats(2 * l, l * OT_LAYER, Scratch(base(l)))
                group(l, 0)
                with pe.Fori(0, HEADS - 1) as p:
                    s = scr_hg(l, p)
                    group(l, p + 1, lambda: hg_a(l, p, s), lambda: hg_b(l, p, s), lambda: hg_c(l, p), lambda: hg_d(l, p, s))
                s, p = scr_hg(l, HEADS - 1), HEADS - 1
                group(l, HEADS, lambda: hg_a(l, p, s), lambda: hg_b(l, p, s), lambda: hg_c(l, p), lambda: hg_d(l, p, s))
                with pe.Fori(0, HEADS - 1) as p:
                    s = scr_rt(l, p)
                    group(l, p + HEADS + 1, lambda: rt_a(l, p, s), lambda: rt_b(l, p, s), lambda: rt_c(l, p, s), lambda: rt_d(l, p))
                s, p = scr_rt(l, HEADS - 1), HEADS - 1
                rt_a(l, p, s)
                rt_b(l, p, s)
                rt_c(l, p, s)
                rt_d(l, p)

                pe.wait_ge(cin_in, 16 * (l + 1))
                _, free = scr_cin(l).job(0)
                pe.wait_ge(scr_read[0], free)
                for f in range(FT):
                    last = mm(SCR[:, 0, f * 16:(f + 1) * 16], CIN[:, f * P:(f + 1) * P], ident[0:16, 0:16], start=True, stop=True)
                last.then_inc(scr_full, 1)

                with pe.Fori(0, 2) as i:
                    for n in range(4):
                        gemm_tile(l, l * SLOT_UNITS + 8 + i, n // 2, n % 2, O_TILE // 2 + 2 * i + n // 2, OH, OL,
                                  (ol_ready, l * 2 * HEADS + 1) if n == 0 else None)
                norm_stats(2 * l + 1, l * OT_LAYER + OT_LAYER - 1, scr_ln1(l))

                with pe.Fori(0, FT // 2) as i:
                    for n in range(4):
                        gemm_tile(l, l * SLOT_UNITS + 10 + i, n // 2, n % 2, F_TILE // 2 + 2 * i + n // 2, XH, XL,
                                  (x_ready, (2 * l + 1) * KT + 1) if n == 0 else None)

                pe.wait_ge(conv_ready, (l + 1) * FT)
                scr = scr_cout(l)
                for q in range(6):
                    bank = 1 - q % 2
                    _, free = scr.job(bank)
                    pe.wait_ge(scr_read[bank], free)
                    for f in range(4 * q, min(4 * q + 4, FT)):
                        last = nc.tensor.transpose(SCR[0:18, bank, (f - 4 * q) * P:(f - 4 * q + 1) * P], CSB[:, f, :], ident)
                    last.then_inc(scr_full, 1)

                with pe.Fori(0, KT // 2) as q:
                    for c in range(2):
                        j = l * SLOT_UNITS + 21 + 2 * q + c
                        pe.wait_ge(acc_read[c], l * ACC_TILES + D_TILE // 2 + q)
                        for s in range(2):
                            pe.wait_ge(w_lo[s], j + 1)
                            products(c, s, P, 0, lambda k: k, HH, HL, s * KD, KD, s == 0, s == 1,
                                     (h_ready, l * FT + s * KD + 1) if c == 0 else None
                                     ).then_inc(acc_full if s == 1 else half_used, 1)
            norm_stats(2 * DEPTH, DEPTH * OT_LAYER, Scratch(base(DEPTH)))
            scr = Scratch(base(DEPTH), SCR_LN)
            pe.wait_ge(ln_out, (2 * DEPTH + 1) * KT)
            for i in range(TT5):
                n = P if i < 4 else R5
                for q in range(2):
                    _, free = scr.job(q)
                    pe.wait_ge(scr_read[q], free)
                    for k in range(4):
                        last = nc.tensor.transpose(SCR[0:n, q, k * P:(k + 1) * P], X[:, 4 * q + k, i * P:i * P + n], ident)
                    last.then_inc(scr_full, 1)

        @block.scalar
        def _(act):
            f = nc.scalar.activation

            act.dma_start(tab[:, :], consts).then_inc(consts_in, 16)
            loads = []
            for l in range(DEPTH):
                loads.append((rows[0:CONV_W * FT, l, :], conv_w[l].rearrange("j (f p) -> (j f) p", p=P)))
                loads.append((rows[CONV_W * FT:ROWS01, l, :], conv_b[l].rearrange("(f p) -> f p", p=P)))
            norms = [(emb_ln_g, emb_ln_b)] + [pr for l in range(DEPTH) for pr in ((ln1_g[l], ln1_b[l]), (ln2_g[l], ln2_b[l]))]
            for n, pr in enumerate(norms):
                for h, src in enumerate(pr):
                    loads.append((rows[16 * n + 8 * h:16 * n + 8 * h + 8, 2, :], src.rearrange("(k p) -> k p", p=P)))
            for at_, src in ((ROW_HG, hg_norm_g), (ROW_RG, rt_gn_g), (ROW_RB, rt_gn_b), (ROW_LB, lb_logits)):
                loads.append((rows[at_:at_ + 8, 2, :], src.rearrange("l (h p) -> (l h) p", p=P)))
            assert len(loads) == N_PARAM_DMAS
            for dst, src in loads:
                act.dma_start(dst, src).then_inc(params_in, 16)

            def split_hi(s, j, used, width=UNIT):
                act.wait_ge(*used)
                act.wait_ge(stage_full[s], 32 * (j + 1))
                f(WH[:, s, 0:width], stage[:, s, 0:width], ACT.Copy, scale=W_SCALE).then_inc(w_hi[s], 1)

            def squares(n, m, y):
                act.wait_ge(y_ready, y)
                act.wait_ge(sq_used, n * KT + m)
                src = X[:, m, :] if isinstance(m, int) else X[:, ds(m, 1), :].rearrange("p o t -> p (o t)")
                f(SQT[:, 0:T], src, ACT.Square).then_inc(sq_ready, 1)

            def norm_apply(n, ot, last=False):
                act.wait_ge(ot_full, ot + 1)
                src = OT[:, :, 0:HALF]
                f(halves(MU[:, 0:T]), src, ACT.Copy)
                f(halves(MSQ[:, 0:T]), src, ACT.Square).then_inc(ot_read, 1)
                act.drain().then_inc(mu_ready, 1)
                act.wait_ge(var_ready, n + 1)
                f(RSTD[:, 0:T], VAR[:, 0:T], ACT.Ln, bias=tab[:, ds(eps_at + n, 1)])
                act.drain()
                f(RSTD[:, 0:T], RSTD[:, 0:T], ACT.Exp, scale=-0.5).then_inc(rstd_ready, 1)
                for m in range(KT):
                    act.wait_ge(ln_sub, n * KT + m + 1)
                    g, b = (par[:, ds(n * 16 + 2 * P + m + 8 * h, 1)] for h in range(2))
                    if not last:
                        f(XH[:, m, :], X[:, m, :], ACT.Identity, scale=g, bias=b)
                    f(X[:, m, :], X[:, m, :], ACT.Identity, scale=g, bias=b).then_inc(ln_out, 1)

            def sigmoid(buf, width, done):
                f(buf[:, 0:width], buf[:, 0:width], ACT.Exp, scale=-1.0)
                act.drain()
                f(buf[:, 0:width], buf[:, 0:width], ACT.Ln, bias=1.0)
                act.drain()
                f(buf[:, 0:width], buf[:, 0:width], ACT.Exp, scale=-1.0).then_inc(done, 1)

            def read_acc(buf, c, tile, done):
                act.wait_ge(acc_full, tile + 1)
                f(halves(buf[:, 0:T]), ACC[:, c, :, 0:HALF], ACT.Copy, scale=INV_W).then_inc(acc_read[c], 1)
                if done is not None:
                    act.drain().then_inc(done, 1)

            def hg_gate(l, p):
                n = l * HEADS + p
                act.wait_ge(f_ready, n + 1)
                f(T1[:, 0:T], Fb[:, 0:T], ACT.Exp, scale=-1.0)
                act.drain()
                f(T2[:, 0:T], T1[:, 0:T], ACT.Ln, bias=1.0)
                f(T3[:, 0:T], T1[:, 0:T], ACT.Ln, bias=1.0, scale=LBT[:, ds(n, 1)]).then_inc(lnf_parts, 1)
                act.wait_ge(f2_ready, n + 1)
                f(Fb[:, 0:T], Fb[:, 0:T], ACT.Exp, scale=-1.0).then_inc(k_raw, 1)

            def hg_query(l, p, tile):
                n = l * HEADS + p
                read_acc(Q, 1, tile, None)
                act.wait_ge(q_clamped, n + 1)
                sigmoid(T1, T, q_sig)
                act.wait_ge(diff_ready, n + 1)
                f(T2[:, 0:TP], T2[:, 0:TP], ACT.Exp)
                f(T3[:, 0:T], T3[:, 0:T], ACT.Exp)
                f(EN[:, :], B[:, TP:T], ACT.Exp, scale=-1.0)
                f(E[:, 0:T], B[:, 0:T], ACT.Exp)
                for i in range(NA):
                    w = KV[:, :, i, 0:A * (i + 1)]
                    last = f(w, w, ACT.Exp)
                last.then_inc(exps_ready, 1)

            def out_gate(hh, tile):
                read_acc(G, 1, tile, g_raw)
                act.wait_ge(g_clamped, hh + 1)
                sigmoid(T1, T, g_sig)

            def hg_a(l, p, scr):
                for dst in (KTOK, VTOK):
                    for c0 in (0, 4, 8):
                        n = min(c0 + 4, NC) - c0
                        bank = scr_bank[0]
                        full, _ = scr.job(bank)
                        act.wait_ge(scr_full, full)
                        f(dst[0:C, c0 * P:(c0 + n) * P], SCR[0:C, bank, 0:n * P], ACT.Copy).then_inc(scr_read[bank], 1)
                        scr_bank[0] = 1 - bank
                full, _ = scr.job(0)
                act.wait_ge(scr_full, full)
                f(KVTS[:, :, :], SCR[0:TS, 0, 0:2 * P].rearrange("p (n v) -> p n v", n=2), ACT.Copy).then_inc(scr_read[0], 1)
                act.drain().then_inc(tok_ready, 1)

            scr_bank = [0]

            def hg_c(l, p):
                act.wait_ge(ot_full, l * OT_LAYER + 2 + p)
                f(SQ[:, 0:SPLIT], OT[:, 0, 0:SPLIT], ACT.Square)
                f(SQ[:, SPLIT:T], OT[:, 1, 0:REST], ACT.Square).then_inc(hsq_ready, 1)

            def high_output(row, hh):
                act.wait_ge(to_ready, hh + 1)
                f(OH[:, ds(row, 1), :].rearrange("p o t -> p (o t)"), TO[:, :], ACT.Copy).then_inc(oh_ready, 1)

            eps_h = tab[:, eps_at + 5:eps_at + 6]

            def hg_d(l, p, scr):
                hh = l * 2 * HEADS + p
                for bank, (a, b) in enumerate(((0, SPLIT), (SPLIT, T))):
                    full, _ = scr.job(bank)
                    act.wait_ge(scr_full, full)
                    f(R[:, a:b], SCR[:, bank, 0:b - a], ACT.Ln, bias=eps_h).then_inc(scr_read[bank], 1)
                act.drain()
                f(R[:, :], R[:, :], ACT.Exp, scale=-0.5).then_inc(hr_ready, 1)
                high_output(p, hh)

            def hg_stages(l, p):
                s = scr_hg(l, p)
                scr_bank[0] = 0

                def d():
                    for b in (1, 0, 1, 0, 1, 0, 1):
                        s.job(b)
                    hg_d(l, p, s)
                return (lambda: hg_a(l, p, s)), None, (lambda: hg_c(l, p)), d

            def rt_a(l, p, scr):
                k_at = cols["k_dec"][0]
                full, _ = scr.job(0)
                act.wait_ge(scr_full, full)
                for i in range(4):
                    last = f(KTOK[:, i * P:(i + 1) * P], SCR[:, 0, i * P:(i + 1) * P], ACT.Copy, scale=tab[:, ds(k_at + i * HEADS + p, 1)])
                last.then_inc(scr_read[0], 1)
                full, _ = scr.job(1)
                act.wait_ge(scr_full, full)
                f(VTOK[:, 0:4 * P], SCR[:, 1, :], ACT.Copy).then_inc(scr_read[1], 1)
                full, _ = scr.job(0)
                act.wait_ge(scr_full, full)
                f(KTOK[0:TAIL, 4 * P:5 * P], SCR[0:TAIL, 0, 0:P], ACT.Copy, scale=tab[0:TAIL, ds(k_at + 4 * HEADS + p, 1)])
                f(VTOK[0:TAIL, 4 * P:5 * P], SCR[0:TAIL, 0, P:2 * P], ACT.Copy)
                f(KVTS[:, 0, :], SCR[0:TS, 0, 2 * P:3 * P], ACT.Copy, scale=tab[0:TS, ds(cols["k_dec_s"][0] + p, 1)])
                f(KVTS[:, 1, :], SCR[0:TS, 0, 3 * P:4 * P], ACT.Copy).then_inc(scr_read[0], 1)
                act.drain().then_inc(tok_ready, 1)
                for bank in (1, 0, 1, 0, 1):
                    scr.job(bank)

            def rt_b(l, p, scr):
                hh = l * 2 * HEADS + HEADS + p
                full, _ = scr.job(0)
                act.wait_ge(fin_stored, 16 * hh)
                act.wait_ge(scr_full, full)
                f(RSB[:, :], SCR[:, 0, 0:P], ACT.Copy).then_inc(scr_read[0], 1)
                act.drain().then_inc(fin_ready, 1)
                act.wait_ge(ot_full, l * OT_LAYER + 2 + HEADS + 2 * p)
                f(SQ[:, 0:SPLIT], OT[:, 0, 0:SPLIT], ACT.Copy)
                f(SQ[:, SPLIT:T], OT[:, 1, 0:REST], ACT.Copy).then_inc(ot_read, 1)
                act.drain().then_inc(o_copied, 1)

            def rt_c(l, p):
                act.wait_ge(oc_ready, l * HEADS + p + 1)
                f(SQ[:, :], TO[:, :], ACT.Square).then_inc(hsq_ready, 1)

            def rt_d(l, p):
                hh = l * 2 * HEADS + HEADS + p
                act.wait_ge(ot_full, l * OT_LAYER + 3 + HEADS + 2 * p)
                f(R[:, 0:SPLIT], OT[:, 0, 0:SPLIT], ACT.Ln, bias=eps_h)
                f(R[:, SPLIT:T], OT[:, 1, 0:REST], ACT.Ln, bias=eps_h).then_inc(ot_read, 1)
                act.drain()
                f(R[:, :], R[:, :], ACT.Exp, scale=-0.5).then_inc(hr_ready, 1)
                high_output(HEADS + p, hh)

            def rt_stages(l, p):
                s = scr_rt(l, p)
                return (lambda: rt_a(l, p, s)), (lambda: rt_b(l, p, s)), (lambda: rt_c(l, p)), (lambda: rt_d(l, p))

            def group(l, g, head, kind, stages=(None,) * 4):
                a, b, c, d = stages
                j, tile = l * SLOT_UNITS + g, l * TILES + 4 * g
                hh = l * 2 * HEADS + kind * HEADS + head
                split_hi(1, j, (acc_full, tile))
                if a is not None:
                    a()
                if kind == 0:
                    hg_gate(l, head)
                if b is not None:
                    b()
                if kind == 0:
                    hg_query(l, head, tile + 1)
                if c is not None:
                    c()
                split_hi(0, j + 1, (acc_full, tile + 2))
                read_acc(V, 0, tile + 2, v_ready)
                if d is not None:
                    d()
                out_gate(hh, tile + 3)

            act.wait_ge(scr_full, 1)
            for b, n in ((0, ROWS01), (1, ROWS01), (2, ROWS2)):
                last = f(par[:, b * P:b * P + n], SCR[:, 0, b * P:b * P + n], ACT.Copy)
            last.then_inc(scr_read[0], 1)
            act.drain().then_inc(params_ready, 1)
            nc.scalar.preload_act_table_set("natural_log_exp_and_others")
            act.wait_ge(lb_max, 1)
            f(LE[:, 1:3, :], LE[:, 1:3, :], ACT.Exp).then_inc(lb_exp, 1)
            with act.Fori(0, KT) as m:
                squares(0, m, 1)

            with act.Fori(0, DEPTH) as l:
                nc.scalar.preload_act_table_set("natural_log_exp_and_others")
                split_hi(0, l * SLOT_UNITS, (acc_full, l * TILES))
                norm_apply(2 * l, l * OT_LAYER)
                act.wait_ge(cso_stored, 32 * l)
                group(l, 0, 0, 0)
                with act.Fori(0, HEADS - 1) as p:
                    group(l, p + 1, p + 1, 0, hg_stages(l, p))
                group(l, HEADS, 0, 1, hg_stages(l, HEADS - 1))
                with act.Fori(0, HEADS - 1) as p:
                    group(l, p + HEADS + 1, p + 1, 1, rt_stages(l, p))
                for stage_ in rt_stages(l, HEADS - 1):
                    stage_()

                full, _ = scr_cin(l).job(0)
                act.wait_ge(scr_full, full)
                f(CST[:, :, :], SCR[:, 0, 0:FT * 16].rearrange("p (f b) -> p f b", f=FT), ACT.Copy).then_inc(scr_read[0], 1)
                act.drain().then_inc(cst_ready, 1)

                with act.Fori(0, 2) as i:
                    for n in range(4):
                        if n % 2 == 0:
                            split_hi(1 - n // 2, l * SLOT_UNITS + 8 + i + n // 2, (acc_full, l * TILES + O_TILE + 4 * i + n))
                        squares(2 * l + 1, 4 * i + n, 2 + 2 * l * KT + 4 * i + n)
                nc.scalar.preload_act_table_set("natural_log_exp_and_others")
                norm_apply(2 * l + 1, l * OT_LAYER + OT_LAYER - 1)

                nc.scalar.preload_act_table(ACT.Gelu_apprx_tanh)
                act.wait_ge(sn_stored, (l + 1) * 2 * HEADS * 16)
                act.wait_ge(fin_stored, (l + 1) * 2 * HEADS * 16)
                with act.Fori(0, FT // 2) as i:
                    n0 = l * FT + 2 * i
                    split_hi(1, l * SLOT_UNITS + 10 + i, (acc_full, l * TILES + F_TILE + 4 * i))
                    for c in range(2):
                        act.wait_ge(h_ready, n0)
                        act.wait_ge(acc_full, l * TILES + F_TILE + 4 * i + c + 1)
                        f(halves(AX[c][:, 2:2 + T]), ACC[:, c, :, 0:HALF], ACT.Copy, scale=INV_W)
                        f(halves(CX[c][:, 0:T]), ACC[:, c, :, 0:HALF], ACT.Identity, scale=CW2[:, ds(n0 + c, 1)],
                          bias=par[:, ds(l * P + CONV_W * FT + 2 * i + c, 1)]).then_inc(acc_read[c], 1)
                        act.drain().then_inc(a_ready, 1)
                    split_hi(0, l * SLOT_UNITS + 11 + i, (acc_full, l * TILES + F_TILE + 4 * i + 2))
                    for c in range(2):
                        act.wait_ge(conv_ready, n0 + c + 1)
                        f(CX[c][:, 0:T], CX[c][:, 0:T], ACT.Gelu_apprx_tanh).then_inc(gelu_ready, 1)
                    for c in range(2):
                        act.wait_ge(ht_ready, n0 + c + 1)
                        f(HH[:, ds(2 * i + c, 1), :].rearrange("p o t -> p (o t)"), CX[c][:, 0:T], ACT.Copy).then_inc(hh_ready, 1)

                scr = scr_cout(l)
                for q in range(6):
                    bank = 1 - q % 2
                    full, _ = scr.job(bank)
                    w = (min(4 * q + 4, FT) - 4 * q) * P
                    act.wait_ge(scr_full, full)
                    f(CSO[:, 4 * q * P:4 * q * P + w], SCR[0:18, bank, 0:w], ACT.Copy).then_inc(scr_read[bank], 1)
                act.drain().then_inc(cso_ready, 1)

                def down(q, last):
                    for c in range(2):
                        split_hi(1, l * SLOT_UNITS + 21 + 2 * q + c, (acc_full, l * TILES + D_TILE + 2 * q + c), UNIT_D)
                        if not (last and c == 1):
                            split_hi(0, l * SLOT_UNITS + 22 + 2 * q + c, (half_used, l * KT + 2 * q + c + 1), UNIT_D)
                        squares(2 * l + 2, 2 * q + c, 2 + (2 * l + 1) * KT + 2 * q + c)
                with act.Fori(0, KT // 2 - 1) as q:
                    down(q, False)
                down(KT // 2 - 1, True)
            nc.scalar.preload_act_table_set("natural_log_exp_and_others")
            norm_apply(2 * DEPTH, DEPTH * OT_LAYER, last=True)
            scr = Scratch(base(DEPTH), SCR_LN)
            for i in range(TT5):
                n = P if i < 4 else R5
                for q in range(2):
                    full, _ = scr.job(q)
                    act.wait_ge(scr_full, full)
                    last = f(XT[0:n, i, q * 512:(q + 1) * 512], SCR[0:n, q, :], ACT.Copy)
                    last.then_inc(scr_read[q], 1)
                act.drain().then_inc(out_ready, 1)
                act.wait_ge(out_ready, i + 1)
                yp = y_prompt.rearrange("b t d -> (b t) d")
                if i == 0:
                    act.dma_start(yp[0:P - N_META, :], XT[N_META:P, 0, :]).then_inc(out_stored, 16)
                elif i < 4:
                    act.dma_start(yp[i * P - N_META:(i + 1) * P - N_META, :], XT[:, i, :]).then_inc(out_stored, 16)
                else:
                    act.dma_start(yp[4 * P - N_META:SEQ, :], XT[0:TAIL, 4, :]).then_inc(out_stored, 16)
                    act.dma_start(y_sample.rearrange("b t d -> (b t) d"), XT[TAIL:R5, 4, :]).then_inc(out_stored, 16)
            act.wait_ge(out_stored, 16 * 6)

        @block.vector
        def _(dve):
            tt, ts, stt = nc.vector.tensor_tensor, nc.vector.tensor_scalar, nc.vector.scalar_tensor_tensor

            def split_lo(s, j, width=UNIT):
                dve.wait_ge(w_hi[s], j + 1)
                stt(out=WL[:, s, 0:width], in0=stage[:, s, 0:width], scalar=W_SCALE, in1=WH[:, s, 0:width],
                    op0=ALU.mult, op1=ALU.subtract).then_inc(w_lo[s], 1)

            def row(m):
                return X[:, m, :] if isinstance(m, int) else X[:, ds(m, 1), :].rearrange("p o t -> p (o t)")

            def zero_sums():
                nc.vector.memset(S1[:, 0:T], 0.0)
                nc.vector.memset(S2[:, 0:T], 0.0)
                dve.drain()

            def add_sums(n, m):
                tt(S1[:, 0:T], S1[:, 0:T], row(m), ALU.add)
                dve.wait_ge(sq_ready, n * KT + m + 1)
                tt(S2[:, 0:T], S2[:, 0:T], SQT[:, 0:T], ALU.add).then_inc(sq_used, 1)
                dve.drain()

            def residual(l, n, m, c, tile):
                dve.wait_ge(acc_full, l * TILES + tile + 1)
                stt(out=halves(row(m)), in0=ACC[:, c, :, 0:HALF], scalar=INV_W / ALPHA, in1=halves(row(m)),
                    op0=ALU.mult, op1=ALU.add).then_inc(acc_read[c], 1)
                dve.drain().then_inc(y_ready, 1)
                add_sums(n, m)

            def norm_apply(n, scr, last=False):
                dve.drain().then_inc(sums_ready, 1)
                dve.wait_ge(mu_ready, n + 1)
                for h in range(2):
                    full, _ = scr.job(h)
                    dve.wait_ge(scr_full, full)
                    tt(VAR[:, h * HALF:(h + 1) * HALF], SCR[:, h, 0:HALF], MSQ[:, h * HALF:(h + 1) * HALF],
                       ALU.subtract).then_inc(scr_read[h], 1)
                dve.drain()
                ts(VAR[:, 0:T], VAR[:, 0:T], 0.0, None, ALU.max).then_inc(var_ready, 1)
                dve.wait_ge(rstd_ready, n + 1)
                tt(MR[:, 0:T], MU[:, 0:T], RSTD[:, 0:T], ALU.mult).then_inc(mr_ready, 1)
                for m in range(KT + 2):
                    if m < KT:
                        tt(X[:, m, :], X[:, m, :], RSTD[:, 0:T], ALU.mult).then_inc(ln_mul, 1)
                    if m >= 2 and not last:
                        dve.wait_ge(ln_out, n * KT + m - 1)
                        tt(XL[:, m - 2, :], X[:, m - 2, :], XH[:, m - 2, :], ALU.subtract).then_inc(x_ready, 1)

            def hg_gate(l, p, tile):
                n = l * HEADS + p
                dve.wait_ge(acc_full, tile + 1)
                ts(halves(Fb[:, 0:T]), ACC[:, 0, :, 0:HALF], INV_W, CLAMP, ALU.mult, ALU.max).then_inc(acc_read[0], 1)
                dve.drain().then_inc(f_ready, 1)
                dve.wait_ge(lnf_parts, n + 1)
                tt(Fb[:, 0:T], Fb[:, 0:T], T2[:, 0:T], ALU.add).then_inc(f2_ready, 1)
                tt(T3[:, 0:T], T3[:, 0:T], T2[:, 0:T], ALU.subtract)
                dve.drain()
                ts(T3[:, 0:T], T3[:, 0:T], LOG_F_MIN, None, ALU.max)
                dve.drain()
                nc.vector.tensor_tensor_scan(B[:, 0:T], keep, T3[:, 0:T], 0.0, ALU.mult, ALU.add)
                dve.wait_ge(k_raw, n + 1)
                ts(Fb[:, 0:T], Fb[:, 0:T], OMLB[:, ds(n, 1)], None, ALU.mult)
                dve.drain()

            def hg_query(l, p, tile, mixed):
                n, hh = l * HEADS + p, l * 2 * HEADS + p
                Bc = B[:, 0:TP].rearrange("p (c t) -> p c t", c=NC)
                Kc = Fb[:, 0:TP].rearrange("p (c t) -> p c t", c=NC)
                dve.wait_ge(acc_full, tile + 1)
                dve.wait_ge(acc_read[1], (tile + 1) // 2 if isinstance(tile, int) else l * ACC_TILES + 2 * p + 1)
                ts(T1[:, 0:T], Q[:, 0:T], CLAMP, None, ALU.max).then_inc(q_clamped, 1)
                anchors = B[:, AT:TP:A]
                tt(T2[:, 0:TP].rearrange("p (a t) -> p a t", t=A), B[:, 0:TP].rearrange("p (a t) -> p a t", t=A),
                   bcast(anchors, A), ALU.subtract)
                tt(T3[:, 0:TP].rearrange("p (c t) -> p c t", c=NC), bcast(B[:, C - 1:TP:C], C), Bc, ALU.subtract)
                tt(T3[:, TP:T].rearrange("p (b t) -> p b t", t=DEC_SEQ), bcast(B[:, TP + DEC_SEQ - 1:T:DEC_SEQ], DEC_SEQ),
                   B[:, TP:T].rearrange("p (b t) -> p b t", t=DEC_SEQ), ALU.subtract)
                for i in range(NA):
                    w = A * (i + 1)
                    last = tt(KV[:, :, i, 0:w], bcast(B[:, A * i + AT:TP:C], w), Bc[:, :, 0:w], ALU.subtract)
                last.then_inc(diff_ready, 1)
                dve.wait_ge(q_sig, n + 1)
                tt(Q[:, 0:T], Q[:, 0:T], T1[:, 0:T], ALU.mult)
                dve.drain()
                dve.wait_ge(exps_ready, n + 1)
                tt(KE[:, 0:T], Fb[:, 0:T], T3[:, 0:T], ALU.mult)
                tt(KVS[:, :], Fb[:, TP:T], EN[:, :], ALU.mult)
                for i in range(NA):
                    w = A * (i + 1)
                    tt(KV[:, :, i, 0:w], KV[:, :, i, 0:w], Kc[:, :, 0:w], ALU.mult)
                tt(QS[:, 0:TP], Q[:, 0:TP], T2[:, 0:TP], ALU.mult)
                if mixed is not None:
                    dve.wait_ge(ot_full, mixed)
                tt(QD[:, 0:T], Q[:, 0:T], E[:, 0:T], ALU.mult)
                dve.drain().then_inc(ew_ready, 1)

            def rotate(c, dst):
                tt(halves(T1[0:64, 0:T]), ACC[64:P, c, :, 0:HALF], halves(sinT[64:P, :]), ALU.mult)
                tt(halves(T1[64:P, 0:T]), ACC[0:64, c, :, 0:HALF], halves(sinT[0:64, :]), ALU.mult)
                tt(halves(T2[:, 0:T]), ACC[:, c, :, 0:HALF], halves(cosT), ALU.mult).then_inc(acc_read[c], 1)
                dve.drain()
                tt(dst[:, 0:T], T1[:, 0:T], T2[:, 0:T], ALU.add)

            def rt_key(tile):
                dve.wait_ge(acc_full, tile + 1)
                rotate(0, KE)

            def rt_query(l, p, tile, mixed):
                dve.wait_ge(acc_full, tile + 1)
                if mixed is not None:
                    dve.wait_ge(ot_full, mixed)
                rotate(1, QD)
                dve.drain()
                tt(QS[:, TP:T], QD[:, TP:T], tab[:, ds(cols["q_dec"][0] + p * TS, TS)], ALU.mult)
                dve.drain().then_inc(ew_ready, 1)

            def out_gate(hh):
                dve.wait_ge(g_raw, hh + 1)
                ts(T1[:, 0:T], G[:, 0:T], CLAMP, None, ALU.max).then_inc(g_clamped, 1)
                dve.wait_ge(g_sig, hh + 1)
                tt(G[:, 0:T], G[:, 0:T], T1[:, 0:T], ALU.mult)
                dve.drain()

            def expand_values(hh):
                dve.wait_ge(tok_ready, hh + 1)
                tt(VX[:, :, :], KVTS[:, 1:2, :].to_broadcast([TS, DEC_BATCH, P]), bcast(seqm[0:TS, :], P),
                   ALU.mult).then_inc(vx_ready, 1)

            def sample_states(hh, scr, banks, decayed):
                dve.wait_ge(s0_in, 16 * (hh + 1))
                dve.wait_ge(sn_stored, 16 * hh)
                decayed()
                dve.drain()
                for n, bank in enumerate(banks):
                    full, _ = scr.job(bank)
                    dve.wait_ge(scr_full, full)
                    w = SN[:, 512 * n:512 * (n + 1)]
                    tt(w, w, SCR[:, bank, :], ALU.add).then_inc(scr_read[bank], 1)
                dve.drain().then_inc(sn_ready, 1)

            def hg_b(l, p, scr):
                hh = l * 2 * HEADS + p
                expand_values(hh)
                for bank, c0, n in ((1, 0, 6), (0, 6, 5)):
                    full, _ = scr.job(bank)
                    dve.wait_ge(scr_full, full)
                    last = tt(PTS[:, c0 * C:(c0 + n) * C].rearrange("p (c t) -> p c t", c=n),
                              SCR[0:C, bank, 0:n * C].rearrange("p (c t) -> p c t", c=n),
                              mask48[0:C, :].unsqueeze(1).to_broadcast([C, n, C]), ALU.mult)
                    if bank == 0:
                        last = tt(PTSS[:, :], SCR[0:TS, 0, 5 * C:5 * C + TS], mask32[0:TS, :], ALU.mult)
                    last.then_inc(scr_read[bank], 1)
                dve.drain().then_inc(pts_ready, 1)
                dve.wait_ge(fin_stored, 16 * hh)
                bank = 1
                for c0 in (0, 4, 8):
                    full, _ = scr.job(bank)
                    if c0:
                        dve.drain()
                    dve.wait_ge(scr_full, full)
                    for c in range(c0, min(c0 + 4, NC)):
                        u, s = SCR[:, bank, (c - c0) * P:(c - c0 + 1) * P], SC[:, c * P:(c + 1) * P]
                        if c == 0:
                            last = nc.vector.tensor_copy(s, u)
                        else:
                            if c > c0:
                                dve.drain()
                            last = stt(out=s, in0=SC[:, (c - 1) * P:c * P], scalar=E[:, C * c + C - 1:C * c + C], in1=u,
                                       op0=ALU.mult, op1=ALU.add)
                    last.then_inc(scr_read[bank], 1)
                    bank = 1 - bank
                dve.drain().then_inc(states_ready, 1)
                dve.drain().then_inc(fin_ready, 1)
                last_e = E[:, TP + DEC_SEQ - 1:T:DEC_SEQ]
                sample_states(hh, scr, (0, 1), lambda: tt(SNb, S0b, bcast(last_e, P), ALU.mult))

            def low_output(row_, hh):
                dve.wait_ge(oh_ready, hh + 1)
                tt(OL[:, ds(row_, 1), :].rearrange("p o t -> p (o t)"), TO[:, :], OH[:, ds(row_, 1), :].rearrange("p o t -> p (o t)"),
                   ALU.subtract).then_inc(ol_ready, 1)

            def hg_d(l, p):
                hh = l * 2 * HEADS + p
                dve.wait_ge(hr_ready, hh + 1)
                tt(TO[:, 0:SPLIT], OT[:, 0, 0:SPLIT], R[:, 0:SPLIT], ALU.mult)
                tt(TO[:, SPLIT:T], OT[:, 1, 0:REST], R[:, SPLIT:T], ALU.mult).then_inc(ot_read, 1)
                dve.drain()
                stt(out=TO[:, :], in0=TO[:, :], scalar=par[:, ds(l * HEADS + 2 * P + ROW_HG + p, 1)], in1=G[:, 0:T],
                    op0=ALU.mult, op1=ALU.mult).then_inc(to_ready, 1)
                low_output(p, hh)

            def hg_stages(l, p):
                s = scr_hg(l, p)
                for b in (0, 1, 0, 1, 0, 1, 0):
                    s.job(b)
                return None, (lambda: hg_b(l, p, s)), None, (lambda: hg_d(l, p))

            def rt_a(l, p, scr):
                hh = l * 2 * HEADS + HEADS + p
                bank = 1
                for job in RT_JOBS:
                    full, _ = scr.job(bank)
                    dve.wait_ge(scr_full, full)
                    for i, t0, t1, o in job:
                        r = P if i < 4 else TAIL
                        u, w = t0 - i * P, t1 - t0
                        last = tt(PTR[0:r, RT_OFF[i] + u:RT_OFF[i] + u + w], SCR[0:r, bank, o:o + w],
                                  tab[0:r, ds(decay_at + p * TP + u, w)], ALU.mult)
                    if job is RT_JOBS[-1]:
                        last = tt(PTSS[:, :], SCR[0:TS, bank, TAIL:TAIL + TS], tab[0:TS, ds(cols["mask_rt"][0] + p * TS, TS)], ALU.mult)
                    last.then_inc(scr_read[bank], 1)
                    bank = 1 - bank
                dve.drain().then_inc(pts_ready, 1)
                expand_values(hh)

            def rt_b(l, p, scr):
                hh = l * 2 * HEADS + HEADS + p
                scr.job(0)
                sample_states(hh, scr, (1, 0), lambda: ts(SN[:, :], S0[:, :], tab[:, ds(cols["gamma4"][0] + p, 1)], None, ALU.mult))

            def rt_c(l, p, scr):
                for bank, (a, b) in ((1, (0, SPLIT)), (0, (SPLIT, T))):
                    full, _ = scr.job(bank)
                    dve.wait_ge(scr_full, full)
                    nc.vector.tensor_copy(TO[:, a:b], SCR[:, bank, 0:b - a]).then_inc(scr_read[bank], 1)
                dve.drain().then_inc(oc_ready, 1)

            def rt_d(l, p):
                hh = l * 2 * HEADS + HEADS + p
                dve.wait_ge(hr_ready, hh + 1)
                tt(TO[:, :], TO[:, :], R[:, :], ALU.mult)
                dve.drain()
                ts(TO[:, :], TO[:, :], par[:, ds(l * HEADS + 2 * P + ROW_RG + p, 1)],
                   par[:, ds(l * HEADS + 2 * P + ROW_RB + p, 1)], ALU.mult, ALU.add)
                dve.drain()
                tt(TO[:, :], TO[:, :], G[:, 0:T], ALU.mult).then_inc(to_ready, 1)
                low_output(HEADS + p, hh)

            def rt_stages(l, p):
                s = scr_rt(l, p)
                for b in (0, 1, 0):
                    s.job(b)
                return (lambda: rt_a(l, p, s)), (lambda: rt_b(l, p, s)), (lambda: rt_c(l, p, s)), (lambda: rt_d(l, p))

            def group(l, g, head, kind, stages=(None,) * 4, mixed=None):
                a, b, c, d = stages
                j, tile = l * SLOT_UNITS + g, l * TILES + 4 * g
                hh = l * 2 * HEADS + kind * HEADS + head
                split_lo(1, j)
                if a is not None:
                    a()
                if kind == 0:
                    hg_gate(l, head, tile)
                else:
                    rt_key(tile)
                if b is not None:
                    b()
                if kind == 0:
                    hg_query(l, head, tile + 1, mixed)
                else:
                    rt_query(l, head, tile + 1, mixed)
                if c is not None:
                    c()
                split_lo(0, j + 1)
                if d is not None:
                    d()
                out_gate(hh)

            dve.wait_ge(params_ready, 1)
            lb = par[:, 2 * P + ROW_LB:2 * P + ROW_LB + 2 * HEADS].rearrange("p (l h) -> p l h", l=DEPTH)
            for l in range(DEPTH):
                ts(CW2[:, l * FT:(l + 1) * FT], par[:, l * P + 2 * FT:l * P + 3 * FT], INV_W, None, ALU.mult)
            tt(LE[:, 0, :], lb[:, 0, :], lb[:, 1, :], ALU.max)
            dve.drain()
            for l in range(DEPTH):
                last = tt(LE[:, 1 + l, :], lb[:, l, :], LE[:, 0, :], ALU.subtract)
            last.then_inc(lb_max, 1)
            dve.wait_ge(lb_exp, 1)
            tt(LE[:, 3, :], LE[:, 1, :], LE[:, 2, :], ALU.add)
            dve.drain()
            nc.vector.reciprocal(LE[:, 3, :], LE[:, 3, :])
            dve.drain()
            for l in range(DEPTH):
                tt(LE[:, 1 + l, :], LE[:, 1 + l, :], LE[:, 3, :], ALU.mult)
            dve.drain()
            tt(LBT[:, 0:HEADS], LE[:, 1, :], LE[:, 1, :], ALU.subtract)
            tt(LE[:, 4, :], LE[:, 1, :], LE[:, 2, :], ALU.add)
            dve.drain()
            tt(LBT[:, HEADS:2 * HEADS], LE[:, 4, :], LE[:, 1, :], ALU.subtract)
            dve.drain()
            ts(OMLB[:, :], LBT[:, :], -1.0, 1.0, ALU.mult, ALU.add)
            dve.drain()

            scr = Scratch((1, 1, 0))
            for i in range(TT5):
                n = P if i < 4 else R5
                for q in range(2):
                    full, _ = scr.job(1 - q)
                    dve.wait_ge(scr_full, full)
                    nc.vector.tensor_copy(X[:, 4 * q:4 * q + 4, i * P:i * P + n],
                                          SCR[:, 1 - q, :].rearrange("p (k t) -> p k t", k=4)[:, :, 0:n]).then_inc(scr_read[1 - q], 1)
            dve.drain().then_inc(y_ready, 1)
            dve.wait_ge(kv_zero, 1)
            zero_sums()
            with dve.Fori(0, KT) as m:
                add_sums(0, m)

            with dve.Fori(0, DEPTH) as l:
                ot0 = l * OT_LAYER
                split_lo(0, l * SLOT_UNITS)
                norm_apply(2 * l, Scratch(base(l)))
                group(l, 0, 0, 0)
                with dve.Fori(0, HEADS - 1) as p:
                    group(l, p + 1, p + 1, 0, hg_stages(l, p), ot0 + 2 + p)
                group(l, HEADS, 0, 1, hg_stages(l, HEADS - 1), ot0 + 1 + HEADS)
                with dve.Fori(0, HEADS - 1) as p:
                    group(l, p + HEADS + 1, p + 1, 1, rt_stages(l, p), ot0 + 2 + HEADS + 2 * p)
                for stage_ in rt_stages(l, HEADS - 1):
                    stage_()

                zero_sums()
                with dve.Fori(0, 2) as i:
                    for n in range(4):
                        if n % 2 == 0:
                            split_lo(1 - n // 2, l * SLOT_UNITS + 8 + i + n // 2)
                        residual(l, 2 * l + 1, 4 * i + n, n % 2, O_TILE + 4 * i + n)
                norm_apply(2 * l + 1, scr_ln1(l))

                dve.wait_ge(cst_ready, l + 1)
                dve.wait_ge(sn_stored, (l + 1) * 2 * HEADS * 16)
                dve.wait_ge(fin_stored, (l + 1) * 2 * HEADS * 16)
                for c in range(2):
                    nc.vector.memset(AX[c][:, 0:2], 0.0)
                dve.drain()
                with dve.Fori(0, FT // 2) as i:
                    n0 = l * FT + 2 * i
                    split_lo(1, l * SLOT_UNITS + 10 + i)
                    for c in range(2):
                        ax, cx, ft = AX[c], CX[c], 2 * i + c
                        w0, w1 = (par[:, ds(l * P + n * FT + 2 * i + c, 1)] for n in range(2))
                        dve.wait_ge(a_ready, n0 + c + 1)
                        nc.vector.tensor_copy(AS[:, :, 2:6], ax[:, 2 + TP:2 + T].rearrange("p (b t) -> p b t", t=DEC_SEQ))
                        nc.vector.tensor_copy(AS[:, :, 0:2], CST[:, ds(ft, 1), :].rearrange("p o (b j) -> p (o b) j", j=2))
                        stt(out=cx[:, 0:TP], in0=ax[:, 1:1 + TP], scalar=w1, in1=cx[:, 0:TP], op0=ALU.mult, op1=ALU.add)
                        dve.drain()
                        cs = cx[:, TP:T].rearrange("p (b t) -> p b t", t=DEC_SEQ)
                        stt(out=cs, in0=AS[:, :, 1:5], scalar=w1, in1=cs, op0=ALU.mult, op1=ALU.add)
                        stt(out=cx[:, 0:TP], in0=ax[:, 0:TP], scalar=w0, in1=cx[:, 0:TP], op0=ALU.mult, op1=ALU.add)
                        nc.vector.tensor_copy(CSB[:, ds(ft, 1), 0:2].rearrange("p o j -> p (o j)"), ax[:, TP:TP + 2])
                        nc.vector.tensor_copy(CSB[:, ds(ft, 1), 2:18].rearrange("p o (b j) -> p (o b) j", j=2), AS[:, :, 4:6])
                        dve.drain()
                        stt(out=cs, in0=AS[:, :, 0:4], scalar=w0, in1=cs, op0=ALU.mult, op1=ALU.add)
                        dve.drain().then_inc(conv_ready, 1)
                    split_lo(0, l * SLOT_UNITS + 11 + i)
                    for c in range(2):
                        cx = CX[c]
                        dve.wait_ge(gelu_ready, n0 + c + 1)
                        dve.wait_ge(acc_full, l * TILES + F_TILE + 4 * i + 3 + c)
                        stt(out=halves(cx[:, 0:T]), in0=ACC[:, c, :, 0:HALF], scalar=INV_W, in1=halves(cx[:, 0:T]),
                            op0=ALU.mult, op1=ALU.mult).then_inc(acc_read[c], 1)
                        dve.drain().then_inc(ht_ready, 1)
                    for c in range(2):
                        one = lambda t: t[:, ds(2 * i + c, 1), :].rearrange("p o t -> p (o t)")
                        dve.wait_ge(hh_ready, n0 + c + 1)
                        tt(one(HL), CX[c][:, 0:T], one(HH), ALU.subtract).then_inc(h_ready, 1)

                zero_sums()

                def down(q, last):
                    for c in range(2):
                        split_lo(1, l * SLOT_UNITS + 21 + 2 * q + c, UNIT_D)
                        if not (last and c == 1):
                            split_lo(0, l * SLOT_UNITS + 22 + 2 * q + c, UNIT_D)
                        residual(l, 2 * l + 2, 2 * q + c, c, D_TILE + 2 * q + c)
                with dve.Fori(0, KT // 2 - 1) as q:
                    down(q, False)
                down(KT // 2 - 1, True)
            norm_apply(2 * DEPTH, Scratch(base(DEPTH)), last=True)


N_PARAM_DMAS = 2 * DEPTH + 2 * (2 * DEPTH + 1) + 4
RT_JOBS = [[(0, 0, SPLIT, 0)], [(0, SPLIT, TP, 0)], [(1, P, TP, 0)],
           [(2, 2 * P, TP, 0), (3, 3 * P, TP, TP - 2 * P)], [(4, 4 * P, TP, 0)]]


_INS = ['x_prompt', 'x_sample', 'state_hgrn', 'state_ret', 'state_conv', 'meta_tokens', 'emb_ln_g', 'emb_ln_b',
        'lb_logits', 'w_in', 'hg_norm_g', 'rt_gn_g', 'rt_gn_b', 'w_o', 'ln1_g', 'ln1_b', 'w_a', 'w_b', 'conv_w',
        'conv_b', 'w_down', 'ln2_g', 'ln2_b']
_OUTS = [(1, SEQ, D_MODEL), (DEC_BATCH, DEC_SEQ, D_MODEL), (DEPTH, 1, HEADS, P, P), (DEPTH, DEC_BATCH, HEADS, P, P),
         (DEPTH, 1, HEADS, P, P), (DEPTH, DEC_BATCH, HEADS, P, P), (DEPTH, 1, CONV_W - 1, D_FF),
         (DEPTH, DEC_BATCH, CONV_W - 1, D_FF)]


def kernel(**inputs):
    import concourse.bacc as _bacc
    from concourse.bass_utils import run_bass_kernel_spmd as _run

    nc = _bacc.Bacc("TRN2", target_bir_lowering=False, num_devices=1)
    arrays, args = {}, []
    for name in _INS:
        a = np.ascontiguousarray(inputs[name])
        arrays[f"in_{name}_dram"] = a
        args.append(nc.dram_tensor(f"in_{name}_dram", a.shape, mybir.dt.from_np(a.dtype), kind="ExternalInput").ap())
    tables = const_tables()
    arrays["in_tables_dram"] = tables
    args.append(nc.dram_tensor("in_tables_dram", tables.shape, F32, kind="ExternalInput").ap())
    for i, shape in enumerate(_OUTS):
        args.append(nc.dram_tensor(f"out_{i}_dram", shape, F32, kind="ExternalOutput").ap())
    hybrid_decoder_step(nc, *args)
    r = _run(nc, [arrays], core_ids=[0])
    return tuple(r.results[0][f"out_{i}_dram"] for i in range(len(_OUTS)))
```

```python
from contextlib import ExitStack

import concourse.bass as bass
import numpy as np
from concourse import mybir

F32 = mybir.dt.float32
F16 = mybir.dt.float16
ALU = mybir.AluOpType
ACT = mybir.ActivationFunctionType

P = 128
D_MODEL = 1024
DEPTH = 2
SEQ = 512
N_META = 16
DEC_BATCH = 8
DEC_SEQ = 4
PAST_LEN = 4096
HEADS = 4
D_FF = 2816
CONV_W = 3
LN_EPS = 1e-5
LOG_F_MIN = float(np.log(1e-6))
ALPHA = (2 * DEPTH) ** 0.25

TP = N_META + SEQ
TS = DEC_BATCH * DEC_SEQ
T = TP + TS
HALF = T // 2
KT = D_MODEL // P
FT = D_FF // P
KD = FT // 2
UNIT = KT * 2 * P
UNIT_D = KD * P
W_SCALE = 64.0
INV_W = 1.0 / W_SCALE

C = 96
CHUNKS = [(t, min(C, TP - t)) for t in range(0, TP, C)]
NC = len(CHUNKS)
LEVELS = (48, 24, 12, 6)
A = 6
AT = 2
SPLIT = 3 * C
REST = T - SPLIT
CLAMP = -44.0

TT5 = 5
R5 = T - 4 * P
TAIL = TP - 4 * P
RT_COLS = [TP - P * i for i in range(TT5)]
RT_OFF = [sum(RT_COLS[:i]) for i in range(TT5)]

U_P, U_O, U_F, U_D = 16, 4, 22, 16
SLOT_UNITS = (U_P + U_O + U_F + U_D) // 2
TILES = 32 + 8 + 2 * FT + 8
ACC_TILES = TILES // 2
O_TILE, F_TILE, D_TILE = 32, 40, 40 + 2 * FT
SCR_START = (11, 6, 5)
SCR_LN = (2, 1, 1)
SCR_HG = (17, 8, 9)
SCR_RT = (13, 7, 6)
SCR_CIN = (1, 1, 0)
SCR_COUT = (6, 3, 3)
SCR_LAYER = tuple(2 * a + HEADS * (b + c) + d + e for a, b, c, d, e in zip(SCR_LN, SCR_HG, SCR_RT, SCR_CIN, SCR_COUT))
OT_LAYER = 2 + HEADS + 2 * HEADS
ROW_HG, ROW_RG, ROW_RB, ROW_LB, ROWS2 = 80, 88, 96, 104, 112
ROWS01 = (CONV_W + 1) * FT


def const_columns():
    at, out = 0, {}
    for name, width in [("ident", P), ("ones_ln", P), ("ones_h", P), ("center", P), ("eps", 8), ("cos", T), ("sin", T),
                        ("keep", T), ("masks", len(LEVELS) * C), ("mask32", TS), ("seq", DEC_BATCH), ("decay", HEADS * TP),
                        ("mask_rt", HEADS * TS), ("q_dec", HEADS * TS), ("k_dec", TT5 * HEADS), ("k_dec_s", HEADS),
                        ("gamma4", HEADS)]:
        out[name] = (at, width)
        at += width
    return out, at


def const_tables():
    cols, n = const_columns()
    tab = np.zeros((P, n), np.float32)

    def put(name, value):
        at, width = cols[name]
        value = np.asarray(value, np.float32).reshape(len(value), width)
        tab[:len(value), at:at + width] = value

    put("ident", np.eye(P))
    put("ones_ln", np.full((P, P), 1.0 / D_MODEL))
    put("ones_h", np.full((P, P), 1.0 / P))
    put("center", np.eye(P) - 1.0 / P)
    eps = np.zeros((P, 8))
    eps[:, 0] = LN_EPS
    eps[:, 1:5] = LN_EPS / ALPHA ** 2
    eps[:, 5] = LN_EPS
    put("eps", eps)
    half = P // 2
    inv = np.float32(10000.0) ** (-np.arange(half, dtype=np.float32) / np.float32(half))
    pos = np.concatenate([np.arange(TP), np.tile(PAST_LEN + np.arange(DEC_SEQ), DEC_BATCH)]).astype(np.float32)
    ang = inv[:, None] * pos[None, :]
    put("cos", np.concatenate([np.cos(ang)] * 2) * INV_W)
    put("sin", np.concatenate([np.sin(ang), -np.sin(ang)]) * INV_W)
    keep = np.ones((P, T))
    keep[:, 0:TP:C] = 0
    keep[:, TP::DEC_SEQ] = 0
    put("keep", keep)
    s, t = np.arange(C)[:, None], np.arange(C)[None, :]
    levels = [(s // (2 * h) == t // (2 * h)) & (s % (2 * h) < h) & (t % (2 * h) >= h) for h in LEVELS[1:]]
    put("masks", np.concatenate(levels + [(s // A == t // A) & (s <= t)], 1))
    tok = np.arange(TS)
    same = tok[:, None] // DEC_SEQ == tok[None, :] // DEC_SEQ
    causal = same & (tok[:, None] <= tok[None, :])
    put("mask32", causal)
    put("seq", tok[:, None] // DEC_SEQ == np.arange(DEC_BATCH)[None, :])
    log_g = np.log1p(-np.exp2(-5.0 - np.arange(HEADS)))
    s, u = np.arange(P)[:, None, None], np.arange(TP)[None, None, :]
    root = P ** -0.5
    rel = np.maximum(u - s, 0)
    put("decay", np.where(u >= s, np.exp(rel * log_g[None, :, None]), 0.0) * root)
    rel = np.maximum(tok[None, :] - tok[:, None], 0)
    put("mask_rt", np.where(causal[:, None, :], np.exp(rel[:, None, :] * log_g[None, :, None]), 0.0) * root)
    put("q_dec", np.broadcast_to(np.exp((tok % DEC_SEQ + 1)[None, None, :] * log_g[None, :, None]), (P, HEADS, TS)))
    left = TP - 1 - (np.arange(TT5)[None, :, None] * P + np.arange(P)[:, None, None])
    put("k_dec", np.where(left >= 0, np.exp(np.maximum(left, 0) * log_g[None, None, :]), 0.0) * root)
    put("k_dec_s", np.exp((DEC_SEQ - 1 - tok % DEC_SEQ)[:, None] * log_g[None, :]) * root)
    put("gamma4", np.broadcast_to(np.exp(DEC_SEQ * log_g), (P, HEADS)))
    return tab


class Scratch:

    def __init__(self, base, *done):
        self.full, self.bank = base[0], [base[1], base[2]]
        for d in done:
            self.full, self.bank = self.full + d[0], [self.bank[0] + d[1], self.bank[1] + d[2]]

    def job(self, bank):
        free = self.bank[bank]
        self.full, self.bank[bank] = self.full + 1, free + 1
        return self.full, free


def hybrid_decoder_step(nc, x_prompt, x_sample, state_hgrn, state_ret, state_conv, meta_tokens, emb_ln_g, emb_ln_b,
                        lb_logits, w_in, hg_norm_g, rt_gn_g, rt_gn_b, w_o, ln1_g, ln1_b, w_a, w_b, conv_w, conv_b,
                        w_down, ln2_g, ln2_b, consts, y_prompt, y_sample, hg_prompt, hg_sample, rt_prompt,
                        rt_sample, conv_prompt, conv_sample):
    cols, n_const = const_columns()
    ds = bass.ds

    w_in_v = w_in.rearrange("l (k p) c -> p (l k) c", p=P)
    w_o_v = w_o.rearrange("l (k p) c -> p (l k) c", p=P)
    w_a_v = w_a.rearrange("l (k p) c -> p (l k) c", p=P)
    w_b_v = w_b.rearrange("l (k p) c -> p (l k) c", p=P)
    w_down_v = w_down.rearrange("l (k p) c -> p (l k) c", p=P)
    s0_hg_v = state_hgrn.rearrange("l b h k v -> (l b h) k v")
    s0_rt_v = state_ret.rearrange("l b h k v -> (l b h) k v")
    sn_hg_v = hg_sample.rearrange("l b h k v -> (l b h) k v")
    sn_rt_v = rt_sample.rearrange("l b h k v -> (l b h) k v")
    fin_hg_v = hg_prompt.rearrange("l b h k v -> (l b h k) v")
    fin_rt_v = rt_prompt.rearrange("l b h k v -> (l b h k) v")
    cin_v = state_conv.rearrange("l b j f -> (l b j) f")
    cp_v = conv_prompt.rearrange("l b j f -> (l b j) f")
    cs_v = conv_sample.rearrange("l b j f -> (l b j) f")
    SEQS = DEC_BATCH * HEADS

    with ExitStack() as ctx:
        def sb(name, shape, dt=F32):
            return ctx.enter_context(nc.sbuf_tensor(name, shape, dt))

        def sem(name):
            return ctx.enter_context(nc.semaphore(name))

        tab = sb("tab", [P, n_const])
        X = sb("X", [P, KT, T])
        XH, XL = sb("XH", [P, KT, T], F16), sb("XL", [P, KT, T], F16)
        OHL = sb("OHL", [P, 2 * KT, T], F16)
        OH, OL = OHL[:, 0:KT, :], OHL[:, KT:2 * KT, :]
        stage = sb("stage", [P, 2, UNIT])
        WH, WL = sb("WH", [P, 2, UNIT], F16), sb("WL", [P, 2, UNIT], F16)
        shared = sb("shared", [P, FT * T])
        HHL = shared[:, :].bitcast(F16).rearrange("p (k t) -> p k t", k=2 * FT)
        HH, HL = HHL[:, 0:FT, :], HHL[:, FT:2 * FT, :]
        Z = sb("Z", [P, len(LEVELS), TP])
        DK, DQ = sb("DK", [P, TP]), sb("DQ", [P, TP])
        Fb, T1, T2, T3, B, Q, QS, QD, KE, E, V, G = (
            sb(n, [P, T + 2]) for n in ("Fb", "T1", "T2", "T3", "B", "Q", "QS", "QD", "KE", "E", "V", "G"))
        at = [0]

        def part(width):
            at[0] += width
            return shared[:, at[0] - width:at[0]]

        KTOK, VTOK, SC = part(NC * P), part(NC * P), part(NC * P)
        KVTOK = shared[:, 0:2 * NC * P].rearrange("p (n c) -> p n c", n=2)
        S0, SN = part(DEC_BATCH * P), part(DEC_BATCH * P)
        PTR = part(RT_OFF[-1] + TAIL)
        SQ, R, TO = part(T), part(T), part(T)
        assert at[0] <= FT * T - D_FF
        CIN = shared[0:2 * DEC_BATCH, FT * T - D_FF:FT * T]
        CSO = OHL[:, :, :].rearrange("p k t -> p (k t)").bitcast(F32)[0:2 + 2 * DEC_BATCH, 0:D_FF]
        XT = shared[:, 0:TT5 * D_MODEL].rearrange("p (i d) -> p i d", i=TT5)
        S0b, SNb = (t.rearrange("p (b v) -> p b v", b=DEC_BATCH) for t in (S0, SN))
        S1, S2, SQT, MU, MSQ, VAR, RSTD, MR = B, Q, E, T1, T2, T3, QS, QD
        AX, CX = (T1, T2), (T3, Fb)
        VX = sb("VX", [TS, DEC_BATCH, P])
        KVTS = sb("KVTS", [TS, 2, P])
        PTS = sb("PTS", [C, TP])
        PTSS = sb("PTSS", [TS, TS])
        RSB = sb("RSB", [P, P])
        KVS = sb("KVS", [P, TS])
        EN = sb("EN", [P, TS])
        AS = sb("AS", [P, DEC_BATCH, CONV_W - 1 + DEC_SEQ])
        CST = sb("CST", [P, FT, 2 * DEC_BATCH])
        CSB = sb("CSB", [P, FT, 2 + 2 * DEC_BATCH])
        rows = stage[:, 1, 0:3 * P].rearrange("p (b c) -> p b c", b=3)
        unread = sb("unread", [1, 3])
        wait_spot = sb("wait_spot", [1, 1])
        par = sb("par", [P, 3 * P])
        CW2 = sb("CW2", [P, DEPTH * FT])
        LBT, OMLB = sb("LBT", [P, DEPTH * HEADS]), sb("OMLB", [P, DEPTH * HEADS])
        LE = sb("LE", [P, 6, HEADS])

        def table(name):
            a, w = cols[name]
            return tab[:, a:a + w]

        ident, ones_ln, ones_h, center = (table(n) for n in ("ident", "ones_ln", "ones_h", "center"))
        cosT, sinT, keep, mask32, seqm = (table(n) for n in ("cos", "sin", "keep", "mask32", "seq"))
        masks = table("masks").rearrange("p (n t) -> p n t", t=C)
        decay_at, eps_at = cols["decay"][0], cols["eps"][0]

        ACC = ctx.enter_context(nc.psum_tensor("ACC", [P, 2, 2, 512], F32))
        OT = ctx.enter_context(nc.psum_tensor("OT", [P, 2, 512], F32))
        SCR = ctx.enter_context(nc.psum_tensor("SCR", [P, 2, 512], F32))

        consts_in, params_in, x_in = sem("consts_in"), sem("params_in"), sem("x_in")
        stage_full = [sem(f"stage_full{s}") for s in range(2)]
        w_hi = [sem(f"w_hi{s}") for s in range(2)]
        w_lo = [sem(f"w_lo{s}") for s in range(2)]
        half_used = sem("half_used")
        acc_full = sem("acc_full")
        acc_read = [sem(f"acc_read{s}") for s in range(2)]
        scr_full = sem("scr_full")
        scr_read = [sem(f"scr_read{s}") for s in range(2)]
        ot_full, ot_read = sem("ot_full"), sem("ot_read")
        params_ready, lb_max, lb_exp = sem("params_ready"), sem("lb_max"), sem("lb_exp")
        pts_zero = sem("pts_zero")
        y_ready, sq_ready, sq_used, sums_ready = sem("y_ready"), sem("sq_ready"), sem("sq_used"), sem("sums_ready")
        mu_ready, var_ready, rstd_ready, mr_ready = sem("mu_ready"), sem("var_ready"), sem("rstd_ready"), sem("mr_ready")
        ln_mul, ln_sub, ln_out, x_ready = sem("ln_mul"), sem("ln_sub"), sem("ln_out"), sem("x_ready")
        f_ready, lnf_parts, f2_ready, k_raw = sem("f_ready"), sem("lnf_parts"), sem("f2_ready"), sem("k_raw")
        q_clamped, q_sig, diff_ready, exps_ready = sem("q_clamped"), sem("q_sig"), sem("diff_ready"), sem("exps_ready")
        ew_ready, v_ready, g_raw, g_clamped, g_sig, g_ready = (
            sem(n) for n in ("ew_ready", "v_ready", "g_raw", "g_clamped", "g_sig", "g_ready"))
        tok_ready, vx_ready, pts_ready, states_ready = sem("tok_ready"), sem("vx_ready"), sem("pts_ready"), sem("states_ready")
        sn_ready, s0_in, sn_stored, fin_stored, fin_ready = (
            sem("sn_ready"), sem("s0_in"), sem("sn_stored"), sem("fin_stored"), sem("fin_ready"))
        o_copied, oc_ready, hsq_ready, hr_ready = sem("o_copied"), sem("oc_ready"), sem("hsq_ready"), sem("hr_ready")
        to_ready, oh_ready, ol_ready = sem("to_ready"), sem("oh_ready"), sem("ol_ready")
        cin_in, cst_ready, a_ready, conv_ready, gelu_ready = (
            sem("cin_in"), sem("cst_ready"), sem("a_ready"), sem("conv_ready"), sem("gelu_ready"))
        ht_ready, hh_ready, h_ready, cso_ready, cso_stored = (
            sem("ht_ready"), sem("hh_ready"), sem("h_ready"), sem("cso_ready"), sem("cso_stored"))
        out_ready, out_stored = sem("out_ready"), sem("out_stored")

        def halves(ap):
            return ap.rearrange("p (a n) -> p a n", a=2)

        def base(l):
            return tuple(s + l * n for s, n in zip(SCR_START, SCR_LAYER))

        def scr_hg(l, p):
            return Scratch(base(l), SCR_LN, tuple(p * n for n in SCR_HG))

        def scr_rt(l, p):
            return Scratch(base(l), SCR_LN, tuple(HEADS * n for n in SCR_HG), tuple(p * n for n in SCR_RT))

        def scr_cin(l):
            return scr_rt(l, HEADS)

        def scr_ln1(l):
            return Scratch(tuple(scr_rt(l, HEADS).job(0)[:1]) + tuple(scr_rt(l, HEADS).bank), (0, 1, 0))

        def scr_cout(l):
            s = scr_ln1(l)
            return Scratch((s.full, *s.bank), SCR_LN)

        def bcast(ap, n):
            return ap.unsqueeze(2).to_broadcast([ap.shape[0], ap.shape[1], n])

        def level_halves(n, src=None):
            h, end = LEVELS[n], TP // (2 * LEVELS[n]) * 2 * LEVELS[n]
            v = (Z[:, n, 0:end] if src is None else src[:, 0:end]).rearrange("p (b t) -> p b t", t=2 * h)
            return v[:, :, 0:h], v[:, :, h:2 * h]

        block = ctx.enter_context(nc.Block())

        @block.sync
        def _(sp):
            xp = x_prompt.rearrange("b t d -> (b t) d")
            first = P - N_META
            sp.dma_start(XT[0:N_META, 0, :], meta_tokens).then_inc(x_in, 16)
            sp.dma_start(XT[N_META:P, 0, :], xp[0:first, :]).then_inc(x_in, 16)
            sp.dma_start(XT[:, 1:4, :], xp[first:first + 3 * P, :].rearrange("(i p) d -> p i d", p=P)).then_inc(x_in, 16)
            sp.dma_start(XT[0:TAIL, 4, :], xp[first + 3 * P:SEQ, :]).then_inc(x_in, 16)
            sp.dma_start(XT[TAIL:R5, 4, :], x_sample.rearrange("b t d -> (b t) d")).then_inc(x_in, 16)

            def load(s, j, halves_):
                sp.wait_ge(w_lo[s], 1 + j)
                for dst, src in halves_:
                    sp.dma_start(dst, src).then_inc(stage_full[s], 16)

            def unit(s):
                return stage[:, s, :].rearrange("p (k c) -> p k c", k=KT)

            def load_sections(s, j, l, p, sections):
                load(s, j, [(unit(s)[:, :, P * n:P * n + P], w_in_v[:, ds(l * KT, KT), ds(p * P + sec * HEADS * P, P)])
                            for n, sec in enumerate(sections)])

            def load_columns(s, j, l, w, c):
                load(s, j, [(unit(s)[:, k:k + KT // 2, :], w[:, ds(l * KT + k, KT // 2), ds(c, 2 * P)])
                            for k in (0, KT // 2)])

            def load_down(s, j, l, m, part_):
                d = stage[:, s, 0:UNIT_D].rearrange("p (k c) -> p k c", k=KD)
                load(s, j, [(d[:, a:b, :], w_down_v[:, ds(l * FT + part_ * KD + a, b - a), ds(m * P, P)])
                            for a, b in ((0, 6), (6, KD))])

            sp.wait_ge(scr_full, 1)
            with sp.Fori(0, DEPTH) as l:
                j0 = l * SLOT_UNITS
                with sp.Fori(0, HEADS) as p:
                    load_sections(0, j0 + p, l, p, (1, 0))
                    load_sections(1, j0 + p, l, p, (2, 3))
                with sp.Fori(0, HEADS) as p:
                    load_sections(0, j0 + HEADS + p, l, p, (5, 4))
                    load_sections(1, j0 + HEADS + p, l, p, (6, 7))
                with sp.Fori(0, 2) as i:
                    load_columns(0, j0 + 8 + i, l, w_o_v, i * 4 * P)
                    load_columns(1, j0 + 8 + i, l, w_o_v, i * 4 * P + 2 * P)
                with sp.Fori(0, FT // 2) as i:
                    load_columns(0, j0 + 10 + i, l, w_a_v, i * 2 * P)
                    load_columns(1, j0 + 10 + i, l, w_b_v, i * 2 * P)
                with sp.Fori(0, KT) as m:
                    load_down(0, j0 + 21 + m, l, m, 0)
                    load_down(1, j0 + 21 + m, l, m, 1)

        @block.gpsimd
        def _(pool):
            for n, counter in enumerate((fin_stored, sn_stored, cso_stored)):
                pool.dma_start(unread[0:1, n:n + 1], consts[0:1, 0:1]).then_inc(counter, 16)
            nc.gpsimd.memset(PTS[:, :], 0.0).then_inc(pts_zero, 1)

            def move(ready, out, src, done):
                pool.wait_ge(params_ready, 1)
                pool.wait_ge(*ready)
                pool.dma_start(out, src).then_inc(done, 16)

            def norm_middle(n):
                pool.wait_ge(mr_ready, n + 1)
                for m in range(KT):
                    pool.wait_ge(ln_mul, n * KT + m + 1)
                    nc.gpsimd.tensor_tensor(X[:, m, :], X[:, m, :], MR[:, 0:T], ALU.subtract).then_inc(ln_sub, 1)

            def head_states(l, p, kind, s0_v, sn_v, fin_v, fin_src):
                hh = l * 2 * HEADS + kind * HEADS + p
                ot_done = l * OT_LAYER + 1 + (p if kind == 0 else HEADS + 2 * p)
                move((ot_full, ot_done), S0b, s0_v[ds(l * SEQS + p, DEC_BATCH, HEADS)].rearrange("b k v -> k b v"), s0_in)
                move((fin_ready, hh + 1), fin_v[ds((l * HEADS + p) * P, P), :], fin_src, fin_stored)
                move((sn_ready, hh + 1), sn_v[ds(l * SEQS + p, DEC_BATCH, HEADS)].rearrange("b k v -> k b v"), SNb, sn_stored)

            with pool.Fori(0, DEPTH) as l:
                norm_middle(2 * l)
                move((acc_full, 1 + l * TILES), CIN, cin_v[ds(l * 2 * DEC_BATCH, 2 * DEC_BATCH), :], cin_in)
                with pool.Fori(0, HEADS) as p:
                    head_states(l, p, 0, s0_hg_v, sn_hg_v, fin_hg_v, SC[:, (NC - 1) * P:NC * P])
                with pool.Fori(0, HEADS) as p:
                    head_states(l, p, 1, s0_rt_v, sn_rt_v, fin_rt_v, RSB[:, :])
                norm_middle(2 * l + 1)
                move((cso_ready, l + 1), cp_v[ds(l * 2, 2), :], CSO[0:2, :], cso_stored)
                move((cso_ready, l + 1), cs_v[ds(l * 2 * DEC_BATCH, 2 * DEC_BATCH), :], CSO[2:18, :], cso_stored)
            norm_middle(2 * DEPTH)
            pool.wait_ge(fin_stored, 16 + 16 * DEPTH * 2 * HEADS)
            pool.wait_ge(sn_stored, 16 + 16 * DEPTH * 2 * HEADS)
            pool.wait_ge(cso_stored, 16 + 32 * DEPTH)

        @block.tensor
        def _(pe):
            mm = nc.tensor.matmul

            def transpose_params():
                pe.wait_ge(consts_in, 16)
                pe.wait_ge(params_in, 16 * N_PARAM_DMAS)
                for b, (at_, n) in enumerate(((0, ROWS01), (P, ROWS01), (2 * P, ROWS2))):
                    last = nc.tensor.transpose(SCR[:, 0, at_:at_ + n], rows[0:n, b, :], ident[0:n, 0:n])
                last.then_inc(scr_full, 1)

            def transpose_x(scr):
                pe.wait_ge(x_in, 5 * 16)
                for i in range(TT5):
                    n = P if i < 4 else R5
                    for q in range(2):
                        bank = 1 - q
                        _, free = scr.job(bank)
                        pe.wait_ge(scr_read[bank], free)
                        for k in range(4):
                            last = nc.tensor.transpose(SCR[:, bank, k * P:k * P + n],
                                                       XT[0:n, i, (4 * q + k) * P:(4 * q + k + 1) * P], ident[0:n, 0:n])
                        last.then_inc(scr_full, 1)

            def norm_stats(n, ot, scr):
                pe.wait_ge(sums_ready, n + 1)
                pe.wait_ge(ot_read, 1 + ot)
                for h in range(2):
                    last = mm(OT[:, h, 0:HALF], ones_ln, S1[:, h * HALF:(h + 1) * HALF], start=True, stop=True)
                last.then_inc(ot_full, 1)
                for h in range(2):
                    _, free = scr.job(h)
                    pe.wait_ge(scr_read[h], free)
                    mm(SCR[:, h, 0:HALF], ones_ln, S2[:, h * HALF:(h + 1) * HALF], start=True, stop=True).then_inc(scr_full, 1)

            def products(acc, s, width, col, wk, xh, xl, xk, n, first, final, wait_k=None, between=()):
                for k in range(n):
                    for step in between[k] if between else ():
                        step()
                    if wait_k is not None:
                        pe.wait_ge(wait_k[0], wait_k[1] + k)
                    for w, x in ((WH, xh), (WH, xl), (WL, xh)):
                        lhs = w[:, s, wk(k) * width + col:wk(k) * width + col + P]
                        begin = first and k == 0 and w is WH and x is xh
                        end = final and k == n - 1 and w is WL
                        for h in range(2):
                            last = mm(ACC[:, acc, h, 0:HALF], lhs, x[:, xk + k, h * HALF:(h + 1) * HALF], start=begin, stop=end)
                return last

            def gemm_tile(l, j, s, c, half_tile, xh, xl, wait_k=None, between=()):
                if c == 0:
                    pe.wait_ge(w_lo[s], 1 + j + 1)
                pe.wait_ge(acc_read[c], 1 + l * ACC_TILES + half_tile)
                products(c, s, 2 * P, c * P, lambda k: k, xh, xl, 0, KT, True, True, wait_k, between).then_inc(acc_full, 1)

            def job(scr, bank):
                _, free = scr.job(bank)
                pe.wait_ge(scr_read[bank], free)

            def hg_steps(l, p, scr):
                hh = l * 2 * HEADS + p

                def level(n, chunks, bank, o):
                    keys, queries = (Z[:, n, :], Z[:, n, :]) if n < len(LEVELS) else (DK[:, :], DQ[:, :])
                    for t, w in chunks:
                        last = mm(SCR[0:w, bank, o:o + w], keys[:, t:t + w], queries[:, t:t + w], start=True, stop=True)
                        o += w
                    return last

                def scores(n):
                    bank, first, second = HG_JOBS[n]
                    if n == 0:
                        pe.wait_ge(ew_ready, hh + 1)
                    job(scr, bank)
                    last = level(*first, bank, 0)
                    if second is not None and second[0] == 0:
                        for c in range(NC - 1):
                            last = mm(SCR[0:C // 2, bank, REST_HG + c * C // 2:REST_HG + (c + 1) * C // 2],
                                      Z[:, 0, C * c:C * c + C // 2], Z[:, 0, C * c + C // 2:C * c + C], start=True, stop=True)
                    elif second is not None:
                        last = level(*second, bank, REST_HG)
                    if n == 1:
                        last = mm(SCR[0:TS, bank, SPLIT:SPLIT + TS], KVS[:, :], QD[:, TP:T], start=True, stop=True)
                    last.then_inc(scr_full, 1)

                def transposes(n):
                    if n == 0:
                        pe.wait_ge(v_ready, hh + 1)
                    bank, sources = n % 2, (KE, V)
                    job(scr, bank)
                    if n < 2:
                        for c in range(4):
                            w = P if c == 0 else C
                            last = nc.tensor.transpose(SCR[0:w, bank, c * P:(c + 1) * P], sources[n][:, C * c:C * c + w], ident)
                    elif n == 2:
                        for i, (c, src) in enumerate((c, src) for c in (4, 5) for src in sources):
                            w = P if c == 4 else CHUNKS[5][1]
                            last = nc.tensor.transpose(SCR[0:w, bank, i * P:(i + 1) * P], src[:, C * c:C * c + w], ident)
                    else:
                        for i, src in enumerate(sources):
                            last = nc.tensor.transpose(SCR[0:TS, bank, i * P:(i + 1) * P], src[:, TP:T], ident)
                    last.then_inc(scr_full, 1)

                def state_steps(n):
                    if n == 0:
                        pe.wait_ge(tok_ready, hh + 1)
                    job(scr, n)
                    for c in range(4 * n, min(4 * n + 4, NC)):
                        w = CHUNKS[c][1]
                        last = mm(SCR[:, n, (c - 4 * n) * P:(c - 4 * n + 1) * P], KTOK[0:w, c * P:(c + 1) * P],
                                  VTOK[0:w, c * P:(c + 1) * P], start=True, stop=True)
                    last.then_inc(scr_full, 1)

                def output(c):
                    if c == 0:
                        pe.wait_ge(pts_ready, hh + 1)
                        pe.wait_ge(states_ready, l * HEADS + p + 1)
                        pe.wait_ge(s0_in, 16 * (hh + 1))
                        pe.wait_ge(ot_read, 1 + l * OT_LAYER + 1 + p)
                    t, w = CHUNKS[c]
                    o = OT[:, c // 3, (c % 3) * C:(c % 3) * C + w]
                    if c:
                        mm(o, SC[:, (c - 1) * P:c * P], QD[:, t:t + w], start=True, stop=False)
                    mm(o, VTOK[0:w, c * P:(c + 1) * P], PTS[0:w, t:t + w], start=(c == 0), stop=True)
                    if c == NC - 1:
                        sample_output(QD).then_inc(ot_full, 1)

                def mean_square(bank):
                    if bank == 0:
                        pe.wait_ge(hsq_ready, hh + 1)
                    a, b = ((0, SPLIT), (SPLIT, T))[bank]
                    job(scr, bank)
                    mm(SCR[:, bank, 0:b - a], ones_h, SQ[:, a:b], start=True, stop=True).then_inc(scr_full, 1)

                steps = [(HG_SLOTS[0][n], lambda n=n: scores(n)) for n in range(len(HG_JOBS))]
                steps += [(HG_SLOTS[1][n], lambda n=n: transposes(n)) for n in range(4)]
                steps += [(HG_SLOTS[2][n], lambda n=n: state_steps(n)) for n in range(2)]
                steps += [(HG_SLOTS[3][n], lambda n=n: sample_steps(hh, scr, n, n)) for n in range(2)]
                steps += [(HG_SLOTS[4][c], lambda c=c: output(c)) for c in range(NC)]
                steps += [(HG_SLOTS[5][n], lambda n=n: mean_square(n)) for n in range(2)]
                return steps

            def sample_steps(hh, scr, n, bank):
                if n == 0:
                    pe.wait_ge(vx_ready, hh + 1)
                job(scr, bank)
                mm(SCR[:, bank, :], KVTS[:, 0, :], VX[:, 4 * n:4 * n + 4, :].rearrange("p b v -> p (b v)"),
                   start=True, stop=True).then_inc(scr_full, 1)

            def sample_output(qs):
                cols_ = OT[:, 1, TP - SPLIT:REST]
                mm(cols_, KVTS[:, 1, :], PTSS[:, :], start=True, stop=False, skip_group_check=True)
                for b in range(DEC_BATCH):
                    last = mm(OT[:, 1, TP - SPLIT + DEC_SEQ * b:TP - SPLIT + DEC_SEQ * (b + 1)], S0b[:, b, :],
                              qs[:, TP + DEC_SEQ * b:TP + DEC_SEQ * (b + 1)], start=False, stop=(b == DEC_BATCH - 1),
                              skip_group_check=True)
                return last

            def rt_steps(l, p, scr):
                hh = l * 2 * HEADS + HEADS + p

                def transposes(bank, src):
                    if src is KE:
                        pe.wait_ge(ew_ready, hh + 1)
                        pe.wait_ge(v_ready, hh + 1)
                    job(scr, bank)
                    for i in range(4):
                        last = nc.tensor.transpose(SCR[:, bank, i * P:(i + 1) * P], src[:, i * P:(i + 1) * P], ident)
                    last.then_inc(scr_full, 1)

                def rest_transposes():
                    job(scr, 0)
                    for n, src in enumerate((KE, V)):
                        nc.tensor.transpose(SCR[0:TAIL, 0, n * P:(n + 1) * P], src[:, 4 * P:TP], ident)
                        last = nc.tensor.transpose(SCR[0:TS, 0, (2 + n) * P:(3 + n) * P], src[:, TP:T], ident)
                    last.then_inc(scr_full, 1)

                def scores(n):
                    bank = 1 - n % 2
                    job(scr, bank)
                    for i, t0, t1, o in RT_JOBS[n]:
                        rows_ = P if i < 4 else TAIL
                        last = mm(SCR[0:rows_, bank, o:o + t1 - t0], KE[:, i * P:i * P + rows_], QD[:, t0:t1], start=True, stop=True)
                    if n == len(RT_JOBS) - 1:
                        last = mm(SCR[0:TS, bank, TAIL:TAIL + TS], KE[:, TP:T], QD[:, TP:T], start=True, stop=True)
                    last.then_inc(scr_full, 1)

                def final_state():
                    pe.wait_ge(tok_ready, hh + 1)
                    job(scr, 0)
                    for i in range(TT5):
                        r = P if i < 4 else TAIL
                        last = mm(SCR[:, 0, 0:P], KTOK[0:r, i * P:(i + 1) * P], VTOK[0:r, i * P:(i + 1) * P], start=(i == 0), stop=(i == 4))
                    last.then_inc(scr_full, 1)

                def output(h):
                    if h == 0:
                        pe.wait_ge(pts_ready, hh + 1)
                        pe.wait_ge(s0_in, 16 * (hh + 1))
                        pe.wait_ge(ot_read, 1 + l * OT_LAYER + 1 + HEADS + 2 * p)
                    a, b = ((0, SPLIT), (SPLIT, TP))[h]
                    tiles = [i for i in range(TT5) if i * P < b]
                    for i in tiles:
                        r, t0 = (P if i < 4 else TAIL), max(a, i * P)
                        mm(OT[:, h, t0 - a:b - a], VTOK[0:r, i * P:(i + 1) * P],
                           PTR[0:r, RT_OFF[i] + t0 - i * P:RT_OFF[i] + b - i * P], start=(i == 0), stop=(i == tiles[-1]),
                           skip_group_check=True)
                    if h == 1:
                        sample_output(QS).then_inc(ot_full, 1)

                def centre(bank):
                    if bank == 1:
                        pe.wait_ge(o_copied, l * HEADS + p + 1)
                    a, b = ((SPLIT, T), (0, SPLIT))[bank]
                    job(scr, bank)
                    mm(SCR[:, bank, 0:b - a], center, SQ[:, a:b], start=True, stop=True).then_inc(scr_full, 1)

                def variance():
                    pe.wait_ge(hsq_ready, hh + 1)
                    pe.wait_ge(ot_read, 1 + l * OT_LAYER + 2 + HEADS + 2 * p)
                    mm(OT[:, 0, 0:SPLIT], ones_h, SQ[:, 0:SPLIT], start=True, stop=True)
                    mm(OT[:, 1, 0:REST], ones_h, SQ[:, SPLIT:T], start=True, stop=True).then_inc(ot_full, 1)

                steps = [(RT_SLOTS[0][0], lambda: transposes(0, KE)), (RT_SLOTS[0][1], lambda: transposes(1, V)),
                         (RT_SLOTS[0][2], rest_transposes)]
                steps += [(RT_SLOTS[1][n], lambda n=n: scores(n)) for n in range(len(RT_JOBS))]
                steps += [(RT_SLOTS[2][0], final_state)]
                steps += [(RT_SLOTS[3][n], lambda n=n: sample_steps(hh, scr, n, 1 - n)) for n in range(2)]
                steps += [(RT_SLOTS[4][h], lambda h=h: output(h)) for h in range(2)]
                steps += [(RT_SLOTS[5][n], lambda n=n: centre(1 - n)) for n in range(2)]
                steps += [(RT_SLOTS[6][0], variance)]
                return steps

            def group(l, g, steps=()):
                j = l * SLOT_UNITS + g
                for n in range(4):
                    between = [[f for slot, f in steps if slot == KT * n + k] for k in range(KT)]
                    gemm_tile(l, j, n // 2, n % 2, 2 * g + n // 2, XH, XL,
                              (x_ready, 2 * l * KT + 1) if n == 0 else None, between)

            transpose_params()
            transpose_x(Scratch((1, 1, 0)))
            with pe.Fori(0, DEPTH) as l:
                norm_stats(2 * l, l * OT_LAYER, Scratch(base(l)))
                group(l, 0)
                with pe.Fori(0, HEADS - 1) as p:
                    group(l, p + 1, hg_steps(l, p, scr_hg(l, p)))
                group(l, HEADS, hg_steps(l, HEADS - 1, scr_hg(l, HEADS - 1)))
                with pe.Fori(0, HEADS - 1) as p:
                    group(l, p + HEADS + 1, rt_steps(l, p, scr_rt(l, p)))
                for _, step in rt_steps(l, HEADS - 1, scr_rt(l, HEADS - 1)):
                    step()

                pe.wait_ge(cin_in, 16 * (l + 1))
                _, free = scr_cin(l).job(0)
                pe.wait_ge(scr_read[0], free)
                for f in range(FT):
                    last = mm(SCR[:, 0, f * 16:(f + 1) * 16], CIN[:, f * P:(f + 1) * P], ident[0:16, 0:16], start=True, stop=True)
                last.then_inc(scr_full, 1)

                with pe.Fori(0, 2) as i:
                    for n in range(4):
                        gemm_tile(l, l * SLOT_UNITS + 8 + i, n // 2, n % 2, O_TILE // 2 + 2 * i + n // 2, OH, OL,
                                  (ol_ready, l * 2 * HEADS + 1) if n == 0 else None)
                norm_stats(2 * l + 1, l * OT_LAYER + OT_LAYER - 1, scr_ln1(l))

                with pe.Fori(0, FT // 2) as i:
                    for n in range(4):
                        gemm_tile(l, l * SLOT_UNITS + 10 + i, n // 2, n % 2, F_TILE // 2 + 2 * i + n // 2, XH, XL,
                                  (x_ready, (2 * l + 1) * KT + 1) if n == 0 else None)

                pe.wait_ge(conv_ready, (l + 1) * FT)
                scr = scr_cout(l)
                for q in range(6):
                    bank = 1 - q % 2
                    _, free = scr.job(bank)
                    pe.wait_ge(scr_read[bank], free)
                    for f in range(4 * q, min(4 * q + 4, FT)):
                        last = nc.tensor.transpose(SCR[0:18, bank, (f - 4 * q) * P:(f - 4 * q + 1) * P], CSB[:, f, :], ident)
                    last.then_inc(scr_full, 1)

                with pe.Fori(0, KT // 2) as q:
                    for c in range(2):
                        j = l * SLOT_UNITS + 21 + 2 * q + c
                        pe.wait_ge(acc_read[c], 1 + l * ACC_TILES + D_TILE // 2 + q)
                        for s in range(2):
                            pe.wait_ge(w_lo[s], 1 + j + 1)
                            products(c, s, P, 0, lambda k: k, HH, HL, s * KD, KD, s == 0, s == 1,
                                     (h_ready, 1 + l * FT + s * KD + 1) if c == 0 else None
                                     ).then_inc(acc_full if s == 1 else half_used, 1)
            norm_stats(2 * DEPTH, DEPTH * OT_LAYER, Scratch(base(DEPTH)))
            scr = Scratch(base(DEPTH), SCR_LN)
            pe.wait_ge(ln_out, (2 * DEPTH + 1) * KT)
            for i in range(TT5):
                n = P if i < 4 else R5
                for q in range(2):
                    _, free = scr.job(q)
                    pe.wait_ge(scr_read[q], free)
                    for k in range(4):
                        last = nc.tensor.transpose(SCR[0:n, q, k * P:(k + 1) * P], X[:, 4 * q + k, i * P:i * P + n], ident)
                    last.then_inc(scr_full, 1)

        @block.scalar
        def _(act):
            f = nc.scalar.activation

            act.dma_start(tab[:, :], consts).then_inc(consts_in, 16)
            loads = []
            for l in range(DEPTH):
                loads.append((rows[0:CONV_W * FT, l, :], conv_w[l].rearrange("j (f p) -> (j f) p", p=P)))
                loads.append((rows[CONV_W * FT:ROWS01, l, :], conv_b[l].rearrange("(f p) -> f p", p=P)))
            norms = [(emb_ln_g, emb_ln_b)] + [pr for l in range(DEPTH) for pr in ((ln1_g[l], ln1_b[l]), (ln2_g[l], ln2_b[l]))]
            for n, pr in enumerate(norms):
                for h, src in enumerate(pr):
                    loads.append((rows[16 * n + 8 * h:16 * n + 8 * h + 8, 2, :], src.rearrange("(k p) -> k p", p=P)))
            for at_, src in ((ROW_HG, hg_norm_g), (ROW_RG, rt_gn_g), (ROW_RB, rt_gn_b), (ROW_LB, lb_logits)):
                loads.append((rows[at_:at_ + 8, 2, :], src.rearrange("l (h p) -> (l h) p", p=P)))
            assert len(loads) == N_PARAM_DMAS
            for dst, src in loads:
                act.dma_start(dst, src).then_inc(params_in, 16)

            def split_hi(s, j, used, width=UNIT):
                act.wait_ge(*used)
                act.wait_ge(stage_full[s], 32 * (j + 1))
                f(WH[:, s, 0:width], stage[:, s, 0:width], ACT.Copy, scale=W_SCALE).then_inc(w_hi[s], 1)

            def squares(n, m, y):
                act.wait_ge(y_ready, y)
                act.wait_ge(sq_used, 1 + n * KT + m)
                src = X[:, m, :] if isinstance(m, int) else X[:, ds(m, 1), :].rearrange("p o t -> p (o t)")
                f(SQT[:, 0:T], src, ACT.Square).then_inc(sq_ready, 1)

            def norm_apply(n, ot, last=False):
                act.wait_ge(ot_full, ot + 1)
                src = OT[:, :, 0:HALF]
                f(halves(MU[:, 0:T]), src, ACT.Copy)
                f(halves(MSQ[:, 0:T]), src, ACT.Square).then_inc(ot_read, 1)
                act.drain().then_inc(mu_ready, 1)
                act.wait_ge(var_ready, n + 1)
                f(RSTD[:, 0:T], VAR[:, 0:T], ACT.Ln, bias=tab[:, ds(eps_at + n, 1)])
                act.drain()
                f(RSTD[:, 0:T], RSTD[:, 0:T], ACT.Exp, scale=-0.5).then_inc(rstd_ready, 1)
                for m in range(KT):
                    act.wait_ge(ln_sub, n * KT + m + 1)
                    g, b = (par[:, ds(n * 16 + 2 * P + m + 8 * h, 1)] for h in range(2))
                    if not last:
                        f(XH[:, m, :], X[:, m, :], ACT.Identity, scale=g, bias=b)
                    f(X[:, m, :], X[:, m, :], ACT.Identity, scale=g, bias=b).then_inc(ln_out, 1)

            def sigmoid(buf, width, done):
                f(buf[:, 0:width], buf[:, 0:width], ACT.Exp, scale=-1.0)
                act.drain()
                f(buf[:, 0:width], buf[:, 0:width], ACT.Ln, bias=1.0)
                act.drain()
                f(buf[:, 0:width], buf[:, 0:width], ACT.Exp, scale=-1.0).then_inc(done, 1)

            def read_acc(buf, c, tile, done):
                act.wait_ge(acc_full, 1 + tile + 1)
                f(halves(buf[:, 0:T]), ACC[:, c, :, 0:HALF], ACT.Copy, scale=INV_W).then_inc(acc_read[c], 1)
                if done is not None:
                    act.drain().then_inc(done, 1)

            def hg_gate(l, p):
                n = l * HEADS + p
                act.wait_ge(f_ready, n + 1)
                f(T1[:, 0:T], Fb[:, 0:T], ACT.Exp, scale=-1.0)
                act.drain()
                f(T2[:, 0:T], T1[:, 0:T], ACT.Ln, bias=1.0)
                f(T3[:, 0:T], T1[:, 0:T], ACT.Ln, bias=1.0, scale=LBT[:, ds(n, 1)]).then_inc(lnf_parts, 1)
                act.wait_ge(f2_ready, n + 1)
                f(Fb[:, 0:T], Fb[:, 0:T], ACT.Exp, scale=-1.0).then_inc(k_raw, 1)

            def hg_query(l, p, tile):
                n = l * HEADS + p
                read_acc(Q, 1, tile, None)
                act.wait_ge(q_clamped, n + 1)
                sigmoid(T1, T, q_sig)
                act.wait_ge(diff_ready, n + 1)
                f(T3[:, 0:T], T3[:, 0:T], ACT.Exp)
                f(EN[:, :], B[:, TP:T], ACT.Exp, scale=-1.0)
                f(E[:, 0:T], B[:, 0:T], ACT.Exp)
                for n in range(len(LEVELS)):
                    for z, sign in zip(level_halves(n), (-1.0, 1.0)):
                        f(z, z, ACT.Exp, scale=sign)
                f(DQ[:, :], DK[:, :], ACT.Exp)
                f(DK[:, :], DK[:, :], ACT.Exp, scale=-1.0).then_inc(exps_ready, 1)

            def out_gate(hh):
                act.wait_ge(g_clamped, hh + 1)
                sigmoid(R, T, g_sig)

            def hg_a(l, p, scr):
                for n, dst in enumerate((KTOK, VTOK)):
                    full, _ = scr.job(n)
                    act.wait_ge(scr_full, full)
                    f(dst[0:C, 0:4 * P], SCR[0:C, n, :], ACT.Copy).then_inc(scr_read[n], 1)
                full, _ = scr.job(0)
                act.wait_ge(scr_full, full)
                for c in (4, 5):
                    w = CHUNKS[c][1]
                    last = f(KVTOK[0:w, :, c * P:(c + 1) * P],
                             SCR[0:w, 0, 2 * (c - 4) * P:2 * (c - 3) * P].rearrange("p (n v) -> p n v", n=2), ACT.Copy)
                last.then_inc(scr_read[0], 1)
                full, _ = scr.job(1)
                act.wait_ge(scr_full, full)
                f(KVTS[:, :, :], SCR[0:TS, 1, 0:2 * P].rearrange("p (n v) -> p n v", n=2), ACT.Copy).then_inc(scr_read[1], 1)
                act.drain().then_inc(tok_ready, 1)

            def hg_c(l, p):
                act.wait_ge(ot_full, l * OT_LAYER + 2 + p)
                f(SQ[:, 0:SPLIT], OT[:, 0, 0:SPLIT], ACT.Square)
                f(SQ[:, SPLIT:T], OT[:, 1, 0:REST], ACT.Square).then_inc(hsq_ready, 1)

            def high_output(row, hh):
                act.wait_ge(to_ready, hh + 1)
                f(OH[:, ds(row, 1), :].rearrange("p o t -> p (o t)"), TO[:, :], ACT.Copy).then_inc(oh_ready, 1)

            eps_h = tab[:, eps_at + 5:eps_at + 6]

            def hg_d(l, p, scr):
                hh = l * 2 * HEADS + p
                act.wait_ge(g_ready, hh + 1)
                for bank, (a, b) in enumerate(((0, SPLIT), (SPLIT, T))):
                    full, _ = scr.job(bank)
                    act.wait_ge(scr_full, full)
                    f(R[:, a:b], SCR[:, bank, 0:b - a], ACT.Ln, bias=eps_h).then_inc(scr_read[bank], 1)
                act.drain()
                f(R[:, :], R[:, :], ACT.Exp, scale=-0.5).then_inc(hr_ready, 1)
                high_output(p, hh)

            def hg_stages(l, p):
                s = scr_hg(l, p)
                for b, _, _ in HG_JOBS:
                    s.job(b)

                def d():
                    for b in (0, 1, 0, 1):
                        s.job(b)
                    hg_d(l, p, s)
                return (lambda: hg_a(l, p, s)), None, (lambda: hg_c(l, p)), d

            def rt_a(l, p, scr):
                k_at = cols["k_dec"][0]
                full, _ = scr.job(0)
                act.wait_ge(scr_full, full)
                for i in range(4):
                    last = f(KTOK[:, i * P:(i + 1) * P], SCR[:, 0, i * P:(i + 1) * P], ACT.Copy, scale=tab[:, ds(k_at + i * HEADS + p, 1)])
                last.then_inc(scr_read[0], 1)
                full, _ = scr.job(1)
                act.wait_ge(scr_full, full)
                f(VTOK[:, 0:4 * P], SCR[:, 1, :], ACT.Copy).then_inc(scr_read[1], 1)
                full, _ = scr.job(0)
                act.wait_ge(scr_full, full)
                f(KTOK[0:TAIL, 4 * P:5 * P], SCR[0:TAIL, 0, 0:P], ACT.Copy, scale=tab[0:TAIL, ds(k_at + 4 * HEADS + p, 1)])
                f(VTOK[0:TAIL, 4 * P:5 * P], SCR[0:TAIL, 0, P:2 * P], ACT.Copy)
                f(KVTS[:, 0, :], SCR[0:TS, 0, 2 * P:3 * P], ACT.Copy, scale=tab[0:TS, ds(cols["k_dec_s"][0] + p, 1)])
                f(KVTS[:, 1, :], SCR[0:TS, 0, 3 * P:4 * P], ACT.Copy).then_inc(scr_read[0], 1)
                act.drain().then_inc(tok_ready, 1)
                for bank in (1, 0, 1, 0, 1):
                    scr.job(bank)

            def rt_b(l, p, scr):
                hh = l * 2 * HEADS + HEADS + p
                full, _ = scr.job(0)
                act.wait_ge(fin_stored, 16 + 16 * hh)
                act.wait_ge(scr_full, full)
                f(RSB[:, :], SCR[:, 0, 0:P], ACT.Copy).then_inc(scr_read[0], 1)
                act.drain().then_inc(fin_ready, 1)
                act.wait_ge(ot_full, l * OT_LAYER + 2 + HEADS + 2 * p)
                f(SQ[:, 0:SPLIT], OT[:, 0, 0:SPLIT], ACT.Copy)
                f(SQ[:, SPLIT:T], OT[:, 1, 0:REST], ACT.Copy).then_inc(ot_read, 1)
                act.drain().then_inc(o_copied, 1)

            def rt_c(l, p):
                act.wait_ge(oc_ready, l * HEADS + p + 1)
                f(SQ[:, :], TO[:, :], ACT.Square).then_inc(hsq_ready, 1)

            def rt_d(l, p):
                hh = l * 2 * HEADS + HEADS + p
                act.wait_ge(g_ready, hh + 1)
                act.wait_ge(ot_full, l * OT_LAYER + 3 + HEADS + 2 * p)
                f(R[:, 0:SPLIT], OT[:, 0, 0:SPLIT], ACT.Ln, bias=eps_h)
                f(R[:, SPLIT:T], OT[:, 1, 0:REST], ACT.Ln, bias=eps_h).then_inc(ot_read, 1)
                act.drain()
                f(R[:, :], R[:, :], ACT.Exp, scale=-0.5).then_inc(hr_ready, 1)
                high_output(HEADS + p, hh)

            def rt_stages(l, p):
                s = scr_rt(l, p)
                return (lambda: rt_a(l, p, s)), (lambda: rt_b(l, p, s)), (lambda: rt_c(l, p)), (lambda: rt_d(l, p))

            def group(l, g, head, kind, stages=(None,) * 4):
                a, b, c, d = stages
                j, tile = l * SLOT_UNITS + g, l * TILES + 4 * g
                hh = l * 2 * HEADS + kind * HEADS + head
                split_hi(1, j, (acc_full, 1 + tile))
                if kind == 0:
                    hg_gate(l, head)
                if a is not None:
                    a()
                if b is not None:
                    b()
                if kind == 0:
                    hg_query(l, head, tile + 1)
                split_hi(0, j + 1, (acc_full, 1 + tile + 2))
                if stages[3] is not None:
                    out_gate(hh - 1)
                if c is not None:
                    c()
                read_acc(V, 0, tile + 2, v_ready)
                if d is not None:
                    d()
                read_acc(G, 1, tile + 3, g_raw)

            act.wait_ge(scr_full, 1)
            for b, n in ((0, ROWS01), (1, ROWS01), (2, ROWS2)):
                last = f(par[:, b * P:b * P + n], SCR[:, 0, b * P:b * P + n], ACT.Copy)
            last.then_inc(scr_read[0], 1)
            act.drain().then_inc(params_ready, 1)
            nc.scalar.preload_act_table_set("natural_log_exp_and_others")
            act.wait_ge(lb_max, 1)
            f(LE[:, 1:3, :], LE[:, 1:3, :], ACT.Exp).then_inc(lb_exp, 1)
            with act.Fori(0, KT) as m:
                squares(0, m, 1)

            with act.Fori(0, DEPTH) as l:
                nc.scalar.preload_act_table_set("natural_log_exp_and_others")
                split_hi(0, l * SLOT_UNITS, (acc_full, 1 + l * TILES))
                norm_apply(2 * l, l * OT_LAYER)
                act.wait_ge(cso_stored, 16 + 32 * l)
                group(l, 0, 0, 0)
                with act.Fori(0, HEADS - 1) as p:
                    group(l, p + 1, p + 1, 0, hg_stages(l, p))
                group(l, HEADS, 0, 1, hg_stages(l, HEADS - 1))
                with act.Fori(0, HEADS - 1) as p:
                    group(l, p + HEADS + 1, p + 1, 1, rt_stages(l, p))
                out_gate((l + 1) * 2 * HEADS - 1)
                for stage_ in rt_stages(l, HEADS - 1):
                    stage_()

                full, _ = scr_cin(l).job(0)
                act.wait_ge(scr_full, full)
                f(CST[:, :, :], SCR[:, 0, 0:FT * 16].rearrange("p (f b) -> p f b", f=FT), ACT.Copy).then_inc(scr_read[0], 1)
                act.drain().then_inc(cst_ready, 1)

                with act.Fori(0, 2) as i:
                    for n in range(4):
                        if n % 2 == 0:
                            split_hi(1 - n // 2, l * SLOT_UNITS + 8 + i + n // 2, (acc_full, 1 + l * TILES + O_TILE + 4 * i + n))
                        squares(2 * l + 1, 4 * i + n, 2 + 2 * l * KT + 4 * i + n)
                nc.scalar.preload_act_table_set("natural_log_exp_and_others")
                norm_apply(2 * l + 1, l * OT_LAYER + OT_LAYER - 1)

                nc.scalar.preload_act_table(ACT.Gelu_apprx_tanh)
                act.wait_ge(sn_stored, 16 + (l + 1) * 2 * HEADS * 16)
                act.wait_ge(fin_stored, 16 + (l + 1) * 2 * HEADS * 16)
                with act.Fori(0, FT // 2) as i:
                    n0 = l * FT + 2 * i
                    split_hi(1, l * SLOT_UNITS + 10 + i, (acc_full, 1 + l * TILES + F_TILE + 4 * i))
                    for c in range(2):
                        act.wait_ge(h_ready, 1 + n0)
                        act.wait_ge(acc_full, 1 + l * TILES + F_TILE + 4 * i + c + 1)
                        f(halves(AX[c][:, 2:2 + T]), ACC[:, c, :, 0:HALF], ACT.Copy, scale=INV_W)
                        f(halves(CX[c][:, 0:T]), ACC[:, c, :, 0:HALF], ACT.Identity, scale=CW2[:, ds(n0 + c, 1)],
                          bias=par[:, ds(l * P + CONV_W * FT + 2 * i + c, 1)]).then_inc(acc_read[c], 1)
                        act.drain().then_inc(a_ready, 1)
                    split_hi(0, l * SLOT_UNITS + 11 + i, (acc_full, 1 + l * TILES + F_TILE + 4 * i + 2))
                    for c in range(2):
                        act.wait_ge(conv_ready, n0 + c + 1)
                        f(CX[c][:, 0:T], CX[c][:, 0:T], ACT.Gelu_apprx_tanh).then_inc(gelu_ready, 1)
                    for c in range(2):
                        act.wait_ge(ht_ready, n0 + c + 1)
                        f(HH[:, ds(2 * i + c, 1), :].rearrange("p o t -> p (o t)"), CX[c][:, 0:T], ACT.Copy).then_inc(hh_ready, 1)

                scr = scr_cout(l)
                for q in range(6):
                    bank = 1 - q % 2
                    full, _ = scr.job(bank)
                    w = (min(4 * q + 4, FT) - 4 * q) * P
                    act.wait_ge(scr_full, full)
                    f(CSO[:, 4 * q * P:4 * q * P + w], SCR[0:18, bank, 0:w], ACT.Copy).then_inc(scr_read[bank], 1)
                act.drain().then_inc(cso_ready, 1)

                def down(q, last):
                    for c in range(2):
                        split_hi(1, l * SLOT_UNITS + 21 + 2 * q + c, (acc_full, 1 + l * TILES + D_TILE + 2 * q + c), UNIT_D)
                        if not (last and c == 1):
                            split_hi(0, l * SLOT_UNITS + 22 + 2 * q + c, (half_used, l * KT + 2 * q + c + 1), UNIT_D)
                        squares(2 * l + 2, 2 * q + c, 2 + (2 * l + 1) * KT + 2 * q + c)
                with act.Fori(0, KT // 2 - 1) as q:
                    down(q, False)
                down(KT // 2 - 1, True)
            nc.scalar.preload_act_table_set("natural_log_exp_and_others")
            norm_apply(2 * DEPTH, DEPTH * OT_LAYER, last=True)
            scr = Scratch(base(DEPTH), SCR_LN)
            for i in range(TT5):
                n = P if i < 4 else R5
                for q in range(2):
                    full, _ = scr.job(q)
                    act.wait_ge(scr_full, full)
                    last = f(XT[0:n, i, q * 512:(q + 1) * 512], SCR[0:n, q, :], ACT.Copy)
                    last.then_inc(scr_read[q], 1)
                act.drain().then_inc(out_ready, 1)
                act.wait_ge(out_ready, i + 1)
                yp = y_prompt.rearrange("b t d -> (b t) d")
                if i == 0:
                    act.dma_start(yp[0:P - N_META, :], XT[N_META:P, 0, :]).then_inc(out_stored, 16)
                elif i < 4:
                    act.dma_start(yp[i * P - N_META:(i + 1) * P - N_META, :], XT[:, i, :]).then_inc(out_stored, 16)
                else:
                    act.dma_start(yp[4 * P - N_META:SEQ, :], XT[0:TAIL, 4, :]).then_inc(out_stored, 16)
                    act.dma_start(y_sample.rearrange("b t d -> (b t) d"), XT[TAIL:R5, 4, :]).then_inc(out_stored, 16)
            act.wait_ge(out_stored, 16 * 6)

        @block.vector
        def _(dve):
            tt, ts, stt = nc.vector.tensor_tensor, nc.vector.tensor_scalar, nc.vector.scalar_tensor_tensor

            def split_lo(s, j, width=UNIT):
                dve.wait_ge(w_hi[s], j + 1)
                stt(out=WL[:, s, 0:width], in0=stage[:, s, 0:width], scalar=W_SCALE, in1=WH[:, s, 0:width],
                    op0=ALU.mult, op1=ALU.subtract).then_inc(w_lo[s], 1)

            def row(m):
                return X[:, m, :] if isinstance(m, int) else X[:, ds(m, 1), :].rearrange("p o t -> p (o t)")

            def zero_sums():
                nc.vector.memset(S1[:, 0:T], 0.0)
                nc.vector.memset(S2[:, 0:T], 0.0)
                dve.drain()

            def add_sums(n, m):
                tt(S1[:, 0:T], S1[:, 0:T], row(m), ALU.add)
                dve.wait_ge(sq_ready, n * KT + m + 1)
                tt(S2[:, 0:T], S2[:, 0:T], SQT[:, 0:T], ALU.add).then_inc(sq_used, 1)
                dve.drain()

            def residual(l, n, m, c, tile):
                dve.wait_ge(acc_full, 1 + l * TILES + tile + 1)
                stt(out=halves(row(m)), in0=ACC[:, c, :, 0:HALF], scalar=INV_W / ALPHA, in1=halves(row(m)),
                    op0=ALU.mult, op1=ALU.add).then_inc(acc_read[c], 1)
                dve.drain().then_inc(y_ready, 1)
                add_sums(n, m)

            def norm_apply(n, scr, last=False):
                dve.drain().then_inc(sums_ready, 1)
                dve.wait_ge(mu_ready, n + 1)
                for h in range(2):
                    full, _ = scr.job(h)
                    dve.wait_ge(scr_full, full)
                    tt(VAR[:, h * HALF:(h + 1) * HALF], SCR[:, h, 0:HALF], MSQ[:, h * HALF:(h + 1) * HALF],
                       ALU.subtract).then_inc(scr_read[h], 1)
                dve.drain()
                ts(VAR[:, 0:T], VAR[:, 0:T], 0.0, None, ALU.max).then_inc(var_ready, 1)
                dve.wait_ge(rstd_ready, n + 1)
                tt(MR[:, 0:T], MU[:, 0:T], RSTD[:, 0:T], ALU.mult).then_inc(mr_ready, 1)
                for m in range(KT + 2):
                    if m < KT:
                        tt(X[:, m, :], X[:, m, :], RSTD[:, 0:T], ALU.mult).then_inc(ln_mul, 1)
                    if m >= 2 and not last:
                        dve.wait_ge(ln_out, n * KT + m - 1)
                        tt(XL[:, m - 2, :], X[:, m - 2, :], XH[:, m - 2, :], ALU.subtract).then_inc(x_ready, 1)

            def hg_gate(l, p, tile):
                n = l * HEADS + p
                dve.wait_ge(acc_full, 1 + tile + 1)
                ts(halves(Fb[:, 0:T]), ACC[:, 0, :, 0:HALF], INV_W, CLAMP, ALU.mult, ALU.max).then_inc(acc_read[0], 1)
                dve.drain().then_inc(f_ready, 1)
                dve.wait_ge(lnf_parts, n + 1)
                tt(Fb[:, 0:T], Fb[:, 0:T], T2[:, 0:T], ALU.add).then_inc(f2_ready, 1)
                tt(T3[:, 0:T], T3[:, 0:T], T2[:, 0:T], ALU.subtract)
                dve.drain()
                ts(T3[:, 0:T], T3[:, 0:T], LOG_F_MIN, None, ALU.max)
                dve.drain()
                nc.vector.tensor_tensor_scan(B[:, 0:T], keep, T3[:, 0:T], 0.0, ALU.mult, ALU.add)
                dve.wait_ge(k_raw, n + 1)
                ts(Fb[:, 0:T], Fb[:, 0:T], OMLB[:, ds(n, 1)], None, ALU.mult)
                dve.drain()

            def hg_exponents(l, p, tile):
                dve.wait_ge(acc_full, 1 + tile + 1)
                dve.wait_ge(acc_read[1], 1 + l * ACC_TILES + 2 * p + 1)
                ts(T1[:, 0:T], Q[:, 0:T], CLAMP, None, ALU.max).then_inc(q_clamped, 1)
                tt(T3[:, 0:TP - TP % C].rearrange("p (c t) -> p c t", t=C), bcast(B[:, C - 1:TP:C], C),
                   B[:, 0:TP - TP % C].rearrange("p (c t) -> p c t", t=C), ALU.subtract)
                tt(T3[:, TP - TP % C:TP], B[:, TP - 1:TP].to_broadcast([P, TP % C]), B[:, TP - TP % C:TP], ALU.subtract)
                tt(T3[:, TP:T].rearrange("p (b t) -> p b t", t=DEC_SEQ), bcast(B[:, TP + DEC_SEQ - 1:T:DEC_SEQ], DEC_SEQ),
                   B[:, TP:T].rearrange("p (b t) -> p b t", t=DEC_SEQ), ALU.subtract)
                for n, h in enumerate(LEVELS):
                    end = TP // (2 * h) * 2 * h
                    tt(Z[:, n, 0:end].rearrange("p (b t) -> p b t", t=2 * h), B[:, 0:end].rearrange("p (b t) -> p b t", t=2 * h),
                       bcast(B[:, h - 1:end:2 * h], 2 * h), ALU.subtract)
                tt(DK[:, :].rearrange("p (b t) -> p b t", t=A), B[:, 0:TP].rearrange("p (b t) -> p b t", t=A),
                   bcast(B[:, AT:TP:A], A), ALU.subtract).then_inc(diff_ready, 1)

            def hg_query(l, p, j, mixed):
                n = l * HEADS + p
                dve.wait_ge(q_sig, n + 1)
                tt(Q[:, 0:T], Q[:, 0:T], T1[:, 0:T], ALU.mult)
                dve.drain()
                dve.wait_ge(exps_ready, n + 1)
                tt(KE[:, 0:T], Fb[:, 0:T], T3[:, 0:T], ALU.mult)
                tt(KVS[:, :], Fb[:, TP:T], EN[:, :], ALU.mult)
                for n in range(len(LEVELS)):
                    for z, src in zip(level_halves(n), (level_halves(n, Fb)[0], level_halves(n, Q)[1])):
                        tt(z, z, src, ALU.mult)
                tt(DK[:, :], DK[:, :], Fb[:, 0:TP], ALU.mult)
                tt(DQ[:, :], DQ[:, :], Q[:, 0:TP], ALU.mult)
                split_lo(0, j)
                if mixed is not None:
                    dve.wait_ge(ot_full, mixed)
                tt(QD[:, 0:T], Q[:, 0:T], E[:, 0:T], ALU.mult)
                dve.drain().then_inc(ew_ready, 1)

            def rotate(c, dst):
                tt(halves(T1[0:64, 0:T]), ACC[64:P, c, :, 0:HALF], halves(sinT[64:P, :]), ALU.mult)
                tt(halves(T1[64:P, 0:T]), ACC[0:64, c, :, 0:HALF], halves(sinT[0:64, :]), ALU.mult)
                tt(halves(T2[:, 0:T]), ACC[:, c, :, 0:HALF], halves(cosT), ALU.mult).then_inc(acc_read[c], 1)
                dve.drain()
                tt(dst[:, 0:T], T1[:, 0:T], T2[:, 0:T], ALU.add)

            def rt_key(tile):
                dve.wait_ge(acc_full, 1 + tile + 1)
                rotate(0, KE)

            def rt_query(l, p, j, tile, mixed):
                dve.wait_ge(acc_full, 1 + tile + 1)
                split_lo(0, j)
                if mixed is not None:
                    dve.wait_ge(ot_full, mixed)
                rotate(1, QD)
                dve.drain()
                tt(QS[:, TP:T], QD[:, TP:T], tab[:, ds(cols["q_dec"][0] + p * TS, TS)], ALU.mult)
                dve.drain().then_inc(ew_ready, 1)

            def clamp_gate(hh):
                dve.wait_ge(g_raw, hh + 1)
                ts(R[:, :], G[:, 0:T], CLAMP, None, ALU.max).then_inc(g_clamped, 1)

            def out_gate(hh):
                dve.wait_ge(g_sig, hh + 1)
                tt(G[:, 0:T], G[:, 0:T], R[:, :], ALU.mult).then_inc(g_ready, 1)
                dve.drain()

            def expand_values(hh):
                dve.wait_ge(tok_ready, hh + 1)
                tt(VX[:, :, :], KVTS[:, 1:2, :].to_broadcast([TS, DEC_BATCH, P]), bcast(seqm[0:TS, :], P),
                   ALU.mult).then_inc(vx_ready, 1)

            def sample_states(hh, scr, banks, decayed):
                dve.wait_ge(s0_in, 16 * (hh + 1))
                dve.wait_ge(sn_stored, 16 + 16 * hh)
                decayed()
                dve.drain()
                for n, bank in enumerate(banks):
                    full, _ = scr.job(bank)
                    dve.wait_ge(scr_full, full)
                    w = SN[:, 512 * n:512 * (n + 1)]
                    tt(w, w, SCR[:, bank, :], ALU.add).then_inc(scr_read[bank], 1)
                dve.drain().then_inc(sn_ready, 1)

            def hg_scores(l, p, scr):
                hh = l * 2 * HEADS + p

                def keep_level(n, chunks, bank, o):
                    regular = [c for c in chunks if c[1] == C]
                    m = masks[0:C, n - 1, :].bitcast(mybir.dt.uint32)
                    t, k = regular[0][0], len(regular)
                    last = nc.vector.copy_predicated(PTS[:, t:t + k * C].rearrange("p (c t) -> p c t", t=C),
                                                     m.unsqueeze(1).to_broadcast([C, k, C]),
                                                     SCR[0:C, bank, o:o + k * C].rearrange("p (c t) -> p c t", t=C))
                    for t, w in chunks[k:]:
                        last = nc.vector.copy_predicated(PTS[0:w, t:t + w], m[0:w, 0:w], SCR[0:w, bank, o + k * C:o + k * C + w])
                    return last

                for n, (bank, first, second) in enumerate(HG_JOBS):
                    full, _ = scr.job(bank)
                    dve.wait_ge(scr_full, full)
                    if n == 0:
                        nc.vector.tensor_copy(PTS[0:C // 2, 0:TP - TP % C].rearrange("p (c t) -> p c t", t=C)[:, :, C // 2:C],
                                              SCR[0:C // 2, bank, REST_HG:REST_HG + (NC - 1) * C // 2].rearrange("p (c t) -> p c t", t=C // 2))
                    elif n == 1:
                        tt(PTSS[:, :], SCR[0:TS, bank, SPLIT:SPLIT + TS], mask32[0:TS, :], ALU.mult)
                    else:
                        nc.vector.memset(wait_spot[:, :], 0.0)
                    dve.drain()
                    last = keep_level(*first, bank, 0)
                    if n and second is not None:
                        dve.drain()
                        last = keep_level(*second, bank, REST_HG)
                    last.then_inc(scr_read[bank], 1)
                dve.drain().then_inc(pts_ready, 1)

            def hg_states(l, p, scr):
                hh = l * 2 * HEADS + p
                expand_values(hh)
                dve.wait_ge(fin_stored, 16 + 16 * hh)
                for n in range(2):
                    full, _ = scr.job(n)
                    if n:
                        dve.drain()
                    dve.wait_ge(scr_full, full)
                    for c in range(4 * n, min(4 * n + 4, NC)):
                        u, s = SCR[:, n, (c - 4 * n) * P:(c - 4 * n + 1) * P], SC[:, c * P:(c + 1) * P]
                        if c == 0:
                            last = nc.vector.tensor_copy(s, u)
                        else:
                            if c > 4 * n:
                                dve.drain()
                            end = sum(CHUNKS[c])
                            last = stt(out=s, in0=SC[:, (c - 1) * P:c * P], scalar=E[:, end - 1:end], in1=u,
                                       op0=ALU.mult, op1=ALU.add)
                    last.then_inc(scr_read[n], 1)
                dve.drain().then_inc(states_ready, 1)
                dve.drain().then_inc(fin_ready, 1)
                last_e = E[:, TP + DEC_SEQ - 1:T:DEC_SEQ]
                sample_states(hh, scr, (0, 1), lambda: tt(SNb, S0b, bcast(last_e, P), ALU.mult))

            def low_output(row_, hh):
                dve.wait_ge(oh_ready, hh + 1)
                tt(OL[:, ds(row_, 1), :].rearrange("p o t -> p (o t)"), TO[:, :], OH[:, ds(row_, 1), :].rearrange("p o t -> p (o t)"),
                   ALU.subtract).then_inc(ol_ready, 1)

            def hg_d(l, p):
                hh = l * 2 * HEADS + p
                dve.wait_ge(hr_ready, hh + 1)
                tt(TO[:, 0:SPLIT], OT[:, 0, 0:SPLIT], R[:, 0:SPLIT], ALU.mult)
                tt(TO[:, SPLIT:T], OT[:, 1, 0:REST], R[:, SPLIT:T], ALU.mult).then_inc(ot_read, 1)
                dve.drain()
                stt(out=TO[:, :], in0=TO[:, :], scalar=par[:, ds(l * HEADS + 2 * P + ROW_HG + p, 1)], in1=G[:, 0:T],
                    op0=ALU.mult, op1=ALU.mult).then_inc(to_ready, 1)
                low_output(p, hh)

            def hg_stages(l, p):
                s = scr_hg(l, p)

                def states():
                    for b in (0, 1, 0, 1):
                        s.job(b)
                    hg_states(l, p, s)
                return (lambda: hg_scores(l, p, s)), states, None, (lambda: hg_d(l, p))

            def rt_a(l, p, scr):
                hh = l * 2 * HEADS + HEADS + p
                bank = 1
                for job in RT_JOBS:
                    full, _ = scr.job(bank)
                    dve.wait_ge(scr_full, full)
                    for i, t0, t1, o in job:
                        r = P if i < 4 else TAIL
                        u, w = t0 - i * P, t1 - t0
                        last = tt(PTR[0:r, RT_OFF[i] + u:RT_OFF[i] + u + w], SCR[0:r, bank, o:o + w],
                                  tab[0:r, ds(decay_at + p * TP + u, w)], ALU.mult)
                    if job is RT_JOBS[-1]:
                        last = tt(PTSS[:, :], SCR[0:TS, bank, TAIL:TAIL + TS], tab[0:TS, ds(cols["mask_rt"][0] + p * TS, TS)], ALU.mult)
                    last.then_inc(scr_read[bank], 1)
                    bank = 1 - bank
                dve.drain().then_inc(pts_ready, 1)
                expand_values(hh)

            def rt_b(l, p, scr):
                hh = l * 2 * HEADS + HEADS + p
                scr.job(0)
                sample_states(hh, scr, (1, 0), lambda: ts(SN[:, :], S0[:, :], tab[:, ds(cols["gamma4"][0] + p, 1)], None, ALU.mult))

            def rt_c(l, p, scr):
                for bank, (a, b) in ((1, (0, SPLIT)), (0, (SPLIT, T))):
                    full, _ = scr.job(bank)
                    dve.wait_ge(scr_full, full)
                    nc.vector.tensor_copy(TO[:, a:b], SCR[:, bank, 0:b - a]).then_inc(scr_read[bank], 1)
                dve.drain().then_inc(oc_ready, 1)

            def rt_d(l, p):
                hh = l * 2 * HEADS + HEADS + p
                dve.wait_ge(hr_ready, hh + 1)
                tt(TO[:, :], TO[:, :], R[:, :], ALU.mult)
                dve.drain()
                ts(TO[:, :], TO[:, :], par[:, ds(l * HEADS + 2 * P + ROW_RG + p, 1)],
                   par[:, ds(l * HEADS + 2 * P + ROW_RB + p, 1)], ALU.mult, ALU.add)
                dve.drain()
                tt(TO[:, :], TO[:, :], G[:, 0:T], ALU.mult).then_inc(to_ready, 1)
                low_output(HEADS + p, hh)

            def rt_stages(l, p):
                s = scr_rt(l, p)
                for b in (0, 1, 0):
                    s.job(b)
                return (lambda: rt_a(l, p, s)), (lambda: rt_b(l, p, s)), (lambda: rt_c(l, p, s)), (lambda: rt_d(l, p))

            def group(l, g, head, kind, stages=(None,) * 4, mixed=None, mixed_kind=None):
                a, b, c, d = stages
                j, tile = l * SLOT_UNITS + g, l * TILES + 4 * g
                hh = l * 2 * HEADS + kind * HEADS + head
                split_lo(1, j)
                if kind == 0:
                    if a is not None:
                        a()
                    hg_gate(l, head, tile)
                    if b is not None:
                        b()
                    hg_exponents(l, head, tile + 1)
                    hg_query(l, head, j + 1, mixed)
                else:
                    if a is not None:
                        a()
                    if mixed_kind == 0:
                        dve.wait_ge(tok_ready, hh)
                    rt_key(tile)
                    if b is not None:
                        b()
                    rt_query(l, head, j + 1, tile + 1, mixed)
                if d is not None:
                    out_gate(hh - 1)
                if c is not None:
                    c()
                if d is not None:
                    d()
                clamp_gate(hh)

            for counter in (*w_lo, acc_full, *acc_read, ot_read, sq_used, h_ready):
                dve.drain().then_inc(counter, 1)
            dve.wait_ge(params_ready, 1)
            lb = par[:, 2 * P + ROW_LB:2 * P + ROW_LB + 2 * HEADS].rearrange("p (l h) -> p l h", l=DEPTH)
            for l in range(DEPTH):
                ts(CW2[:, l * FT:(l + 1) * FT], par[:, l * P + 2 * FT:l * P + 3 * FT], INV_W, None, ALU.mult)
            tt(LE[:, 0, :], lb[:, 0, :], lb[:, 1, :], ALU.max)
            dve.drain()
            for l in range(DEPTH):
                last = tt(LE[:, 1 + l, :], lb[:, l, :], LE[:, 0, :], ALU.subtract)
            last.then_inc(lb_max, 1)
            dve.wait_ge(lb_exp, 1)
            tt(LE[:, 3, :], LE[:, 1, :], LE[:, 2, :], ALU.add)
            dve.drain()
            nc.vector.reciprocal(LE[:, 3, :], LE[:, 3, :])
            dve.drain()
            for l in range(DEPTH):
                tt(LE[:, 1 + l, :], LE[:, 1 + l, :], LE[:, 3, :], ALU.mult)
            dve.drain()
            tt(LBT[:, 0:HEADS], LE[:, 1, :], LE[:, 1, :], ALU.subtract)
            tt(LE[:, 4, :], LE[:, 1, :], LE[:, 2, :], ALU.add)
            dve.drain()
            tt(LBT[:, HEADS:2 * HEADS], LE[:, 4, :], LE[:, 1, :], ALU.subtract)
            dve.drain()
            ts(OMLB[:, :], LBT[:, :], -1.0, 1.0, ALU.mult, ALU.add)
            dve.drain()

            scr = Scratch((1, 1, 0))
            for i in range(TT5):
                n = P if i < 4 else R5
                for q in range(2):
                    full, _ = scr.job(1 - q)
                    dve.wait_ge(scr_full, full)
                    nc.vector.tensor_copy(X[:, 4 * q:4 * q + 4, i * P:i * P + n],
                                          SCR[:, 1 - q, :].rearrange("p (k t) -> p k t", k=4)[:, :, 0:n]).then_inc(scr_read[1 - q], 1)
            dve.drain().then_inc(y_ready, 1)
            dve.wait_ge(pts_zero, 1)
            zero_sums()
            with dve.Fori(0, KT) as m:
                add_sums(0, m)

            with dve.Fori(0, DEPTH) as l:
                ot0 = l * OT_LAYER
                split_lo(0, l * SLOT_UNITS)
                norm_apply(2 * l, Scratch(base(l)))
                group(l, 0, 0, 0)
                with dve.Fori(0, HEADS - 1) as p:
                    group(l, p + 1, p + 1, 0, hg_stages(l, p), ot0 + 2 + p)
                group(l, HEADS, 0, 1, hg_stages(l, HEADS - 1), ot0 + 1 + HEADS, 0)
                with dve.Fori(0, HEADS - 1) as p:
                    group(l, p + HEADS + 1, p + 1, 1, rt_stages(l, p), ot0 + 2 + HEADS + 2 * p)
                out_gate((l + 1) * 2 * HEADS - 1)
                for stage_ in rt_stages(l, HEADS - 1):
                    stage_()

                zero_sums()
                with dve.Fori(0, 2) as i:
                    for n in range(4):
                        if n % 2 == 0:
                            split_lo(1 - n // 2, l * SLOT_UNITS + 8 + i + n // 2)
                        residual(l, 2 * l + 1, 4 * i + n, n % 2, O_TILE + 4 * i + n)
                norm_apply(2 * l + 1, scr_ln1(l))

                dve.wait_ge(cst_ready, l + 1)
                dve.wait_ge(sn_stored, 16 + (l + 1) * 2 * HEADS * 16)
                dve.wait_ge(fin_stored, 16 + (l + 1) * 2 * HEADS * 16)
                for c in range(2):
                    nc.vector.memset(AX[c][:, 0:2], 0.0)
                dve.drain()
                with dve.Fori(0, FT // 2) as i:
                    n0 = l * FT + 2 * i
                    split_lo(1, l * SLOT_UNITS + 10 + i)
                    for c in range(2):
                        ax, cx, ft = AX[c], CX[c], 2 * i + c
                        w0, w1 = (par[:, ds(l * P + n * FT + 2 * i + c, 1)] for n in range(2))
                        dve.wait_ge(a_ready, n0 + c + 1)
                        nc.vector.tensor_copy(AS[:, :, 2:6], ax[:, 2 + TP:2 + T].rearrange("p (b t) -> p b t", t=DEC_SEQ))
                        nc.vector.tensor_copy(AS[:, :, 0:2], CST[:, ds(ft, 1), :].rearrange("p o (b j) -> p (o b) j", j=2))
                        stt(out=cx[:, 0:TP], in0=ax[:, 1:1 + TP], scalar=w1, in1=cx[:, 0:TP], op0=ALU.mult, op1=ALU.add)
                        dve.drain()
                        cs = cx[:, TP:T].rearrange("p (b t) -> p b t", t=DEC_SEQ)
                        stt(out=cs, in0=AS[:, :, 1:5], scalar=w1, in1=cs, op0=ALU.mult, op1=ALU.add)
                        stt(out=cx[:, 0:TP], in0=ax[:, 0:TP], scalar=w0, in1=cx[:, 0:TP], op0=ALU.mult, op1=ALU.add)
                        nc.vector.tensor_copy(CSB[:, ds(ft, 1), 0:2].rearrange("p o j -> p (o j)"), ax[:, TP:TP + 2])
                        nc.vector.tensor_copy(CSB[:, ds(ft, 1), 2:18].rearrange("p o (b j) -> p (o b) j", j=2), AS[:, :, 4:6])
                        dve.drain()
                        stt(out=cs, in0=AS[:, :, 0:4], scalar=w0, in1=cs, op0=ALU.mult, op1=ALU.add)
                        dve.drain().then_inc(conv_ready, 1)
                    split_lo(0, l * SLOT_UNITS + 11 + i)
                    for c in range(2):
                        cx = CX[c]
                        dve.wait_ge(gelu_ready, n0 + c + 1)
                        dve.wait_ge(acc_full, 1 + l * TILES + F_TILE + 4 * i + 3 + c)
                        stt(out=halves(cx[:, 0:T]), in0=ACC[:, c, :, 0:HALF], scalar=INV_W, in1=halves(cx[:, 0:T]),
                            op0=ALU.mult, op1=ALU.mult).then_inc(acc_read[c], 1)
                        dve.drain().then_inc(ht_ready, 1)
                    for c in range(2):
                        one = lambda t: t[:, ds(2 * i + c, 1), :].rearrange("p o t -> p (o t)")
                        dve.wait_ge(hh_ready, n0 + c + 1)
                        tt(one(HL), CX[c][:, 0:T], one(HH), ALU.subtract).then_inc(h_ready, 1)

                zero_sums()

                def down(q, last):
                    for c in range(2):
                        split_lo(1, l * SLOT_UNITS + 21 + 2 * q + c, UNIT_D)
                        if not (last and c == 1):
                            split_lo(0, l * SLOT_UNITS + 22 + 2 * q + c, UNIT_D)
                        residual(l, 2 * l + 2, 2 * q + c, c, D_TILE + 2 * q + c)
                with dve.Fori(0, KT // 2 - 1) as q:
                    down(q, False)
                down(KT // 2 - 1, True)
            norm_apply(2 * DEPTH, Scratch(base(DEPTH)), last=True)


N_PARAM_DMAS = 2 * DEPTH + 2 * (2 * DEPTH + 1) + 4
RT_JOBS = [[(0, 0, SPLIT, 0)], [(0, SPLIT, TP, 0)], [(1, P, TP, 0)],
           [(2, 2 * P, TP, 0), (3, 3 * P, TP, TP - 2 * P)], [(4, 4 * P, TP, 0)]]


HG_SLOTS = ([1, 2, 3, 4, 5, 6, 7], [10, 11, 12, 13], [15, 16], [17, 18], [21, 21, 22, 22, 23, 23], [28, 29])
REST_HG = TP - SPLIT
LEFT, RIGHT = CHUNKS[:3], CHUNKS[3:]
HG_JOBS = [(1, (1, RIGHT), (0, None)), (0, (1, LEFT), None), (1, (2, LEFT), None), (0, (2, RIGHT), (3, RIGHT)),
           (1, (3, LEFT), None), (0, (4, LEFT), None), (1, (4, RIGHT), None)]
RT_SLOTS = ([3, 4, 5], [6, 7, 8, 9, 10], [11], [12, 13], [15, 16], [21, 22], [28])


_INS = ['x_prompt', 'x_sample', 'state_hgrn', 'state_ret', 'state_conv', 'meta_tokens', 'emb_ln_g', 'emb_ln_b',
        'lb_logits', 'w_in', 'hg_norm_g', 'rt_gn_g', 'rt_gn_b', 'w_o', 'ln1_g', 'ln1_b', 'w_a', 'w_b', 'conv_w',
        'conv_b', 'w_down', 'ln2_g', 'ln2_b']
_OUTS = [(1, SEQ, D_MODEL), (DEC_BATCH, DEC_SEQ, D_MODEL), (DEPTH, 1, HEADS, P, P), (DEPTH, DEC_BATCH, HEADS, P, P),
         (DEPTH, 1, HEADS, P, P), (DEPTH, DEC_BATCH, HEADS, P, P), (DEPTH, 1, CONV_W - 1, D_FF),
         (DEPTH, DEC_BATCH, CONV_W - 1, D_FF)]


def kernel(**inputs):
    import concourse.bacc as _bacc
    from concourse.bass_utils import run_bass_kernel_spmd as _run

    nc = _bacc.Bacc("TRN2", target_bir_lowering=False, num_devices=1)
    arrays, args = {}, []
    for name in _INS:
        a = np.ascontiguousarray(inputs[name])
        arrays[f"in_{name}_dram"] = a
        args.append(nc.dram_tensor(f"in_{name}_dram", a.shape, mybir.dt.from_np(a.dtype), kind="ExternalInput").ap())
    tables = const_tables()
    arrays["in_tables_dram"] = tables
    args.append(nc.dram_tensor("in_tables_dram", tables.shape, F32, kind="ExternalInput").ap())
    for i, shape in enumerate(_OUTS):
        args.append(nc.dram_tensor(f"out_{i}_dram", shape, F32, kind="ExternalOutput").ap())
    hybrid_decoder_step(nc, *args)
    r = _run(nc, [arrays], core_ids=[0])
    return tuple(r.results[0][f"out_{i}_dram"] for i in range(len(_OUTS)))
```

```python
from contextlib import ExitStack

import concourse.bass as bass
import numpy as np
from concourse import mybir

F32 = mybir.dt.float32
F16 = mybir.dt.float16
ALU = mybir.AluOpType
ACT = mybir.ActivationFunctionType

P = 128
D_MODEL = 1024
DEPTH = 2
SEQ = 512
N_META = 16
DEC_BATCH = 8
DEC_SEQ = 4
PAST_LEN = 4096
HEADS = 4
D_FF = 2816
CONV_W = 3
LN_EPS = 1e-5
LOG_F_MIN = float(np.log(1e-6))
ALPHA = (2 * DEPTH) ** 0.25

TP = N_META + SEQ
TS = DEC_BATCH * DEC_SEQ
T = TP + TS
HALF = T // 2
KT = D_MODEL // P
FT = D_FF // P
KD = FT // 2
UNIT = KT * 2 * P
UNIT_D = KD * P
W_SCALE = 64.0
INV_W = 1.0 / W_SCALE

C = 96
CHUNKS = [(t, min(C, TP - t)) for t in range(0, TP, C)]
NC = len(CHUNKS)
LEVELS = (48, 24, 12, 6)
A = 6
AT = 2
SPLIT = 3 * C
REST = T - SPLIT
CLAMP = -44.0

TT5 = 5
R5 = T - 4 * P
TAIL = TP - 4 * P
RT_COLS = [TP - P * i for i in range(TT5)]
RT_OFF = [sum(RT_COLS[:i]) for i in range(TT5)]

U_P, U_O, U_F, U_D = 16, 4, 22, 16
SLOT_UNITS = (U_P + U_O + U_F + U_D) // 2
TILES = 32 + 8 + 2 * FT + 8
ACC_TILES = TILES // 2
O_TILE, F_TILE, D_TILE = 32, 40, 40 + 2 * FT
SCR_START = (11, 6, 5)
SCR_LN = (2, 1, 1)
SCR_HG = (17, 9, 8)
SCR_RT = (13, 7, 6)
SCR_CIN = (1, 1, 0)
SCR_COUT = (6, 3, 3)
SCR_LAYER = tuple(2 * a + HEADS * (b + c) + d + e for a, b, c, d, e in zip(SCR_LN, SCR_HG, SCR_RT, SCR_CIN, SCR_COUT))
OT_LAYER = 2 + HEADS + 2 * HEADS
ROW_HG, ROW_RG, ROW_RB, ROW_LB, ROWS2 = 80, 88, 96, 104, 112
ROWS01 = (CONV_W + 1) * FT


def const_columns():
    at, out = 0, {}
    for name, width in [("ident", P), ("ones_ln", P), ("ones_h", P), ("center", P), ("eps", 8), ("cos", T), ("sin", T),
                        ("keep", T), ("masks", len(LEVELS) * C), ("mask32", TS), ("seq", DEC_BATCH), ("decay", HEADS * TP),
                        ("mask_rt", HEADS * TS), ("q_dec", HEADS * TS), ("k_dec", TT5 * HEADS), ("k_dec_s", HEADS),
                        ("gamma4", HEADS)]:
        out[name] = (at, width)
        at += width
    return out, at


def const_tables():
    cols, n = const_columns()
    tab = np.zeros((P, n), np.float32)

    def put(name, value):
        at, width = cols[name]
        value = np.asarray(value, np.float32).reshape(len(value), width)
        tab[:len(value), at:at + width] = value

    put("ident", np.eye(P))
    put("ones_ln", np.full((P, P), 1.0 / D_MODEL))
    put("ones_h", np.full((P, P), 1.0 / P))
    put("center", np.eye(P) - 1.0 / P)
    eps = np.zeros((P, 8))
    eps[:, 0] = LN_EPS
    eps[:, 1:5] = LN_EPS / ALPHA ** 2
    eps[:, 5] = LN_EPS
    put("eps", eps)
    half = P // 2
    inv = np.float32(10000.0) ** (-np.arange(half, dtype=np.float32) / np.float32(half))
    pos = np.concatenate([np.arange(TP), np.tile(PAST_LEN + np.arange(DEC_SEQ), DEC_BATCH)]).astype(np.float32)
    ang = inv[:, None] * pos[None, :]
    put("cos", np.concatenate([np.cos(ang)] * 2) * INV_W)
    put("sin", np.concatenate([np.sin(ang), -np.sin(ang)]) * INV_W)
    keep = np.ones((P, T))
    keep[:, 0:TP:C] = 0
    keep[:, TP::DEC_SEQ] = 0
    put("keep", keep)
    s, t = np.arange(C)[:, None], np.arange(C)[None, :]
    levels = [(s // (2 * h) == t // (2 * h)) & (s % (2 * h) < h) & (t % (2 * h) >= h) for h in LEVELS[1:]]
    put("masks", np.concatenate(levels + [(s // A == t // A) & (s <= t)], 1))
    tok = np.arange(TS)
    same = tok[:, None] // DEC_SEQ == tok[None, :] // DEC_SEQ
    causal = same & (tok[:, None] <= tok[None, :])
    put("mask32", causal)
    put("seq", tok[:, None] // DEC_SEQ == np.arange(DEC_BATCH)[None, :])
    log_g = np.log1p(-np.exp2(-5.0 - np.arange(HEADS)))
    s, u = np.arange(P)[:, None, None], np.arange(TP)[None, None, :]
    root = P ** -0.5
    rel = np.maximum(u - s, 0)
    put("decay", np.where(u >= s, np.exp(rel * log_g[None, :, None]), 0.0) * root)
    rel = np.maximum(tok[None, :] - tok[:, None], 0)
    put("mask_rt", np.where(causal[:, None, :], np.exp(rel[:, None, :] * log_g[None, :, None]), 0.0) * root)
    put("q_dec", np.broadcast_to(np.exp((tok % DEC_SEQ + 1)[None, None, :] * log_g[None, :, None]), (P, HEADS, TS)))
    left = TP - 1 - (np.arange(TT5)[None, :, None] * P + np.arange(P)[:, None, None])
    put("k_dec", np.where(left >= 0, np.exp(np.maximum(left, 0) * log_g[None, None, :]), 0.0) * root)
    put("k_dec_s", np.exp((DEC_SEQ - 1 - tok % DEC_SEQ)[:, None] * log_g[None, :]) * root)
    put("gamma4", np.broadcast_to(np.exp(DEC_SEQ * log_g), (P, HEADS)))
    return tab


class Scratch:

    def __init__(self, base, *done):
        self.full, self.bank = base[0], [base[1], base[2]]
        for d in done:
            self.full, self.bank = self.full + d[0], [self.bank[0] + d[1], self.bank[1] + d[2]]

    def job(self, bank):
        free = self.bank[bank]
        self.full, self.bank[bank] = self.full + 1, free + 1
        return self.full, free


def hybrid_decoder_step(nc, x_prompt, x_sample, state_hgrn, state_ret, state_conv, meta_tokens, emb_ln_g, emb_ln_b,
                        lb_logits, w_in, hg_norm_g, rt_gn_g, rt_gn_b, w_o, ln1_g, ln1_b, w_a, w_b, conv_w, conv_b,
                        w_down, ln2_g, ln2_b, consts, y_prompt, y_sample, hg_prompt, hg_sample, rt_prompt,
                        rt_sample, conv_prompt, conv_sample):
    cols, n_const = const_columns()
    ds = bass.ds

    w_in_v = w_in.rearrange("l (k p) c -> p (l k) c", p=P)
    w_o_v = w_o.rearrange("l (k p) c -> p (l k) c", p=P)
    w_a_v = w_a.rearrange("l (k p) c -> p (l k) c", p=P)
    w_b_v = w_b.rearrange("l (k p) c -> p (l k) c", p=P)
    w_down_v = w_down.rearrange("l (k p) c -> p (l k) c", p=P)
    s0_hg_v = state_hgrn.rearrange("l b h k v -> (l b h) k v")
    s0_rt_v = state_ret.rearrange("l b h k v -> (l b h) k v")
    sn_hg_v = hg_sample.rearrange("l b h k v -> (l b h) k v")
    sn_rt_v = rt_sample.rearrange("l b h k v -> (l b h) k v")
    fin_hg_v = hg_prompt.rearrange("l b h k v -> (l b h k) v")
    fin_rt_v = rt_prompt.rearrange("l b h k v -> (l b h k) v")
    cin_v = state_conv.rearrange("l b j f -> (l b j) f")
    cp_v = conv_prompt.rearrange("l b j f -> (l b j) f")
    cs_v = conv_sample.rearrange("l b j f -> (l b j) f")
    SEQS = DEC_BATCH * HEADS

    with ExitStack() as ctx:
        def sb(name, shape, dt=F32):
            return ctx.enter_context(nc.sbuf_tensor(name, shape, dt))

        def sem(name):
            return ctx.enter_context(nc.semaphore(name))

        tab = sb("tab", [P, n_const])
        X = sb("X", [P, KT, T])
        XH, XL = sb("XH", [P, KT, T], F16), sb("XL", [P, KT, T], F16)
        OHL = sb("OHL", [P, 2 * KT, T], F16)
        OH, OL = OHL[:, 0:KT, :], OHL[:, KT:2 * KT, :]
        stage = sb("stage", [P, 2, UNIT])
        WH, WL = sb("WH", [P, 2, UNIT], F16), sb("WL", [P, 2, UNIT], F16)
        shared = sb("shared", [P, FT * T])
        HHL = shared[:, :].bitcast(F16).rearrange("p (k t) -> p k t", k=2 * FT)
        HH, HL = HHL[:, 0:FT, :], HHL[:, FT:2 * FT, :]
        Z = sb("Z", [P, len(LEVELS), TP])
        DK, DQ = sb("DK", [P, TP]), sb("DQ", [P, TP])
        Fb, T1, T2, T3, B, Q, QS, QD, KE, E, V, G = (
            sb(n, [P, T + 2]) for n in ("Fb", "T1", "T2", "T3", "B", "Q", "QS", "QD", "KE", "E", "V", "G"))
        at = [0]

        def part(width):
            at[0] += width
            return shared[:, at[0] - width:at[0]]

        KTOK, VTOK, SC = part(NC * P), part(NC * P), part(NC * P)
        KVTOK = shared[:, 0:2 * NC * P].rearrange("p (n c) -> p n c", n=2)
        S0, SN = part(DEC_BATCH * P), part(DEC_BATCH * P)
        PTR = part(RT_OFF[-1] + TAIL)
        SQ, R, TO = part(T), part(T), part(T)
        assert at[0] <= FT * T - D_FF
        CIN = shared[0:2 * DEC_BATCH, FT * T - D_FF:FT * T]
        CSO = OHL[:, :, :].rearrange("p k t -> p (k t)").bitcast(F32)[0:2 + 2 * DEC_BATCH, 0:D_FF]
        XT = shared[:, 0:TT5 * D_MODEL].rearrange("p (i d) -> p i d", i=TT5)
        S0b, SNb = (t.rearrange("p (b v) -> p b v", b=DEC_BATCH) for t in (S0, SN))
        S1, S2, SQT, MU, MSQ, VAR, RSTD = B, Q, E, T1, T2, T3, QS
        AX, CX = (T1, T2), (T3, Fb)
        VX = sb("VX", [TS, DEC_BATCH, P])
        KVTS = sb("KVTS", [TS, 2, P])
        PTS = sb("PTS", [C, TP])
        PTSS = sb("PTSS", [TS, TS])
        RSB = sb("RSB", [P, P])
        KVS = sb("KVS", [P, TS])
        EN = sb("EN", [P, TS])
        AS = sb("AS", [P, DEC_BATCH, CONV_W - 1 + DEC_SEQ])
        CST = sb("CST", [P, FT, 2 * DEC_BATCH])
        CSB = sb("CSB", [P, FT, 2 + 2 * DEC_BATCH])
        rows = stage[:, 1, 0:3 * P].rearrange("p (b c) -> p b c", b=3)
        unread = sb("unread", [1, 3])
        wait_spot = sb("wait_spot", [1, 1])
        par = sb("par", [P, 3 * P])
        CW2 = sb("CW2", [P, DEPTH * FT])
        LBT, OMLB = sb("LBT", [P, DEPTH * HEADS]), sb("OMLB", [P, DEPTH * HEADS])
        LE = sb("LE", [P, 6, HEADS])

        def table(name):
            a, w = cols[name]
            return tab[:, a:a + w]

        first_tables = cols["cos"][0]
        ident, ones_ln, ones_h, center = (table(n) for n in ("ident", "ones_ln", "ones_h", "center"))
        cosT, sinT, keep, mask32, seqm = (table(n) for n in ("cos", "sin", "keep", "mask32", "seq"))
        masks = table("masks").rearrange("p (n t) -> p n t", t=C)
        decay_at, eps_at = cols["decay"][0], cols["eps"][0]

        ACC = ctx.enter_context(nc.psum_tensor("ACC", [P, 2, 2, 512], F32))
        OT = ctx.enter_context(nc.psum_tensor("OT", [P, 2, 512], F32))
        SCR = ctx.enter_context(nc.psum_tensor("SCR", [P, 2, 512], F32))

        consts_in, tables_in, params_in = sem("consts_in"), sem("tables_in"), sem("params_in")
        x_in = [sem(f"x_in{i}") for i in range(3)]
        stage_full = [sem(f"stage_full{s}") for s in range(2)]
        w_hi = [sem(f"w_hi{s}") for s in range(2)]
        w_lo = [sem(f"w_lo{s}") for s in range(2)]
        half_used = sem("half_used")
        acc_full = sem("acc_full")
        acc_read = [sem(f"acc_read{s}") for s in range(2)]
        scr_full = sem("scr_full")
        scr_read = [sem(f"scr_read{s}") for s in range(2)]
        ot_full, ot_read = sem("ot_full"), sem("ot_read")
        params_ready, lb_max, lb_exp = sem("params_ready"), sem("lb_max"), sem("lb_exp")
        pts_zero = sem("pts_zero")
        y_ready, sq_ready, sq_used, sums_ready = sem("y_ready"), sem("sq_ready"), sem("sq_used"), sem("sums_ready")
        mu_ready, msq_ready, var_ready, rstd_ready = sem("mu_ready"), sem("msq_ready"), sem("var_ready"), sem("rstd_ready")
        ln_mul, ln_sub, ln_out, x_ready = sem("ln_mul"), sem("ln_sub"), sem("ln_out"), sem("x_ready")
        f_ready, lnf_parts, f2_ready, k_ready = sem("f_ready"), sem("lnf_parts"), sem("f2_ready"), sem("k_ready")
        q_clamped, q_sig, diff_ready, exps_ready = sem("q_clamped"), sem("q_sig"), sem("diff_ready"), sem("exps_ready")
        ew_ready, v_ready, g_raw, g_clamped, g_sig, g_ready = (
            sem(n) for n in ("ew_ready", "v_ready", "g_raw", "g_clamped", "g_sig", "g_ready"))
        tok_ready, vx_ready, pts_ready, states_ready = sem("tok_ready"), sem("vx_ready"), sem("pts_ready"), sem("states_ready")
        decays_used = sem("decays_used")
        sn_decayed, e_ready = sem("sn_decayed"), sem("e_ready")
        sn_ready, s0_in, sn_stored, fin_stored, fin_ready = (
            sem("sn_ready"), sem("s0_in"), sem("sn_stored"), sem("fin_stored"), sem("fin_ready"))
        o_copied, oc_ready, hsq_ready, hr_ready = sem("o_copied"), sem("oc_ready"), sem("hsq_ready"), sem("hr_ready")
        to_ready, oh_ready, ol_ready = sem("to_ready"), sem("oh_ready"), sem("ol_ready")
        cin_in, cst_ready, a_ready, conv_ready, gelu_ready = (
            sem("cin_in"), sem("cst_ready"), sem("a_ready"), sem("conv_ready"), sem("gelu_ready"))
        ht_ready, hh_ready, h_ready, cso_ready, cso_stored = (
            sem("ht_ready"), sem("hh_ready"), sem("h_ready"), sem("cso_ready"), sem("cso_stored"))
        out_ready, out_right, out_stored = sem("out_ready"), sem("out_right"), sem("out_stored")

        def halves(ap):
            return ap.rearrange("p (a n) -> p a n", a=2)

        def base(l):
            return tuple(s + l * n for s, n in zip(SCR_START, SCR_LAYER))

        def scr_hg(l, p):
            return Scratch(base(l), SCR_LN, tuple(p * n for n in SCR_HG))

        def scr_rt(l, p):
            return Scratch(base(l), SCR_LN, tuple(HEADS * n for n in SCR_HG), tuple(p * n for n in SCR_RT))

        def scr_cin(l):
            return scr_rt(l, HEADS)

        def scr_ln1(l):
            return Scratch(tuple(scr_rt(l, HEADS).job(0)[:1]) + tuple(scr_rt(l, HEADS).bank), (0, 1, 0))

        def scr_cout(l):
            s = scr_ln1(l)
            return Scratch((s.full, *s.bank), SCR_LN)

        def bcast(ap, n):
            return ap.unsqueeze(2).to_broadcast([ap.shape[0], ap.shape[1], n])

        def level_halves(n, src=None):
            h, end = LEVELS[n], TP // (2 * LEVELS[n]) * 2 * LEVELS[n]
            v = (Z[:, n, 0:end] if src is None else src[:, 0:end]).rearrange("p (b t) -> p b t", t=2 * h)
            return v[:, :, 0:h], v[:, :, h:2 * h]

        block = ctx.enter_context(nc.Block())

        @block.sync
        def _(sp):
            xp = x_prompt.rearrange("b t d -> (b t) d")
            first = P - N_META
            sp.dma_start(XT[0:N_META, 0, :], meta_tokens).then_inc(x_in[0], 16)
            sp.dma_start(XT[N_META:P, 0, :], xp[0:first, :]).then_inc(x_in[0], 16)
            sp.dma_start(XT[:, 1:4, :], xp[first:first + 3 * P, :].rearrange("(i p) d -> p i d", p=P)).then_inc(x_in[1], 16)
            sp.dma_start(XT[0:TAIL, 4, :], xp[first + 3 * P:SEQ, :]).then_inc(x_in[2], 16)
            sp.dma_start(XT[TAIL:R5, 4, :], x_sample.rearrange("b t d -> (b t) d")).then_inc(x_in[2], 16)

            def load(s, j, halves_):
                sp.wait_ge(w_lo[s], 1 + j)
                for dst, src in halves_:
                    sp.dma_start(dst, src).then_inc(stage_full[s], 16)

            def unit(s):
                return stage[:, s, :].rearrange("p (k c) -> p k c", k=KT)

            def load_sections(s, j, l, p, sections):
                load(s, j, [(unit(s)[:, :, P * n:P * n + P], w_in_v[:, ds(l * KT, KT), ds(p * P + sec * HEADS * P, P)])
                            for n, sec in enumerate(sections)])

            def load_columns(s, j, l, w, c):
                load(s, j, [(unit(s)[:, k:k + KT // 2, :], w[:, ds(l * KT + k, KT // 2), ds(c, 2 * P)])
                            for k in (0, KT // 2)])

            def load_down(s, j, l, m, part_):
                d = stage[:, s, 0:UNIT_D].rearrange("p (k c) -> p k c", k=KD)
                load(s, j, [(d[:, a:b, :], w_down_v[:, ds(l * FT + part_ * KD + a, b - a), ds(m * P, P)])
                            for a, b in ((0, 6), (6, KD))])

            sp.wait_ge(scr_full, SCR_START[0])
            with sp.Fori(0, DEPTH) as l:
                j0 = l * SLOT_UNITS
                with sp.Fori(0, HEADS) as p:
                    load_sections(0, j0 + p, l, p, (1, 0))
                    load_sections(1, j0 + p, l, p, (2, 3))
                with sp.Fori(0, HEADS) as p:
                    load_sections(0, j0 + HEADS + p, l, p, (5, 4))
                    load_sections(1, j0 + HEADS + p, l, p, (6, 7))
                with sp.Fori(0, 2) as i:
                    load_columns(0, j0 + 8 + i, l, w_o_v, i * 4 * P)
                    load_columns(1, j0 + 8 + i, l, w_o_v, i * 4 * P + 2 * P)
                with sp.Fori(0, FT // 2) as i:
                    load_columns(0, j0 + 10 + i, l, w_a_v, i * 2 * P)
                    load_columns(1, j0 + 10 + i, l, w_b_v, i * 2 * P)
                with sp.Fori(0, KT) as m:
                    load_down(0, j0 + 21 + m, l, m, 0)
                    load_down(1, j0 + 21 + m, l, m, 1)

        @block.gpsimd
        def _(pool):
            for n, counter in enumerate((fin_stored, sn_stored, cso_stored)):
                pool.dma_start(unread[0:1, n:n + 1], consts[0:1, 0:1]).then_inc(counter, 16)
            nc.gpsimd.memset(PTS[:, :], 0.0).then_inc(pts_zero, 1)

            def move(ready, out, src, done):
                pool.wait_ge(params_ready, 1)
                pool.wait_ge(*ready)
                pool.dma_start(out, src).then_inc(done, 16)

            def norm_centre(n):
                pool.wait_ge(mu_ready, n + 1)
                for m in range(KT):
                    nc.gpsimd.tensor_tensor(X[:, m, :], X[:, m, :], MU[:, 0:T], ALU.subtract).then_inc(ln_sub, 1)

            def head_states(l, p, kind, s0_v, sn_v, fin_v, fin_src):
                hh = l * 2 * HEADS + kind * HEADS + p
                ot_done = l * OT_LAYER + 1 + (p if kind == 0 else HEADS + 2 * p)
                move((ot_full, ot_done), S0b, s0_v[ds(l * SEQS + p, DEC_BATCH, HEADS)].rearrange("b k v -> k b v"), s0_in)
                pool.wait_ge(tok_ready, hh + 1)
                nc.gpsimd.tensor_tensor(VX[:, :, :], KVTS[:, 1:2, :].to_broadcast([TS, DEC_BATCH, P]), bcast(seqm[0:TS, :], P),
                                        ALU.mult).then_inc(vx_ready, 1)
                if kind == 0:
                    pool.wait_ge(s0_in, 16 * (hh + 1))
                    pool.wait_ge(sn_stored, 16 + 16 * hh)
                    nc.gpsimd.tensor_tensor(SNb, S0b, bcast(E[:, TP + DEC_SEQ - 1:T:DEC_SEQ], P), ALU.mult).then_inc(sn_decayed, 1)
                move((fin_ready, hh + 1), fin_v[ds((l * HEADS + p) * P, P), :], fin_src, fin_stored)
                move((sn_ready, hh + 1), sn_v[ds(l * SEQS + p, DEC_BATCH, HEADS)].rearrange("b k v -> k b v"), SNb, sn_stored)

            with pool.Fori(0, DEPTH) as l:
                norm_centre(2 * l)
                move((acc_full, 1 + l * TILES), CIN, cin_v[ds(l * 2 * DEC_BATCH, 2 * DEC_BATCH), :], cin_in)
                with pool.Fori(0, HEADS) as p:
                    head_states(l, p, 0, s0_hg_v, sn_hg_v, fin_hg_v, SC[:, (NC - 1) * P:NC * P])
                with pool.Fori(0, HEADS) as p:
                    head_states(l, p, 1, s0_rt_v, sn_rt_v, fin_rt_v, RSB[:, :])
                norm_centre(2 * l + 1)
                move((cso_ready, l + 1), cp_v[ds(l * 2, 2), :], CSO[0:2, :], cso_stored)
                move((cso_ready, l + 1), cs_v[ds(l * 2 * DEC_BATCH, 2 * DEC_BATCH), :], CSO[2:18, :], cso_stored)
            norm_centre(2 * DEPTH)
            pool.wait_ge(fin_stored, 16 + 16 * DEPTH * 2 * HEADS)
            pool.wait_ge(sn_stored, 16 + 16 * DEPTH * 2 * HEADS)
            pool.wait_ge(cso_stored, 16 + 32 * DEPTH)

        @block.tensor
        def _(pe):
            mm = nc.tensor.matmul

            def job(scr, bank):
                _, free = scr.job(bank)
                pe.wait_ge(scr_read[bank], free)

            def transpose_params(scr):
                pe.wait_ge(params_in, 16 * N_PARAM_DMAS)
                job(scr, 0)
                for b, (at_, n) in enumerate(((0, ROWS01), (P, ROWS01), (2 * P, ROWS2))):
                    last = nc.tensor.transpose(SCR[:, 0, at_:at_ + n], rows[0:n, b, :], ident[0:n, 0:n])
                last.then_inc(scr_full, 1)

            def transpose_x(scr):
                pe.wait_ge(consts_in, 16)
                for i in range(TT5):
                    n = P if i < 4 else R5
                    if i in (0, 1, 4):
                        pe.wait_ge(x_in[(i + 2) // 3], (32, 16, 32)[(i + 2) // 3])
                    for q in range(2):
                        bank = 1 - q
                        _, free = scr.job(bank)
                        if i:
                            pe.wait_ge(scr_read[bank], free)
                        for k in range(4):
                            last = nc.tensor.transpose(SCR[:, bank, k * P:k * P + n],
                                                       XT[0:n, i, (4 * q + k) * P:(4 * q + k + 1) * P], ident[0:n, 0:n])
                        last.then_inc(scr_full, 1)

            def norm_means():
                pe.wait_ge(y_ready, 1)
                for h in range(2):
                    for m in range(KT):
                        last = mm(OT[:, h, 0:HALF], ones_ln, X[:, m, h * HALF:(h + 1) * HALF], start=(m == 0), stop=(m == KT - 1))
                last.then_inc(ot_full, 1)

            def norm_stats(n, ot, scr, means=True):
                pe.wait_ge(sums_ready, n + 1)
                if means:
                    pe.wait_ge(ot_read, 1 + ot)
                    for h in range(2):
                        last = mm(OT[:, h, 0:HALF], ones_ln, S1[:, h * HALF:(h + 1) * HALF], start=True, stop=True)
                    last.then_inc(ot_full, 1)
                for h in range(2):
                    _, free = scr.job(h)
                    pe.wait_ge(scr_read[h], free)
                    mm(SCR[:, h, 0:HALF], ones_ln, S2[:, h * HALF:(h + 1) * HALF], start=True, stop=True).then_inc(scr_full, 1)

            def products(acc, s, width, col, wk, xh, xl, xk, n, first, final, wait_k=None, between=()):
                for k in range(n):
                    for step in between[k] if between else ():
                        step()
                    if wait_k is not None:
                        pe.wait_ge(wait_k[0], wait_k[1] + k)
                    for w, x in ((WH, xh), (WH, xl), (WL, xh)):
                        lhs = w[:, s, wk(k) * width + col:wk(k) * width + col + P]
                        begin = first and k == 0 and w is WH and x is xh
                        end = final and k == n - 1 and w is WL
                        for h in range(2):
                            last = mm(ACC[:, acc, h, 0:HALF], lhs, x[:, xk + k, h * HALF:(h + 1) * HALF], start=begin, stop=end)
                return last

            def gemm_tile(l, j, s, c, half_tile, xh, xl, wait_k=None, between=()):
                if c == 0:
                    pe.wait_ge(w_lo[s], 1 + j + 1)
                pe.wait_ge(acc_read[c], 1 + l * ACC_TILES + half_tile)
                products(c, s, 2 * P, c * P, lambda k: k, xh, xl, 0, KT, True, True, wait_k, between).then_inc(acc_full, 1)

            def gemm_pair(l, j, half_tile, xh, xl, wait_k):
                pe.wait_ge(w_lo[0], 1 + j + 1)
                for c in range(2):
                    pe.wait_ge(acc_read[c], 1 + l * ACC_TILES + half_tile)
                for k in range(KT):
                    for c in range(2):
                        last = products(c, 0, 2 * P, c * P, lambda _, k=k: k, xh, xl, k, 1, k == 0, k == KT - 1,
                                        (wait_k[0], wait_k[1] + k) if c == 0 else None)
                        if k == KT - 1:
                            last.then_inc(acc_full, 1)

            def hg_steps(l, p, scr, slots):
                hh = l * 2 * HEADS + p

                def level(n, chunks, bank, o):
                    keys, queries = (Z[:, n, :], Z[:, n, :]) if n < len(LEVELS) else (DK[:, :], DQ[:, :])
                    for t, w in chunks:
                        last = mm(SCR[0:w, bank, o:o + w], keys[:, t:t + w], queries[:, t:t + w], start=True, stop=True)
                        o += w
                    return last

                def scores(n):
                    bank, first, second = HG_JOBS[n]
                    if n == 0:
                        pe.wait_ge(ew_ready, hh + 1)
                    job(scr, bank)
                    last = level(*first, bank, 0)
                    if second is not None and second[0] == 0:
                        for c in range(NC - 1):
                            last = mm(SCR[0:C // 2, bank, REST_HG + c * C // 2:REST_HG + (c + 1) * C // 2],
                                      Z[:, 0, C * c:C * c + C // 2], Z[:, 0, C * c + C // 2:C * c + C], start=True, stop=True)
                    elif second is not None:
                        last = level(*second, bank, REST_HG)
                    if n == 1:
                        last = mm(SCR[0:TS, bank, SPLIT:SPLIT + TS], KVS[:, :], QD[:, TP:T], start=True, stop=True)
                    last.then_inc(scr_full, 1)

                def transposes(n):
                    if n == 0:
                        pe.wait_ge(v_ready, hh + 1)
                    bank, sources = 1 - n % 2, (KE, V)
                    job(scr, bank)
                    if n < 2:
                        for c in range(4):
                            w = P if c == 0 else C
                            last = nc.tensor.transpose(SCR[0:w, bank, c * P:(c + 1) * P], sources[n][:, C * c:C * c + w], ident)
                    elif n == 2:
                        for i, (c, src) in enumerate((c, src) for c in (4, 5) for src in sources):
                            w = P if c == 4 else CHUNKS[5][1]
                            last = nc.tensor.transpose(SCR[0:w, bank, i * P:(i + 1) * P], src[:, C * c:C * c + w], ident)
                    else:
                        for i, src in enumerate(sources):
                            last = nc.tensor.transpose(SCR[0:TS, bank, i * P:(i + 1) * P], src[:, TP:T], ident)
                    last.then_inc(scr_full, 1)

                def state_steps(n):
                    if n == 0:
                        pe.wait_ge(tok_ready, hh + 1)
                    job(scr, 1 - n)
                    for c in range(4 * n, min(4 * n + 4, NC)):
                        w = CHUNKS[c][1]
                        last = mm(SCR[:, 1 - n, (c - 4 * n) * P:(c - 4 * n + 1) * P], KTOK[0:w, c * P:(c + 1) * P],
                                  VTOK[0:w, c * P:(c + 1) * P], start=True, stop=True)
                    last.then_inc(scr_full, 1)

                def output(c):
                    if c == 0:
                        pe.wait_ge(pts_ready, hh + 1)
                        pe.wait_ge(states_ready, l * HEADS + p + 1)
                        pe.wait_ge(s0_in, 16 * (hh + 1))
                        pe.wait_ge(ot_read, 1 + l * OT_LAYER + 1 + p)
                    t, w = CHUNKS[c]
                    o = OT[:, c // 3, (c % 3) * C:(c % 3) * C + w]
                    if c:
                        mm(o, SC[:, (c - 1) * P:c * P], QD[:, t:t + w], start=True, stop=False)
                    mm(o, VTOK[0:w, c * P:(c + 1) * P], PTS[0:w, t:t + w], start=(c == 0), stop=True)
                    if c == NC - 1:
                        sample_output(QD).then_inc(ot_full, 1)

                def mean_square(bank):
                    if bank == 0:
                        pe.wait_ge(hsq_ready, hh + 1)
                    a, b = ((0, SPLIT), (SPLIT, T))[bank]
                    job(scr, bank)
                    mm(SCR[:, bank, 0:b - a], ones_h, SQ[:, a:b], start=True, stop=True).then_inc(scr_full, 1)

                steps = [(slots[0][n], lambda n=n: scores(n)) for n in range(len(HG_JOBS))]
                steps += [(slots[1][n], lambda n=n: transposes(n)) for n in range(4)]
                steps += [(slots[2][n], lambda n=n: state_steps(n)) for n in range(2)]
                steps += [(slots[3][n], lambda n=n: sample_steps(hh, scr, n, 1 - n)) for n in range(2)]
                steps += [(slots[4][c], lambda c=c: output(c)) for c in range(NC)]
                steps += [(slots[5][n], lambda n=n: mean_square(n)) for n in range(2)]
                return steps

            def sample_steps(hh, scr, n, bank):
                if n == 0:
                    pe.wait_ge(vx_ready, hh + 1)
                job(scr, bank)
                mm(SCR[:, bank, :], KVTS[:, 0, :], VX[:, 4 * n:4 * n + 4, :].rearrange("p b v -> p (b v)"),
                   start=True, stop=True).then_inc(scr_full, 1)

            def sample_output(qs):
                cols_ = OT[:, 1, TP - SPLIT:REST]
                mm(cols_, KVTS[:, 1, :], PTSS[:, :], start=True, stop=False, skip_group_check=True)
                for b in range(DEC_BATCH):
                    last = mm(OT[:, 1, TP - SPLIT + DEC_SEQ * b:TP - SPLIT + DEC_SEQ * (b + 1)], S0b[:, b, :],
                              qs[:, TP + DEC_SEQ * b:TP + DEC_SEQ * (b + 1)], start=False, stop=(b == DEC_BATCH - 1),
                              skip_group_check=True)
                return last

            def rt_steps(l, p, scr):
                hh = l * 2 * HEADS + HEADS + p

                def transposes(bank, src):
                    if src is KE:
                        pe.wait_ge(ew_ready, hh + 1)
                        pe.wait_ge(v_ready, hh + 1)
                    job(scr, bank)
                    for i in range(4):
                        last = nc.tensor.transpose(SCR[:, bank, i * P:(i + 1) * P], src[:, i * P:(i + 1) * P], ident)
                    last.then_inc(scr_full, 1)

                def rest_transposes():
                    job(scr, 0)
                    for n, src in enumerate((KE, V)):
                        nc.tensor.transpose(SCR[0:TAIL, 0, n * P:(n + 1) * P], src[:, 4 * P:TP], ident)
                        last = nc.tensor.transpose(SCR[0:TS, 0, (2 + n) * P:(3 + n) * P], src[:, TP:T], ident)
                    last.then_inc(scr_full, 1)

                def scores(n):
                    bank = 1 - n % 2
                    job(scr, bank)
                    for i, t0, t1, o in RT_JOBS[n]:
                        rows_ = P if i < 4 else TAIL
                        last = mm(SCR[0:rows_, bank, o:o + t1 - t0], KE[:, i * P:i * P + rows_], QD[:, t0:t1], start=True, stop=True)
                    if n == len(RT_JOBS) - 1:
                        last = mm(SCR[0:TS, bank, TAIL:TAIL + TS], KE[:, TP:T], QD[:, TP:T], start=True, stop=True)
                    last.then_inc(scr_full, 1)

                def final_state():
                    pe.wait_ge(tok_ready, hh + 1)
                    job(scr, 0)
                    for i in range(TT5):
                        r = P if i < 4 else TAIL
                        last = mm(SCR[:, 0, 0:P], KTOK[0:r, i * P:(i + 1) * P], VTOK[0:r, i * P:(i + 1) * P], start=(i == 0), stop=(i == 4))
                    last.then_inc(scr_full, 1)

                def output(h):
                    if h == 0:
                        pe.wait_ge(pts_ready, hh + 1)
                        pe.wait_ge(s0_in, 16 * (hh + 1))
                        pe.wait_ge(ot_read, 1 + l * OT_LAYER + 1 + HEADS + 2 * p)
                    a, b = ((0, SPLIT), (SPLIT, TP))[h]
                    tiles = [i for i in range(TT5) if i * P < b]
                    for i in tiles:
                        r, t0 = (P if i < 4 else TAIL), max(a, i * P)
                        mm(OT[:, h, t0 - a:b - a], VTOK[0:r, i * P:(i + 1) * P],
                           PTR[0:r, RT_OFF[i] + t0 - i * P:RT_OFF[i] + b - i * P], start=(i == 0), stop=(i == tiles[-1]),
                           skip_group_check=True)
                    if h == 1:
                        sample_output(QS).then_inc(ot_full, 1)

                def centre(bank):
                    if bank == 1:
                        pe.wait_ge(o_copied, l * HEADS + p + 1)
                    a, b = ((SPLIT, T), (0, SPLIT))[bank]
                    job(scr, bank)
                    mm(SCR[:, bank, 0:b - a], center, SQ[:, a:b], start=True, stop=True).then_inc(scr_full, 1)

                def variance():
                    pe.wait_ge(hsq_ready, hh + 1)
                    pe.wait_ge(ot_read, 1 + l * OT_LAYER + 2 + HEADS + 2 * p)
                    mm(OT[:, 0, 0:SPLIT], ones_h, SQ[:, 0:SPLIT], start=True, stop=True)
                    mm(OT[:, 1, 0:REST], ones_h, SQ[:, SPLIT:T], start=True, stop=True).then_inc(ot_full, 1)

                steps = [(RT_SLOTS[0][0], lambda: transposes(0, KE)), (RT_SLOTS[0][1], lambda: transposes(1, V)),
                         (RT_SLOTS[0][2], rest_transposes)]
                steps += [(RT_SLOTS[1][n], lambda n=n: scores(n)) for n in range(len(RT_JOBS))]
                steps += [(RT_SLOTS[2][0], final_state)]
                steps += [(RT_SLOTS[3][n], lambda n=n: sample_steps(hh, scr, n, 1 - n)) for n in range(2)]
                steps += [(RT_SLOTS[4][h], lambda h=h: output(h)) for h in range(2)]
                steps += [(RT_SLOTS[5][n], lambda n=n: centre(1 - n)) for n in range(2)]
                steps += [(RT_SLOTS[6][0], variance)]
                return steps

            def group(l, g, steps=()):
                j = l * SLOT_UNITS + g
                if not steps:
                    gemm_pair(l, j, 2 * g, XH, XL, (x_ready, 2 * l * KT + 1))
                for n in range(0 if steps else 2, 4):
                    between = [[f for slot, f in steps if slot == KT * n + k] for k in range(KT)]
                    gemm_tile(l, j, n // 2, n % 2, 2 * g + n // 2, XH, XL, None, between)

            def conv_states(l):
                pe.wait_ge(cin_in, 16 * (l + 1))
                job(scr_cin(l), 0)
                for f in range(FT):
                    last = mm(SCR[:, 0, f * 16:(f + 1) * 16], CIN[:, f * P:(f + 1) * P], ident[0:16, 0:16], start=True, stop=True)
                last.then_inc(scr_full, 1)

            def output_projection(l, steps):
                j = l * SLOT_UNITS + 8
                pe.wait_ge(w_lo[0], 1 + j + 1)
                for c in range(2):
                    pe.wait_ge(acc_read[c], 1 + l * ACC_TILES + O_TILE // 2)
                    products(c, 0, 2 * P, c * P, lambda k: k, OH, OL, 0, KT - 1, True, False,
                             (ol_ready, l * 2 * HEADS + 1) if c == 0 else None,
                             [[f for slot, f in steps if slot // 2 == (KT - 1) * c + k] for k in range(KT - 1)])
                for slot, step in steps:
                    if slot // 2 >= 2 * (KT - 1):
                        step()
                conv_states(l)
                for c in range(2):
                    products(c, 0, 2 * P, c * P, lambda k: KT - 1, OH, OL, KT - 1, 1, False, True,
                             (ol_ready, (l + 1) * 2 * HEADS)).then_inc(acc_full, 1)
                for n in range(2, 8):
                    gemm_tile(l, j + n // 4, n // 2 % 2, n % 2, O_TILE // 2 + n // 2, OH, OL)

            scr = Scratch((0, 0, 0))
            transpose_x(scr)
            transpose_params(scr)
            norm_means()
            norm_stats(0, 0, Scratch(base(0)), means=False)
            with pe.Fori(0, DEPTH) as l:
                group(l, 0)
                with pe.Fori(0, HEADS - 1) as p:
                    group(l, p + 1, hg_steps(l, p, scr_hg(l, p), HG_SLOTS))
                group(l, HEADS, hg_steps(l, HEADS - 1, scr_hg(l, HEADS - 1), HG_SLOTS_RT))
                with pe.Fori(0, HEADS - 1) as p:
                    group(l, p + HEADS + 1, rt_steps(l, p, scr_rt(l, p)))
                output_projection(l, rt_steps(l, HEADS - 1, scr_rt(l, HEADS - 1)))
                norm_stats(2 * l + 1, l * OT_LAYER + OT_LAYER - 1, scr_ln1(l))

                gemm_pair(l, l * SLOT_UNITS + 10, F_TILE // 2, XH, XL, (x_ready, (2 * l + 1) * KT + 1))
                for n in range(2, 4):
                    gemm_tile(l, l * SLOT_UNITS + 10, 1, n % 2, F_TILE // 2 + 1, XH, XL)
                with pe.Fori(1, FT // 2) as i:
                    for n in range(4):
                        gemm_tile(l, l * SLOT_UNITS + 10 + i, n // 2, n % 2, F_TILE // 2 + 2 * i + n // 2, XH, XL)

                pe.wait_ge(conv_ready, (l + 1) * FT)
                scr = scr_cout(l)
                for q in range(6):
                    bank = 1 - q % 2
                    _, free = scr.job(bank)
                    pe.wait_ge(scr_read[bank], free)
                    for f in range(4 * q, min(4 * q + 4, FT)):
                        last = nc.tensor.transpose(SCR[0:18, bank, (f - 4 * q) * P:(f - 4 * q + 1) * P], CSB[:, f, :], ident)
                    last.then_inc(scr_full, 1)

                with pe.Fori(0, KT // 2) as q:
                    for c in range(2):
                        j = l * SLOT_UNITS + 21 + 2 * q + c
                        pe.wait_ge(acc_read[c], 1 + l * ACC_TILES + D_TILE // 2 + q)
                        for s in range(2):
                            pe.wait_ge(w_lo[s], 1 + j + 1)
                            products(c, s, P, 0, lambda k: k, HH, HL, s * KD, KD, s == 0, s == 1,
                                     (h_ready, 1 + l * FT + s * KD + 1) if c == 0 else None
                                     ).then_inc(acc_full if s == 1 else half_used, 1)
                norm_stats(2 * l + 2, (l + 1) * OT_LAYER, Scratch(base(l + 1)))
            scr = Scratch(base(DEPTH), SCR_LN)
            pe.wait_ge(ln_out, (2 * DEPTH + 1) * KT)
            for i in range(TT5):
                n = P if i < 4 else R5
                for q in range(2):
                    _, free = scr.job(q)
                    pe.wait_ge(scr_read[q], free)
                    for k in range(4):
                        last = nc.tensor.transpose(SCR[0:n, q, k * P:(k + 1) * P], X[:, 4 * q + k, i * P:i * P + n], ident)
                    last.then_inc(scr_full, 1)

        @block.scalar
        def _(act):
            f = nc.scalar.activation

            act.dma_start(tab[:, 0:first_tables], consts[:, 0:first_tables]).then_inc(consts_in, 16)
            loads = []
            for l in range(DEPTH):
                loads.append((rows[0:CONV_W * FT, l, :], conv_w[l].rearrange("j (f p) -> (j f) p", p=P)))
                loads.append((rows[CONV_W * FT:ROWS01, l, :], conv_b[l].rearrange("(f p) -> f p", p=P)))
            norms = [(emb_ln_g, emb_ln_b)] + [pr for l in range(DEPTH) for pr in ((ln1_g[l], ln1_b[l]), (ln2_g[l], ln2_b[l]))]
            for n, pr in enumerate(norms):
                for h, src in enumerate(pr):
                    loads.append((rows[16 * n + 8 * h:16 * n + 8 * h + 8, 2, :], src.rearrange("(k p) -> k p", p=P)))
            for at_, src in ((ROW_HG, hg_norm_g), (ROW_RG, rt_gn_g), (ROW_RB, rt_gn_b), (ROW_LB, lb_logits)):
                loads.append((rows[at_:at_ + 8, 2, :], src.rearrange("l (h p) -> (l h) p", p=P)))
            assert len(loads) == N_PARAM_DMAS
            for dst, src in loads:
                act.dma_start(dst, src).then_inc(params_in, 16)
            act.dma_start(tab[:, first_tables:n_const], consts[:, first_tables:n_const]).then_inc(tables_in, 16)

            def split_hi(s, j, used, width=UNIT):
                act.wait_ge(*used)
                act.wait_ge(stage_full[s], 32 * (j + 1))
                f(WH[:, s, 0:width], stage[:, s, 0:width], ACT.Copy, scale=W_SCALE).then_inc(w_hi[s], 1)

            def squares(n, m, y):
                act.wait_ge(y_ready, y)
                act.wait_ge(sq_used, 1 + n * KT + m)
                src = X[:, m, :] if isinstance(m, int) else X[:, ds(m, 1), :].rearrange("p o t -> p (o t)")
                f(SQT[:, 0:T], src, ACT.Square).then_inc(sq_ready, 1)

            def norm_apply(n, ot, last=False):
                act.wait_ge(ot_full, ot + 1)
                src = OT[:, :, 0:HALF]
                f(halves(MU[:, 0:T]), src, ACT.Copy).then_inc(mu_ready, 1)
                f(halves(MSQ[:, 0:T]), src, ACT.Square).then_inc(ot_read, 1)
                act.drain().then_inc(msq_ready, 1)
                act.wait_ge(var_ready, n + 1)
                f(RSTD[:, 0:T], VAR[:, 0:T], ACT.Ln, bias=tab[:, ds(eps_at + n, 1)])
                act.drain()
                f(RSTD[:, 0:T], RSTD[:, 0:T], ACT.Exp, scale=-0.5).then_inc(rstd_ready, 1)
                for m in range(KT):
                    act.wait_ge(ln_mul, n * KT + m + 1)
                    g, b = (par[:, ds(n * 16 + 2 * P + m + 8 * h, 1)] for h in range(2))
                    if not last:
                        f(XH[:, m, :], X[:, m, :], ACT.Identity, scale=g, bias=b)
                    f(X[:, m, :], X[:, m, :], ACT.Identity, scale=g, bias=b).then_inc(ln_out, 1)

            def sigmoid(buf, width, done):
                f(buf[:, 0:width], buf[:, 0:width], ACT.Exp, scale=-1.0)
                act.drain()
                f(buf[:, 0:width], buf[:, 0:width], ACT.Ln, bias=1.0)
                act.drain()
                f(buf[:, 0:width], buf[:, 0:width], ACT.Exp, scale=-1.0).then_inc(done, 1)

            def read_acc(buf, c, tile, done):
                act.wait_ge(acc_full, 1 + tile + 1)
                f(halves(buf[:, 0:T]), ACC[:, c, :, 0:HALF], ACT.Copy, scale=INV_W).then_inc(acc_read[c], 1)
                if done is not None:
                    act.drain().then_inc(done, 1)

            def hg_gate(l, p):
                n = l * HEADS + p
                act.wait_ge(f_ready, n + 1)
                f(T1[:, 0:T], Fb[:, 0:T], ACT.Exp, scale=-1.0)
                act.drain()
                f(T2[:, 0:T], T1[:, 0:T], ACT.Ln, bias=1.0)
                f(T3[:, 0:T], T1[:, 0:T], ACT.Ln, bias=1.0, scale=LBT[:, ds(n, 1)]).then_inc(lnf_parts, 1)
                act.wait_ge(f2_ready, n + 1)
                f(Fb[:, 0:T], Fb[:, 0:T], ACT.Exp, scale=-1.0)
                act.drain()
                f(Fb[:, 0:T], Fb[:, 0:T], ACT.Copy, scale=OMLB[:, ds(n, 1)]).then_inc(k_ready, 1)

            def hg_exponentials(l, p):
                act.wait_ge(diff_ready, l * HEADS + p + 1)
                f(T3[:, 0:T], T3[:, 0:T], ACT.Exp)
                f(EN[:, :], B[:, TP:T], ACT.Exp, scale=-1.0)
                for n in range(len(LEVELS)):
                    for z, sign in zip(level_halves(n), (-1.0, 1.0)):
                        f(z, z, ACT.Exp, scale=sign)
                f(DQ[:, :], DK[:, :], ACT.Exp)
                f(DK[:, :], DK[:, :], ACT.Exp, scale=-1.0).then_inc(exps_ready, 1)

            def hg_query(l, p):
                act.wait_ge(q_clamped, l * HEADS + p + 1)
                sigmoid(T1, T, q_sig)
                act.wait_ge(decays_used, 1 + l * HEADS + p)
                act.wait_ge(sn_decayed, 1 + l * HEADS + p)
                f(E[:, 0:T], B[:, 0:T], ACT.Exp).then_inc(e_ready, 1)

            def out_gate(hh):
                act.wait_ge(g_clamped, hh + 1)
                sigmoid(R, T, g_sig)

            def hg_a(l, p, scr):
                for bank, dst in ((1, KTOK), (0, VTOK)):
                    full, _ = scr.job(bank)
                    act.wait_ge(scr_full, full)
                    f(dst[0:C, 0:4 * P], SCR[0:C, bank, :], ACT.Copy).then_inc(scr_read[bank], 1)
                full, _ = scr.job(1)
                act.wait_ge(scr_full, full)
                for c in (4, 5):
                    w = CHUNKS[c][1]
                    last = f(KVTOK[0:w, :, c * P:(c + 1) * P],
                             SCR[0:w, 1, 2 * (c - 4) * P:2 * (c - 3) * P].rearrange("p (n v) -> p n v", n=2), ACT.Copy)
                last.then_inc(scr_read[1], 1)
                full, _ = scr.job(0)
                act.wait_ge(scr_full, full)
                f(KVTS[:, :, :], SCR[0:TS, 0, 0:2 * P].rearrange("p (n v) -> p n v", n=2), ACT.Copy).then_inc(scr_read[0], 1)
                act.drain().then_inc(tok_ready, 1)

            def hg_c(l, p):
                act.wait_ge(ot_full, l * OT_LAYER + 2 + p)
                f(SQ[:, 0:SPLIT], OT[:, 0, 0:SPLIT], ACT.Square)
                f(SQ[:, SPLIT:T], OT[:, 1, 0:REST], ACT.Square).then_inc(hsq_ready, 1)

            def high_output(row, hh):
                act.wait_ge(to_ready, hh + 1)
                f(OH[:, ds(row, 1), :].rearrange("p o t -> p (o t)"), TO[:, :], ACT.Copy).then_inc(oh_ready, 1)

            eps_h = tab[:, eps_at + 5:eps_at + 6]

            def hg_d(l, p, scr):
                hh = l * 2 * HEADS + p
                act.wait_ge(g_ready, hh + 1)
                for bank, (a, b) in enumerate(((0, SPLIT), (SPLIT, T))):
                    full, _ = scr.job(bank)
                    act.wait_ge(scr_full, full)
                    f(R[:, a:b], SCR[:, bank, 0:b - a], ACT.Ln, bias=eps_h).then_inc(scr_read[bank], 1)
                act.drain()
                f(R[:, :], R[:, :], ACT.Exp, scale=-0.5).then_inc(hr_ready, 1)
                high_output(p, hh)

            def hg_stages(l, p):
                s = scr_hg(l, p)
                for b, _, _ in HG_JOBS:
                    s.job(b)

                def d():
                    for b in (1, 0, 1, 0):
                        s.job(b)
                    hg_d(l, p, s)
                return (lambda: hg_a(l, p, s)), None, (lambda: hg_c(l, p)), None, d

            def rt_a(l, p, scr):
                k_at = cols["k_dec"][0]
                full, _ = scr.job(0)
                act.wait_ge(scr_full, full)
                for i in range(4):
                    last = f(KTOK[:, i * P:(i + 1) * P], SCR[:, 0, i * P:(i + 1) * P], ACT.Copy, scale=tab[:, ds(k_at + i * HEADS + p, 1)])
                last.then_inc(scr_read[0], 1)
                full, _ = scr.job(1)
                act.wait_ge(scr_full, full)
                f(VTOK[:, 0:4 * P], SCR[:, 1, :], ACT.Copy).then_inc(scr_read[1], 1)
                full, _ = scr.job(0)
                act.wait_ge(scr_full, full)
                f(KTOK[0:TAIL, 4 * P:5 * P], SCR[0:TAIL, 0, 0:P], ACT.Copy, scale=tab[0:TAIL, ds(k_at + 4 * HEADS + p, 1)])
                f(VTOK[0:TAIL, 4 * P:5 * P], SCR[0:TAIL, 0, P:2 * P], ACT.Copy)
                f(KVTS[:, 0, :], SCR[0:TS, 0, 2 * P:3 * P], ACT.Copy, scale=tab[0:TS, ds(cols["k_dec_s"][0] + p, 1)])
                f(KVTS[:, 1, :], SCR[0:TS, 0, 3 * P:4 * P], ACT.Copy).then_inc(scr_read[0], 1)
                act.drain().then_inc(tok_ready, 1)
                for bank in (1, 0, 1, 0, 1):
                    scr.job(bank)

            def rt_b(l, p, scr):
                hh = l * 2 * HEADS + HEADS + p
                full, _ = scr.job(0)
                act.wait_ge(fin_stored, 16 + 16 * hh)
                act.wait_ge(scr_full, full)
                f(RSB[:, :], SCR[:, 0, 0:P], ACT.Copy).then_inc(scr_read[0], 1)
                act.drain().then_inc(fin_ready, 1)
                act.wait_ge(ot_full, l * OT_LAYER + 2 + HEADS + 2 * p)
                f(SQ[:, 0:SPLIT], OT[:, 0, 0:SPLIT], ACT.Copy)
                f(SQ[:, SPLIT:T], OT[:, 1, 0:REST], ACT.Copy).then_inc(ot_read, 1)
                act.drain().then_inc(o_copied, 1)

            def rt_c(l, p):
                act.wait_ge(oc_ready, l * HEADS + p + 1)
                f(SQ[:, :], TO[:, :], ACT.Square).then_inc(hsq_ready, 1)

            def rt_d(l, p):
                hh = l * 2 * HEADS + HEADS + p
                act.wait_ge(g_ready, hh + 1)
                act.wait_ge(ot_full, l * OT_LAYER + 3 + HEADS + 2 * p)
                f(R[:, 0:SPLIT], OT[:, 0, 0:SPLIT], ACT.Ln, bias=eps_h)
                f(R[:, SPLIT:T], OT[:, 1, 0:REST], ACT.Ln, bias=eps_h).then_inc(ot_read, 1)
                act.drain()
                f(R[:, :], R[:, :], ACT.Exp, scale=-0.5).then_inc(hr_ready, 1)
                high_output(HEADS + p, hh)

            def rt_stages(l, p):
                s = scr_rt(l, p)
                return (lambda: rt_a(l, p, s)), (lambda: rt_b(l, p, s)), None, (lambda: rt_c(l, p)), (lambda: rt_d(l, p))

            def group(l, g, head, kind, stages=(None,) * 5):
                a, b, output_squares, c, d = stages
                j, tile = l * SLOT_UNITS + g, l * TILES + 4 * g
                hh = l * 2 * HEADS + kind * HEADS + head
                split_hi(1, j, (acc_full, 1 + tile))
                if output_squares is not None:
                    out_gate(hh - 1)
                if a is not None:
                    a()
                if kind == 0:
                    hg_gate(l, head)
                if b is not None:
                    b()
                if kind == 0:
                    if d is None:
                        read_acc(Q, 1, tile + 1, None)
                    hg_exponentials(l, head)
                    if d is not None:
                        read_acc(Q, 1, tile + 1, None)
                split_hi(0, j + 1, (acc_full, 1 + tile + 2))
                if kind == 0:
                    hg_query(l, head)
                if output_squares is not None:
                    output_squares()
                if c is not None:
                    out_gate(hh - 1)
                    c()
                read_acc(V, 0, tile + 2, v_ready)
                if d is not None:
                    d()
                read_acc(G, 1, tile + 3, g_raw)

            act.wait_ge(scr_full, SCR_START[0])
            for b, n in ((0, ROWS01), (1, ROWS01), (2, ROWS2)):
                last = f(par[:, b * P:b * P + n], SCR[:, 0, b * P:b * P + n], ACT.Copy)
            last.then_inc(scr_read[0], 1)
            act.drain().then_inc(params_ready, 1)
            nc.scalar.preload_act_table_set("natural_log_exp_and_others")
            act.wait_ge(lb_max, 1)
            f(LE[:, 1:3, :], LE[:, 1:3, :], ACT.Exp).then_inc(lb_exp, 1)
            act.wait_ge(y_ready, 1)
            for m in range(KT):
                if m >= 2:
                    act.wait_ge(sq_used, 1 + m - 1)
                f((E, QD)[m % 2][:, 0:T], X[:, m, :], ACT.Square).then_inc(sq_ready, 1)

            with act.Fori(0, DEPTH) as l:
                nc.scalar.preload_act_table_set("natural_log_exp_and_others")
                split_hi(0, l * SLOT_UNITS, (acc_full, 1 + l * TILES))
                norm_apply(2 * l, l * OT_LAYER)
                act.wait_ge(cso_stored, 16 + 32 * l)
                group(l, 0, 0, 0)
                with act.Fori(0, HEADS - 1) as p:
                    group(l, p + 1, p + 1, 0, hg_stages(l, p))
                group(l, HEADS, 0, 1, hg_stages(l, HEADS - 1))
                with act.Fori(0, HEADS - 1) as p:
                    group(l, p + HEADS + 1, p + 1, 1, rt_stages(l, p))
                out_gate((l + 1) * 2 * HEADS - 1)
                for stage_ in rt_stages(l, HEADS - 1):
                    if stage_ is not None:
                        stage_()

                full, _ = scr_cin(l).job(0)
                act.wait_ge(scr_full, full)
                f(CST[:, :, :], SCR[:, 0, 0:FT * 16].rearrange("p (f b) -> p f b", f=FT), ACT.Copy).then_inc(scr_read[0], 1)
                act.drain().then_inc(cst_ready, 1)

                with act.Fori(0, 2) as i:
                    for n in range(4):
                        if n % 2 == 0:
                            split_hi(1 - n // 2, l * SLOT_UNITS + 8 + i + n // 2, (acc_full, 1 + l * TILES + O_TILE + 4 * i + n))
                        squares(2 * l + 1, 4 * i + n, 2 + 2 * l * KT + 4 * i + n)
                nc.scalar.preload_act_table_set("natural_log_exp_and_others")
                norm_apply(2 * l + 1, l * OT_LAYER + OT_LAYER - 1)

                nc.scalar.preload_act_table(ACT.Gelu_apprx_tanh)
                act.wait_ge(sn_stored, 16 + (l + 1) * 2 * HEADS * 16)
                act.wait_ge(fin_stored, 16 + (l + 1) * 2 * HEADS * 16)
                with act.Fori(0, FT // 2) as i:
                    n0 = l * FT + 2 * i
                    split_hi(1, l * SLOT_UNITS + 10 + i, (acc_full, 1 + l * TILES + F_TILE + 4 * i))
                    for c in range(2):
                        act.wait_ge(h_ready, 1 + n0)
                        act.wait_ge(acc_full, 1 + l * TILES + F_TILE + 4 * i + c + 1)
                        f(halves(AX[c][:, 2:2 + T]), ACC[:, c, :, 0:HALF], ACT.Copy, scale=INV_W)
                        f(halves(CX[c][:, 0:T]), ACC[:, c, :, 0:HALF], ACT.Identity, scale=CW2[:, ds(n0 + c, 1)],
                          bias=par[:, ds(l * P + CONV_W * FT + 2 * i + c, 1)]).then_inc(acc_read[c], 1)
                        act.drain().then_inc(a_ready, 1)
                    split_hi(0, l * SLOT_UNITS + 11 + i, (acc_full, 1 + l * TILES + F_TILE + 4 * i + 2))
                    for c in range(2):
                        act.wait_ge(conv_ready, n0 + c + 1)
                        f(CX[c][:, 0:T], CX[c][:, 0:T], ACT.Gelu_apprx_tanh).then_inc(gelu_ready, 1)
                    for c in range(2):
                        act.wait_ge(ht_ready, n0 + c + 1)
                        f(HH[:, ds(2 * i + c, 1), :].rearrange("p o t -> p (o t)"), CX[c][:, 0:T], ACT.Copy).then_inc(hh_ready, 1)

                scr = scr_cout(l)
                for q in range(6):
                    bank = 1 - q % 2
                    full, _ = scr.job(bank)
                    w = (min(4 * q + 4, FT) - 4 * q) * P
                    act.wait_ge(scr_full, full)
                    f(CSO[:, 4 * q * P:4 * q * P + w], SCR[0:18, bank, 0:w], ACT.Copy).then_inc(scr_read[bank], 1)
                act.drain().then_inc(cso_ready, 1)

                def down(q, last):
                    for c in range(2):
                        split_hi(1, l * SLOT_UNITS + 21 + 2 * q + c, (acc_full, 1 + l * TILES + D_TILE + 2 * q + c), UNIT_D)
                        if not (last and c == 1):
                            split_hi(0, l * SLOT_UNITS + 22 + 2 * q + c, (half_used, l * KT + 2 * q + c + 1), UNIT_D)
                        squares(2 * l + 2, 2 * q + c, 2 + (2 * l + 1) * KT + 2 * q + c)
                with act.Fori(0, KT // 2 - 1) as q:
                    down(q, False)
                down(KT // 2 - 1, True)
            nc.scalar.preload_act_table_set("natural_log_exp_and_others")
            norm_apply(2 * DEPTH, DEPTH * OT_LAYER, last=True)
            scr = Scratch(base(DEPTH), SCR_LN)
            for i in range(TT5):
                n = P if i < 4 else R5
                full, _ = scr.job(0)
                scr.job(1)
                act.wait_ge(scr_full, full)
                f(XT[0:n, i, 0:512], SCR[0:n, 0, :], ACT.Copy).then_inc(scr_read[0], 1)
                act.drain().then_inc(out_ready, 1)
                act.wait_ge(out_ready, i + 1)
                act.wait_ge(out_right, i + 1)
                yp = y_prompt.rearrange("b t d -> (b t) d")
                if i == 0:
                    act.dma_start(yp[0:P - N_META, :], XT[N_META:P, 0, :]).then_inc(out_stored, 16)
                elif i < 4:
                    act.dma_start(yp[i * P - N_META:(i + 1) * P - N_META, :], XT[:, i, :]).then_inc(out_stored, 16)
                else:
                    act.dma_start(yp[4 * P - N_META:SEQ, :], XT[0:TAIL, 4, :]).then_inc(out_stored, 16)
                    act.dma_start(y_sample.rearrange("b t d -> (b t) d"), XT[TAIL:R5, 4, :]).then_inc(out_stored, 16)
            act.wait_ge(out_stored, 16 * 6)

        @block.vector
        def _(dve):
            tt, ts, stt = nc.vector.tensor_tensor, nc.vector.tensor_scalar, nc.vector.scalar_tensor_tensor

            def split_lo(s, j, width=UNIT):
                dve.wait_ge(w_hi[s], j + 1)
                stt(out=WL[:, s, 0:width], in0=stage[:, s, 0:width], scalar=W_SCALE, in1=WH[:, s, 0:width],
                    op0=ALU.mult, op1=ALU.subtract).then_inc(w_lo[s], 1)

            def row(m):
                return X[:, m, :] if isinstance(m, int) else X[:, ds(m, 1), :].rearrange("p o t -> p (o t)")

            def zero_sums():
                nc.vector.memset(S1[:, 0:T], 0.0)
                nc.vector.memset(S2[:, 0:T], 0.0)
                dve.drain()

            def add_sums(n, m):
                tt(S1[:, 0:T], S1[:, 0:T], row(m), ALU.add)
                dve.wait_ge(sq_ready, n * KT + m + 1)
                tt(S2[:, 0:T], S2[:, 0:T], SQT[:, 0:T], ALU.add).then_inc(sq_used, 1)
                dve.drain()

            def residual(l, n, m, c, tile):
                dve.wait_ge(acc_full, 1 + l * TILES + tile + 1)
                stt(out=halves(row(m)), in0=ACC[:, c, :, 0:HALF], scalar=INV_W / ALPHA, in1=halves(row(m)),
                    op0=ALU.mult, op1=ALU.add).then_inc(acc_read[c], 1)
                dve.drain().then_inc(y_ready, 1)
                add_sums(n, m)

            def norm_apply(n, scr, last=False):
                dve.drain().then_inc(sums_ready, 1)
                dve.wait_ge(msq_ready, n + 1)
                for h in range(2):
                    full, _ = scr.job(h)
                    dve.wait_ge(scr_full, full)
                    tt(VAR[:, h * HALF:(h + 1) * HALF], SCR[:, h, 0:HALF], MSQ[:, h * HALF:(h + 1) * HALF],
                       ALU.subtract).then_inc(scr_read[h], 1)
                dve.drain()
                ts(VAR[:, 0:T], VAR[:, 0:T], 0.0, None, ALU.max).then_inc(var_ready, 1)
                dve.wait_ge(rstd_ready, n + 1)
                for m in range(KT + 2):
                    if m < KT:
                        dve.wait_ge(ln_sub, n * KT + m + 1)
                        tt(X[:, m, :], X[:, m, :], RSTD[:, 0:T], ALU.mult).then_inc(ln_mul, 1)
                    if m >= 2 and not last:
                        dve.wait_ge(ln_out, n * KT + m - 1)
                        tt(XL[:, m - 2, :], X[:, m - 2, :], XH[:, m - 2, :], ALU.subtract).then_inc(x_ready, 1)

            def hg_gate(l, p, tile):
                n = l * HEADS + p
                dve.wait_ge(acc_full, 1 + tile + 1)
                ts(halves(Fb[:, 0:T]), ACC[:, 0, :, 0:HALF], INV_W, CLAMP, ALU.mult, ALU.max).then_inc(acc_read[0], 1)
                dve.drain().then_inc(f_ready, 1)
                dve.wait_ge(lnf_parts, n + 1)
                tt(Fb[:, 0:T], Fb[:, 0:T], T2[:, 0:T], ALU.add).then_inc(f2_ready, 1)
                tt(T3[:, 0:T], T3[:, 0:T], T2[:, 0:T], ALU.subtract)
                dve.drain()
                ts(T3[:, 0:T], T3[:, 0:T], LOG_F_MIN, None, ALU.max)
                dve.drain()
                nc.vector.tensor_tensor_scan(B[:, 0:T], keep, T3[:, 0:T], 0.0, ALU.mult, ALU.add)
                dve.drain()

            def hg_exponents(l, p):
                tt(T3[:, 0:TP - TP % C].rearrange("p (c t) -> p c t", t=C), bcast(B[:, C - 1:TP:C], C),
                   B[:, 0:TP - TP % C].rearrange("p (c t) -> p c t", t=C), ALU.subtract)
                tt(T3[:, TP - TP % C:TP], B[:, TP - 1:TP].to_broadcast([P, TP % C]), B[:, TP - TP % C:TP], ALU.subtract)
                tt(T3[:, TP:T].rearrange("p (b t) -> p b t", t=DEC_SEQ), bcast(B[:, TP + DEC_SEQ - 1:T:DEC_SEQ], DEC_SEQ),
                   B[:, TP:T].rearrange("p (b t) -> p b t", t=DEC_SEQ), ALU.subtract)
                for n, h in enumerate(LEVELS):
                    end = TP // (2 * h) * 2 * h
                    tt(Z[:, n, 0:end].rearrange("p (b t) -> p b t", t=2 * h), B[:, 0:end].rearrange("p (b t) -> p b t", t=2 * h),
                       bcast(B[:, h - 1:end:2 * h], 2 * h), ALU.subtract)
                tt(DK[:, :].rearrange("p (b t) -> p b t", t=A), B[:, 0:TP].rearrange("p (b t) -> p b t", t=A),
                   bcast(B[:, AT:TP:A], A), ALU.subtract).then_inc(diff_ready, 1)

            def hg_query(l, p, j, mixed, steps):
                n = l * HEADS + p
                dve.wait_ge(acc_read[1], 1 + l * ACC_TILES + 2 * p + 1)
                ts(T1[:, 0:T], Q[:, 0:T], CLAMP, None, ALU.max).then_inc(q_clamped, 1)
                dve.wait_ge(k_ready, n + 1)
                dve.wait_ge(exps_ready, n + 1)
                tt(KE[:, 0:T], Fb[:, 0:T], T3[:, 0:T], ALU.mult)
                tt(KVS[:, :], Fb[:, TP:T], EN[:, :], ALU.mult)
                for m in range(len(LEVELS)):
                    left, _ = level_halves(m)
                    tt(left, left, level_halves(m, Fb)[0], ALU.mult)
                tt(DK[:, :], DK[:, :], Fb[:, 0:TP], ALU.mult)
                dve.wait_ge(q_sig, n + 1)
                tt(Q[:, 0:T], Q[:, 0:T], T1[:, 0:T], ALU.mult)
                dve.drain()
                for m in range(len(LEVELS)):
                    _, right = level_halves(m)
                    tt(right, right, level_halves(m, Q)[1], ALU.mult)
                tt(DQ[:, :], DQ[:, :], Q[:, 0:TP], ALU.mult)
                for step in steps:
                    step()
                split_lo(0, j)
                dve.wait_ge(e_ready, n + 1)
                if mixed is not None:
                    dve.wait_ge(ot_full, mixed)
                tt(QD[:, 0:T], Q[:, 0:T], E[:, 0:T], ALU.mult)
                dve.drain().then_inc(ew_ready, 1)

            def rotate(c, dst):
                tt(halves(T1[0:64, 0:T]), ACC[64:P, c, :, 0:HALF], halves(sinT[64:P, :]), ALU.mult)
                tt(halves(T1[64:P, 0:T]), ACC[0:64, c, :, 0:HALF], halves(sinT[0:64, :]), ALU.mult)
                tt(halves(T2[:, 0:T]), ACC[:, c, :, 0:HALF], halves(cosT), ALU.mult).then_inc(acc_read[c], 1)
                dve.drain()
                tt(dst[:, 0:T], T1[:, 0:T], T2[:, 0:T], ALU.add)

            def rt_key(tile):
                dve.wait_ge(acc_full, 1 + tile + 1)
                rotate(0, KE)

            def rt_query(l, p, j, tile, mixed):
                dve.wait_ge(acc_full, 1 + tile + 1)
                split_lo(0, j)
                if mixed is not None:
                    dve.wait_ge(ot_full, mixed)
                rotate(1, QD)
                dve.drain()
                tt(QS[:, TP:T], QD[:, TP:T], tab[:, ds(cols["q_dec"][0] + p * TS, TS)], ALU.mult)
                dve.drain().then_inc(ew_ready, 1)

            def clamp_gate(hh):
                dve.wait_ge(g_raw, hh + 1)
                ts(R[:, :], G[:, 0:T], CLAMP, None, ALU.max).then_inc(g_clamped, 1)

            def out_gate(hh):
                dve.wait_ge(g_sig, hh + 1)
                tt(G[:, 0:T], G[:, 0:T], R[:, :], ALU.mult).then_inc(g_ready, 1)
                dve.drain()

            def decay_states(hh, decayed):
                dve.wait_ge(s0_in, 16 * (hh + 1))
                dve.wait_ge(sn_stored, 16 + 16 * hh)
                decayed()
                dve.drain()

            def add_sample_steps(scr, banks):
                for n, bank in enumerate(banks):
                    full, _ = scr.job(bank)
                    dve.wait_ge(scr_full, full)
                    w = SN[:, 512 * n:512 * (n + 1)]
                    tt(w, w, SCR[:, bank, :], ALU.add).then_inc(scr_read[bank], 1)
                dve.drain().then_inc(sn_ready, 1)

            def hg_scores(l, p, scr):
                hh = l * 2 * HEADS + p

                def keep_level(n, chunks, bank, o):
                    regular = [c for c in chunks if c[1] == C]
                    m = masks[0:C, n - 1, :].bitcast(mybir.dt.uint32)
                    t, k = regular[0][0], len(regular)
                    last = nc.vector.copy_predicated(PTS[:, t:t + k * C].rearrange("p (c t) -> p c t", t=C),
                                                     m.unsqueeze(1).to_broadcast([C, k, C]),
                                                     SCR[0:C, bank, o:o + k * C].rearrange("p (c t) -> p c t", t=C))
                    for t, w in chunks[k:]:
                        last = nc.vector.copy_predicated(PTS[0:w, t:t + w], m[0:w, 0:w], SCR[0:w, bank, o + k * C:o + k * C + w])
                    return last

                for n, (bank, first, second) in enumerate(HG_JOBS):
                    full, _ = scr.job(bank)
                    dve.wait_ge(scr_full, full)
                    if n == 0:
                        nc.vector.tensor_copy(PTS[0:C // 2, 0:TP - TP % C].rearrange("p (c t) -> p c t", t=C)[:, :, C // 2:C],
                                              SCR[0:C // 2, bank, REST_HG:REST_HG + (NC - 1) * C // 2].rearrange("p (c t) -> p c t", t=C // 2))
                    elif n == 1:
                        tt(PTSS[:, :], SCR[0:TS, bank, SPLIT:SPLIT + TS], mask32[0:TS, :], ALU.mult)
                    else:
                        nc.vector.memset(wait_spot[:, :], 0.0)
                    dve.drain()
                    last = keep_level(*first, bank, 0)
                    if n and second is not None:
                        dve.drain()
                        last = keep_level(*second, bank, REST_HG)
                    last.then_inc(scr_read[bank], 1)
                dve.drain().then_inc(pts_ready, 1)

            def hg_states(l, p, scr):
                hh = l * 2 * HEADS + p
                dve.wait_ge(fin_stored, 16 + 16 * hh)
                for n in range(2):
                    full, _ = scr.job(1 - n)
                    if n:
                        dve.drain()
                    dve.wait_ge(scr_full, full)
                    for c in range(4 * n, min(4 * n + 4, NC)):
                        u, s = SCR[:, 1 - n, (c - 4 * n) * P:(c - 4 * n + 1) * P], SC[:, c * P:(c + 1) * P]
                        if c == 0:
                            last = nc.vector.tensor_copy(s, u)
                        else:
                            if c > 4 * n:
                                dve.drain()
                            end = sum(CHUNKS[c])
                            last = stt(out=s, in0=SC[:, (c - 1) * P:c * P], scalar=E[:, end - 1:end], in1=u,
                                       op0=ALU.mult, op1=ALU.add)
                    last.then_inc(scr_read[1 - n], 1)
                dve.drain().then_inc(states_ready, 1)
                dve.drain().then_inc(decays_used, 1)
                dve.drain().then_inc(fin_ready, 1)

            def sample_states(l, p, scr):
                dve.wait_ge(sn_decayed, 1 + l * HEADS + p + 1)
                add_sample_steps(scr, (1, 0))

            def low_output(row_, hh):
                dve.wait_ge(oh_ready, hh + 1)
                tt(OL[:, ds(row_, 1), :].rearrange("p o t -> p (o t)"), TO[:, :], OH[:, ds(row_, 1), :].rearrange("p o t -> p (o t)"),
                   ALU.subtract).then_inc(ol_ready, 1)

            def hg_d(l, p):
                hh = l * 2 * HEADS + p
                dve.wait_ge(hr_ready, hh + 1)
                tt(TO[:, 0:SPLIT], OT[:, 0, 0:SPLIT], R[:, 0:SPLIT], ALU.mult)
                tt(TO[:, SPLIT:T], OT[:, 1, 0:REST], R[:, SPLIT:T], ALU.mult).then_inc(ot_read, 1)
                dve.drain()
                stt(out=TO[:, :], in0=TO[:, :], scalar=par[:, ds(l * HEADS + 2 * P + ROW_HG + p, 1)], in1=G[:, 0:T],
                    op0=ALU.mult, op1=ALU.mult).then_inc(to_ready, 1)
                low_output(p, hh)

            def hg_stages(l, p):
                s = scr_hg(l, p)

                def states():
                    for b in (1, 0, 1, 0):
                        s.job(b)
                    hg_states(l, p, s)
                return (lambda: hg_scores(l, p, s)), states, None, (lambda: hg_d(l, p)), (lambda: sample_states(l, p, s))

            def rt_a(l, p, scr):
                hh = l * 2 * HEADS + HEADS + p
                bank = 1
                for job in RT_JOBS:
                    full, _ = scr.job(bank)
                    dve.wait_ge(scr_full, full)
                    for i, t0, t1, o in job:
                        r = P if i < 4 else TAIL
                        u, w = t0 - i * P, t1 - t0
                        last = tt(PTR[0:r, RT_OFF[i] + u:RT_OFF[i] + u + w], SCR[0:r, bank, o:o + w],
                                  tab[0:r, ds(decay_at + p * TP + u, w)], ALU.mult)
                    if job is RT_JOBS[-1]:
                        last = tt(PTSS[:, :], SCR[0:TS, bank, TAIL:TAIL + TS], tab[0:TS, ds(cols["mask_rt"][0] + p * TS, TS)], ALU.mult)
                    last.then_inc(scr_read[bank], 1)
                    bank = 1 - bank
                dve.drain().then_inc(pts_ready, 1)

            def rt_b(l, p, scr):
                hh = l * 2 * HEADS + HEADS + p
                scr.job(0)
                decay_states(hh, lambda: ts(SN[:, :], S0[:, :], tab[:, ds(cols["gamma4"][0] + p, 1)], None, ALU.mult))
                add_sample_steps(scr, (1, 0))

            def rt_c(l, p, scr):
                for bank, (a, b) in ((1, (0, SPLIT)), (0, (SPLIT, T))):
                    full, _ = scr.job(bank)
                    dve.wait_ge(scr_full, full)
                    nc.vector.tensor_copy(TO[:, a:b], SCR[:, bank, 0:b - a]).then_inc(scr_read[bank], 1)
                dve.drain().then_inc(oc_ready, 1)

            def rt_d(l, p):
                hh = l * 2 * HEADS + HEADS + p
                dve.wait_ge(hr_ready, hh + 1)
                tt(TO[:, :], TO[:, :], R[:, :], ALU.mult)
                dve.drain()
                ts(TO[:, :], TO[:, :], par[:, ds(l * HEADS + 2 * P + ROW_RG + p, 1)],
                   par[:, ds(l * HEADS + 2 * P + ROW_RB + p, 1)], ALU.mult, ALU.add)
                dve.drain()
                tt(TO[:, :], TO[:, :], G[:, 0:T], ALU.mult).then_inc(to_ready, 1)
                low_output(HEADS + p, hh)

            def rt_stages(l, p):
                s = scr_rt(l, p)
                for b in (0, 1, 0):
                    s.job(b)
                return (lambda: rt_a(l, p, s)), (lambda: rt_b(l, p, s)), (lambda: rt_c(l, p, s)), (lambda: rt_d(l, p))

            def group(l, g, head, kind, stages=(None,) * 4, mixed=None, after_hgrn=False):
                a, b, c, d, *steps = stages
                j, tile = l * SLOT_UNITS + g, l * TILES + 4 * g
                hh = l * 2 * HEADS + kind * HEADS + head
                if a is not None:
                    a()
                split_lo(1, j)
                if kind == 0:
                    hg_gate(l, head, tile)
                    hg_exponents(l, head)
                    if b is not None:
                        b()
                    if d is not None:
                        out_gate(hh - 1)
                    hg_query(l, head, j + 1, mixed, steps)
                else:
                    if after_hgrn:
                        dve.wait_ge(tok_ready, hh)
                    rt_key(tile)
                    if b is not None:
                        b()
                    for step in steps:
                        step()
                    if steps:
                        out_gate(hh - 1)
                    rt_query(l, head, j + 1, tile + 1, mixed)
                if c is not None:
                    out_gate(hh - 1)
                    c()
                if d is not None:
                    d()
                clamp_gate(hh)

            for counter in (*w_lo, acc_full, *acc_read, ot_read, sq_used, h_ready, decays_used, sn_decayed):
                dve.drain().then_inc(counter, 1)
            scr = Scratch((0, 0, 0))
            for i in range(TT5):
                n = P if i < 4 else R5
                for q in range(2):
                    full, _ = scr.job(1 - q)
                    dve.wait_ge(scr_full, full)
                    nc.vector.tensor_copy(X[:, 4 * q:4 * q + 4, i * P:i * P + n],
                                          SCR[:, 1 - q, :].rearrange("p (k t) -> p k t", k=4)[:, :, 0:n]).then_inc(scr_read[1 - q], 1)
            dve.drain().then_inc(y_ready, 1)
            dve.wait_ge(params_ready, 1)
            lb = par[:, 2 * P + ROW_LB:2 * P + ROW_LB + 2 * HEADS].rearrange("p (l h) -> p l h", l=DEPTH)
            for l in range(DEPTH):
                ts(CW2[:, l * FT:(l + 1) * FT], par[:, l * P + 2 * FT:l * P + 3 * FT], INV_W, None, ALU.mult)
            tt(LE[:, 0, :], lb[:, 0, :], lb[:, 1, :], ALU.max)
            dve.drain()
            for l in range(DEPTH):
                last = tt(LE[:, 1 + l, :], lb[:, l, :], LE[:, 0, :], ALU.subtract)
            last.then_inc(lb_max, 1)
            dve.wait_ge(lb_exp, 1)
            tt(LE[:, 3, :], LE[:, 1, :], LE[:, 2, :], ALU.add)
            dve.drain()
            nc.vector.reciprocal(LE[:, 3, :], LE[:, 3, :])
            dve.drain()
            for l in range(DEPTH):
                tt(LE[:, 1 + l, :], LE[:, 1 + l, :], LE[:, 3, :], ALU.mult)
            dve.drain()
            tt(LBT[:, 0:HEADS], LE[:, 1, :], LE[:, 1, :], ALU.subtract)
            tt(LE[:, 4, :], LE[:, 1, :], LE[:, 2, :], ALU.add)
            dve.drain()
            tt(LBT[:, HEADS:2 * HEADS], LE[:, 4, :], LE[:, 1, :], ALU.subtract)
            dve.drain()
            ts(OMLB[:, :], LBT[:, :], -1.0, 1.0, ALU.mult, ALU.add)
            dve.drain()

            dve.wait_ge(pts_zero, 1)
            dve.wait_ge(tables_in, 16)
            zero_sums()
            for m in range(KT):
                dve.wait_ge(sq_ready, m + 1)
                tt(S2[:, 0:T], S2[:, 0:T], (E, QD)[m % 2][:, 0:T], ALU.add).then_inc(sq_used, 1)
                dve.drain()

            with dve.Fori(0, DEPTH) as l:
                ot0 = l * OT_LAYER
                split_lo(0, l * SLOT_UNITS)
                norm_apply(2 * l, Scratch(base(l)))
                group(l, 0, 0, 0)
                with dve.Fori(0, HEADS - 1) as p:
                    group(l, p + 1, p + 1, 0, hg_stages(l, p), ot0 + 2 + p)
                group(l, HEADS, 0, 1, hg_stages(l, HEADS - 1), ot0 + 1 + HEADS, after_hgrn=True)
                with dve.Fori(0, HEADS - 1) as p:
                    group(l, p + HEADS + 1, p + 1, 1, rt_stages(l, p), ot0 + 2 + HEADS + 2 * p)
                out_gate((l + 1) * 2 * HEADS - 1)
                for stage_ in rt_stages(l, HEADS - 1):
                    stage_()

                zero_sums()
                with dve.Fori(0, 2) as i:
                    for n in range(4):
                        if n % 2 == 0:
                            split_lo(1 - n // 2, l * SLOT_UNITS + 8 + i + n // 2)
                        residual(l, 2 * l + 1, 4 * i + n, n % 2, O_TILE + 4 * i + n)
                norm_apply(2 * l + 1, scr_ln1(l))

                dve.wait_ge(cst_ready, l + 1)
                dve.wait_ge(sn_stored, 16 + (l + 1) * 2 * HEADS * 16)
                dve.wait_ge(fin_stored, 16 + (l + 1) * 2 * HEADS * 16)
                for c in range(2):
                    nc.vector.memset(AX[c][:, 0:2], 0.0)
                dve.drain()
                with dve.Fori(0, FT // 2) as i:
                    n0 = l * FT + 2 * i
                    split_lo(1, l * SLOT_UNITS + 10 + i)
                    for c in range(2):
                        ax, cx, ft = AX[c], CX[c], 2 * i + c
                        w0, w1 = (par[:, ds(l * P + n * FT + 2 * i + c, 1)] for n in range(2))
                        dve.wait_ge(a_ready, n0 + c + 1)
                        nc.vector.tensor_copy(AS[:, :, 2:6], ax[:, 2 + TP:2 + T].rearrange("p (b t) -> p b t", t=DEC_SEQ))
                        nc.vector.tensor_copy(AS[:, :, 0:2], CST[:, ds(ft, 1), :].rearrange("p o (b j) -> p (o b) j", j=2))
                        stt(out=cx[:, 0:TP], in0=ax[:, 1:1 + TP], scalar=w1, in1=cx[:, 0:TP], op0=ALU.mult, op1=ALU.add)
                        dve.drain()
                        cs = cx[:, TP:T].rearrange("p (b t) -> p b t", t=DEC_SEQ)
                        stt(out=cs, in0=AS[:, :, 1:5], scalar=w1, in1=cs, op0=ALU.mult, op1=ALU.add)
                        stt(out=cx[:, 0:TP], in0=ax[:, 0:TP], scalar=w0, in1=cx[:, 0:TP], op0=ALU.mult, op1=ALU.add)
                        nc.vector.tensor_copy(CSB[:, ds(ft, 1), 0:2].rearrange("p o j -> p (o j)"), ax[:, TP:TP + 2])
                        nc.vector.tensor_copy(CSB[:, ds(ft, 1), 2:18].rearrange("p o (b j) -> p (o b) j", j=2), AS[:, :, 4:6])
                        dve.drain()
                        stt(out=cs, in0=AS[:, :, 0:4], scalar=w0, in1=cs, op0=ALU.mult, op1=ALU.add)
                        dve.drain().then_inc(conv_ready, 1)
                    split_lo(0, l * SLOT_UNITS + 11 + i)
                    for c in range(2):
                        cx = CX[c]
                        dve.wait_ge(gelu_ready, n0 + c + 1)
                        dve.wait_ge(acc_full, 1 + l * TILES + F_TILE + 4 * i + 3 + c)
                        stt(out=halves(cx[:, 0:T]), in0=ACC[:, c, :, 0:HALF], scalar=INV_W, in1=halves(cx[:, 0:T]),
                            op0=ALU.mult, op1=ALU.mult).then_inc(acc_read[c], 1)
                        dve.drain().then_inc(ht_ready, 1)
                    for c in range(2):
                        one = lambda t: t[:, ds(2 * i + c, 1), :].rearrange("p o t -> p (o t)")
                        dve.wait_ge(hh_ready, n0 + c + 1)
                        tt(one(HL), CX[c][:, 0:T], one(HH), ALU.subtract).then_inc(h_ready, 1)

                zero_sums()

                def down(q, last):
                    for c in range(2):
                        split_lo(1, l * SLOT_UNITS + 21 + 2 * q + c, UNIT_D)
                        if not (last and c == 1):
                            split_lo(0, l * SLOT_UNITS + 22 + 2 * q + c, UNIT_D)
                        residual(l, 2 * l + 2, 2 * q + c, c, D_TILE + 2 * q + c)
                with dve.Fori(0, KT // 2 - 1) as q:
                    down(q, False)
                down(KT // 2 - 1, True)
            norm_apply(2 * DEPTH, Scratch(base(DEPTH)), last=True)
            scr = Scratch(base(DEPTH), SCR_LN)
            for i in range(TT5):
                n = P if i < 4 else R5
                scr.job(0)
                full, _ = scr.job(1)
                dve.wait_ge(scr_full, full)
                nc.vector.tensor_copy(XT[0:n, i, 512:1024], SCR[0:n, 1, :]).then_inc(scr_read[1], 1)
                dve.drain().then_inc(out_right, 1)


N_PARAM_DMAS = 2 * DEPTH + 2 * (2 * DEPTH + 1) + 4
RT_JOBS = [[(0, 0, SPLIT, 0)], [(0, SPLIT, TP, 0)], [(1, P, TP, 0)],
           [(2, 2 * P, TP, 0), (3, 3 * P, TP, TP - 2 * P)], [(4, 4 * P, TP, 0)]]


HG_SLOTS = ([1, 2, 3, 4, 5, 6, 7], [7, 8, 9, 10], [12, 13], [22, 22], [23, 23, 24, 24, 25, 25], [28, 28])
HG_SLOTS_RT = ([1, 2, 3, 4, 5, 6, 7], [7, 8, 9, 10], [12, 13], [15, 16], [18, 19, 20, 21, 22, 23], [27, 27])
REST_HG = TP - SPLIT
LEFT, RIGHT = CHUNKS[:3], CHUNKS[3:]
HG_JOBS = [(0, (1, RIGHT), (0, None)), (1, (1, LEFT), None), (0, (2, LEFT), None), (1, (2, RIGHT), (3, RIGHT)),
           (0, (3, LEFT), None), (1, (4, LEFT), None), (0, (4, RIGHT), None)]
RT_SLOTS = ([4, 5, 6], [6, 7, 8, 9, 10], [12], [12, 13], [15, 16], [21, 22], [29])


_INS = ['x_prompt', 'x_sample', 'state_hgrn', 'state_ret', 'state_conv', 'meta_tokens', 'emb_ln_g', 'emb_ln_b',
        'lb_logits', 'w_in', 'hg_norm_g', 'rt_gn_g', 'rt_gn_b', 'w_o', 'ln1_g', 'ln1_b', 'w_a', 'w_b', 'conv_w',
        'conv_b', 'w_down', 'ln2_g', 'ln2_b']
_OUTS = [(1, SEQ, D_MODEL), (DEC_BATCH, DEC_SEQ, D_MODEL), (DEPTH, 1, HEADS, P, P), (DEPTH, DEC_BATCH, HEADS, P, P),
         (DEPTH, 1, HEADS, P, P), (DEPTH, DEC_BATCH, HEADS, P, P), (DEPTH, 1, CONV_W - 1, D_FF),
         (DEPTH, DEC_BATCH, CONV_W - 1, D_FF)]


def kernel(**inputs):
    import concourse.bacc as _bacc
    from concourse.bass_utils import run_bass_kernel_spmd as _run

    nc = _bacc.Bacc("TRN2", target_bir_lowering=False, num_devices=1)
    arrays, args = {}, []
    for name in _INS:
        a = np.ascontiguousarray(inputs[name])
        arrays[f"in_{name}_dram"] = a
        args.append(nc.dram_tensor(f"in_{name}_dram", a.shape, mybir.dt.from_np(a.dtype), kind="ExternalInput").ap())
    tables = const_tables()
    arrays["in_tables_dram"] = tables
    args.append(nc.dram_tensor("in_tables_dram", tables.shape, F32, kind="ExternalInput").ap())
    for i, shape in enumerate(_OUTS):
        args.append(nc.dram_tensor(f"out_{i}_dram", shape, F32, kind="ExternalOutput").ap())
    hybrid_decoder_step(nc, *args)
    r = _run(nc, [arrays], core_ids=[0])
    return tuple(r.results[0][f"out_{i}_dram"] for i in range(len(_OUTS)))
```
